# Optimizing a Trainium2 kernel written in Bass

```python
import math
import jax, jax.numpy as jnp
from jax import lax
import numpy as np

D_MODEL = 1024
BATCH = 1
SEQ = 1024
DEPTH = 2

N_EVEN = (DEPTH + 1) // 2
N_ODD = DEPTH // 2

MLA_HEADS = 8
MLA_NOPE = 64
MLA_ROPE = 32
MLA_V = 64
MLA_Q_RANK = 256
MLA_KV_RANK = 128
MLA_WIDTH = MLA_HEADS * MLA_V
ROPE_BASE = 10000.0
Q_BLOCK = 128

S5_WIDTH = 256
S5_GROUP = 16
S5_GROUPS = S5_WIDTH // S5_GROUP
S5_STATE = 64
DT_MIN = 1e-3
DT_MAX = 1e-1

GLA_HEADS = 4
GLA_KEY_WIDTH = D_MODEL // 2
GLA_WIDTH = D_MODEL
GLA_DK = GLA_KEY_WIDTH // GLA_HEADS
GLA_DV = GLA_WIDTH // GLA_HEADS
GLA_GATE_RANK = 16
GLA_GATE_NORM = 16.0
GLA_CHUNK = 64

EVEN_SPLITS = (MLA_Q_RANK, MLA_KV_RANK, MLA_ROPE, MLA_WIDTH, S5_WIDTH, S5_WIDTH)
EVEN_IN = sum(EVEN_SPLITS)
EVEN_MIX = MLA_WIDTH + S5_WIDTH
ODD_SPLITS = (GLA_KEY_WIDTH, GLA_KEY_WIDTH, GLA_WIDTH, GLA_GATE_RANK, GLA_WIDTH)
ODD_IN = sum(ODD_SPLITS)
ODD_MIX = GLA_WIDTH

DEEPNORM_ALPHA = (2 * DEPTH) ** 0.25
DEEPNORM_BETA = (8 * DEPTH) ** -0.25
LN_EPS = 1e-5
RMS_EPS = 1e-6

kernel_name = "hybrid_mla_s5_gla_deepnorm"

def _split(h, sizes):
    idx = [int(i) for i in np.cumsum(sizes)[:-1]]
    return jnp.split(h, idx, axis=-1)

def rms_norm(x, g):
    xf = x.astype(jnp.float32)
    y = xf * lax.rsqrt(jnp.mean(xf * xf, axis=-1, keepdims=True) + RMS_EPS)
    return (y * g.astype(jnp.float32)).astype(x.dtype)

def layer_norm(x, g, b):
    xf = x.astype(jnp.float32)
    mu = jnp.mean(xf, axis=-1, keepdims=True)
    xc = xf - mu
    var = jnp.mean(xc * xc, axis=-1, keepdims=True)
    y = xc * lax.rsqrt(var + LN_EPS) * g.astype(jnp.float32) + b.astype(jnp.float32)
    return y.astype(x.dtype)

def rope_tables(pos, dtype):
    half = MLA_ROPE // 2
    inv_freq = ROPE_BASE ** (-jnp.arange(half, dtype=jnp.float32) / half)
    ang = pos.astype(jnp.float32)[..., None] * inv_freq
    return jnp.cos(ang).astype(dtype), jnp.sin(ang).astype(dtype)

def apply_rope(x, cos, sin):
    half = x.shape[-1] // 2
    x1, x2 = x[..., :half], x[..., half:]
    return jnp.concatenate([x1 * cos - x2 * sin, x2 * cos + x1 * sin], axis=-1)

def mla_attention(cq, ckv, k_rope_raw, pos, q_norm, kv_norm, w_uq, w_ukv):
    B, S, _ = cq.shape
    H = MLA_HEADS
    q = (rms_norm(cq, q_norm) @ w_uq).reshape(B, S, H, MLA_NOPE + MLA_ROPE)
    kv = (rms_norm(ckv, kv_norm) @ w_ukv).reshape(B, S, H, MLA_NOPE + MLA_V)
    q_nope, q_pe = q[..., :MLA_NOPE], q[..., MLA_NOPE:]
    k_nope, v = kv[..., :MLA_NOPE], kv[..., MLA_NOPE:]
    cos, sin = rope_tables(pos, q.dtype)
    q_pe = apply_rope(q_pe, cos[:, :, None, :], sin[:, :, None, :])
    k_pe = apply_rope(k_rope_raw, cos, sin)
    scale = (MLA_NOPE + MLA_ROPE) ** -0.5
    nb = S // Q_BLOCK
    qn_blocks = q_nope.reshape(B, nb, Q_BLOCK, H, MLA_NOPE).transpose(1, 0, 2, 3, 4)
    qp_blocks = q_pe.reshape(B, nb, Q_BLOCK, H, MLA_ROPE).transpose(1, 0, 2, 3, 4)
    k_idx = jnp.arange(S)

    def block(args):
        qn, qp, i = args
        s = (jnp.einsum('bqhd,bkhd->bhqk', qn, k_nope)
             + jnp.einsum('bqhr,bkr->bhqk', qp, k_pe)).astype(jnp.float32) * scale
        q_idx = i * Q_BLOCK + jnp.arange(Q_BLOCK)
        causal = k_idx[None, :] <= q_idx[:, None]
        s = jnp.where(causal, s, -jnp.inf)
        p = jax.nn.softmax(s, axis=-1).astype(v.dtype)
        return jnp.einsum('bhqk,bkhd->bqhd', p, v)

    o = lax.map(block, (qn_blocks, qp_blocks, jnp.arange(nb)))
    return o.transpose(1, 0, 2, 3, 4).reshape(B, S, H * MLA_V)

def s5_layer(u, a_re, a_im, log_dt, b_re, b_im, c_re, c_im, d_skip, w_glu, b_glu):
    B, S, W = u.shape
    f32 = jnp.float32
    uf = u.astype(f32).reshape(B, S, S5_GROUPS, S5_GROUP)
    dt = jnp.exp(log_dt.astype(f32))[:, None]
    ar, ai = a_re.astype(f32), a_im.astype(f32)
    mag = jnp.exp(ar * dt)
    lr, li = mag * jnp.cos(ai * dt), mag * jnp.sin(ai * dt)
    den = ar * ar + ai * ai
    nr, ni = lr - 1.0, li
    zr = (nr * ar + ni * ai) / den
    zi = (ni * ar - nr * ai) / den
    br, bi = b_re.astype(f32), b_im.astype(f32)
    bbr = zr[..., None] * br - zi[..., None] * bi
    bbi = zr[..., None] * bi + zi[..., None] * br
    xr = jnp.einsum('gph,bsgh->bsgp', bbr, uf)
    xi = jnp.einsum('gph,bsgh->bsgp', bbi, uf)
    a_seq_r = jnp.broadcast_to(lr, (1, S) + lr.shape)
    a_seq_i = jnp.broadcast_to(li, (1, S) + li.shape)

    def combine(e1, e2):
        a1r, a1i, b1r, b1i = e1
        a2r, a2i, b2r, b2i = e2
        return (a2r * a1r - a2i * a1i,
                a2r * a1i + a2i * a1r,
                a2r * b1r - a2i * b1i + b2r,
                a2r * b1i + a2i * b1r + b2i)

    _, _, hr, hi = lax.associative_scan(combine, (a_seq_r, a_seq_i, xr, xi), axis=1)
    y = (jnp.einsum('ghp,bsgp->bsgh', c_re.astype(f32), hr)
         - jnp.einsum('ghp,bsgp->bsgh', c_im.astype(f32), hi)).reshape(B, S, W)
    y = y + d_skip.astype(f32) * u.astype(f32)
    y = jax.nn.gelu(y)
    y = y * jax.nn.sigmoid(y @ w_glu.astype(f32) + b_glu.astype(f32))
    return y.astype(u.dtype)

def gla_layer(q, k, v, gk_low, w_gk2, b_gk, g_norm):
    B, S, _ = q.shape
    H, DK, DV, C = GLA_HEADS, GLA_DK, GLA_DV, GLA_CHUNK
    N = S // C
    f32 = jnp.float32
    log_a = jax.nn.log_sigmoid((gk_low @ w_gk2 + b_gk).astype(f32)) / GLA_GATE_NORM

    def heads(t, d):
        return t.reshape(B, N, C, H, d).transpose(0, 3, 1, 2, 4).astype(f32)

    qh = heads(q, DK) * (DK ** -0.5)
    kh, vh, gh = heads(k, DK), heads(v, DV), heads(log_a, DK)
    bcum = jnp.cumsum(gh, axis=3)
    b_last = bcum[:, :, :, -1:]
    q_dec = qh * jnp.exp(bcum)
    k_inv = kh * jnp.exp(-bcum)
    k_to_end = kh * jnp.exp(b_last - bcum)
    tri = jnp.tril(jnp.ones((C, C), dtype=bool))
    att = jnp.where(tri, jnp.einsum('bhncd,bhnsd->bhncs', q_dec, k_inv), 0.0)
    o_intra = jnp.einsum('bhncs,bhnsv->bhncv', att, vh)

    def step(state, xs):
        qd, kend, vc, decay = xs
        o = jnp.einsum('bhcd,bhdv->bhcv', qd, state)
        state = state * decay[..., None] + jnp.einsum('bhcd,bhcv->bhdv', kend, vc)
        return state, o

    xs = (q_dec.transpose(2, 0, 1, 3, 4), k_to_end.transpose(2, 0, 1, 3, 4),
          vh.transpose(2, 0, 1, 3, 4), jnp.exp(b_last[:, :, :, 0]).transpose(2, 0, 1, 3))
    state0 = jnp.zeros((B, H, DK, DV), f32)
    _, o_inter = lax.scan(step, state0, xs)
    o = o_intra + o_inter.transpose(1, 2, 0, 3, 4)
    o = o.transpose(0, 2, 3, 1, 4).reshape(B, S, H, DV)
    o = rms_norm(o, g_norm).reshape(B, S, H * DV)
    return o.astype(q.dtype)

def even_layer(x, pos, w_in, q_norm, kv_norm, w_uq, w_ukv, a_re, a_im, log_dt,
               b_re, b_im, c_re, c_im, d_skip, w_glu, b_glu, w_out):
    h = x @ w_in
    cq, ckv, k_rope, g_mla, u, g_s5 = _split(h, EVEN_SPLITS)
    o_mla = mla_attention(cq, ckv, k_rope, pos, q_norm, kv_norm, w_uq, w_ukv) * jax.nn.silu(g_mla)
    o_s5 = s5_layer(u, a_re, a_im, log_dt, b_re, b_im, c_re, c_im, d_skip, w_glu, b_glu) * jax.nn.silu(g_s5)
    return jnp.concatenate([o_mla, o_s5], axis=-1) @ w_out

def odd_layer(x, w_in, w_gk2, b_gk, g_norm, w_out):
    h = x @ w_in
    q, k, v, gk_low, g = _split(h, ODD_SPLITS)
    o = gla_layer(q, k, v, gk_low, w_gk2, b_gk, g_norm) * jax.nn.silu(g)
    return o @ w_out

def setup_inputs(seed: int = 0) -> dict:
    key = jax.random.key(seed)
    ks = jax.random.split(key, 32)
    nrm = lambda k, shape, s: jax.random.normal(k, shape, jnp.float32) * s
    G, P, GS = S5_GROUPS, S5_STATE, S5_GROUP
    x = jax.random.normal(ks[0], (BATCH, SEQ, D_MODEL), jnp.float32)
    positions = jnp.broadcast_to(jnp.arange(SEQ, dtype=jnp.int32)[None, :], (BATCH, SEQ))
    ln_g = 1.0 + nrm(ks[1], (DEPTH, D_MODEL), 0.02)
    ln_b = nrm(ks[2], (DEPTH, D_MODEL), 0.02)
    even_w_in = nrm(ks[3], (N_EVEN, D_MODEL, EVEN_IN), D_MODEL ** -0.5)
    mla_q_norm = 1.0 + nrm(ks[4], (N_EVEN, MLA_Q_RANK), 0.02)
    mla_kv_norm = 1.0 + nrm(ks[5], (N_EVEN, MLA_KV_RANK), 0.02)
    mla_w_uq = nrm(ks[6], (N_EVEN, MLA_Q_RANK, MLA_HEADS * (MLA_NOPE + MLA_ROPE)), MLA_Q_RANK ** -0.5)
    mla_w_ukv = nrm(ks[7], (N_EVEN, MLA_KV_RANK, MLA_HEADS * (MLA_NOPE + MLA_V)), MLA_KV_RANK ** -0.5)
    n_idx = jnp.arange(P, dtype=jnp.float32)
    s5_a_re = -0.5 * jnp.exp(nrm(ks[8], (N_EVEN, G, P), 0.01))
    s5_a_im = math.pi * n_idx + nrm(ks[9], (N_EVEN, G, P), 0.01)
    s5_log_dt = jax.random.uniform(ks[10], (N_EVEN, G), jnp.float32, math.log(DT_MIN), math.log(DT_MAX))
    s5_b_re = nrm(ks[11], (N_EVEN, G, P, GS), (2 * GS) ** -0.5)
    s5_b_im = nrm(ks[12], (N_EVEN, G, P, GS), (2 * GS) ** -0.5)
    s5_c_re = nrm(ks[13], (N_EVEN, G, GS, P), (2 * P) ** -0.5)
    s5_c_im = nrm(ks[14], (N_EVEN, G, GS, P), (2 * P) ** -0.5)
    s5_d = nrm(ks[15], (N_EVEN, S5_WIDTH), 1.0)
    s5_w_glu = nrm(ks[16], (N_EVEN, S5_WIDTH, S5_WIDTH), S5_WIDTH ** -0.5)
    s5_b_glu = nrm(ks[17], (N_EVEN, S5_WIDTH), 0.02)
    even_w_out = nrm(ks[18], (N_EVEN, EVEN_MIX, D_MODEL), EVEN_MIX ** -0.5 * DEEPNORM_BETA)
    odd_w_in = nrm(ks[19], (N_ODD, D_MODEL, ODD_IN), D_MODEL ** -0.5)
    gla_w_gk2 = nrm(ks[20], (N_ODD, GLA_GATE_RANK, GLA_KEY_WIDTH), GLA_GATE_RANK ** -0.5)
    gla_b_gk = nrm(ks[21], (N_ODD, GLA_KEY_WIDTH), 0.02)
    gla_g_norm = 1.0 + nrm(ks[22], (N_ODD, GLA_DV), 0.02)
    odd_w_out = nrm(ks[23], (N_ODD, ODD_MIX, D_MODEL), ODD_MIX ** -0.5 * DEEPNORM_BETA)
    return {"x": x, "positions": positions, "ln_g": ln_g, "ln_b": ln_b,
            "even_w_in": even_w_in, "mla_q_norm": mla_q_norm, "mla_kv_norm": mla_kv_norm,
            "mla_w_uq": mla_w_uq, "mla_w_ukv": mla_w_ukv,
            "s5_a_re": s5_a_re, "s5_a_im": s5_a_im, "s5_log_dt": s5_log_dt,
            "s5_b_re": s5_b_re, "s5_b_im": s5_b_im, "s5_c_re": s5_c_re, "s5_c_im": s5_c_im,
            "s5_d": s5_d, "s5_w_glu": s5_w_glu, "s5_b_glu": s5_b_glu, "even_w_out": even_w_out,
            "odd_w_in": odd_w_in, "gla_w_gk2": gla_w_gk2, "gla_b_gk": gla_b_gk,
            "gla_g_norm": gla_g_norm, "odd_w_out": odd_w_out}

def reference(x, positions, ln_g, ln_b, even_w_in, mla_q_norm, mla_kv_norm, mla_w_uq, mla_w_ukv,
              s5_a_re, s5_a_im, s5_log_dt, s5_b_re, s5_b_im, s5_c_re, s5_c_im, s5_d, s5_w_glu,
              s5_b_glu, even_w_out, odd_w_in, gla_w_gk2, gla_b_gk, gla_g_norm, odd_w_out):
    for layer in range(DEPTH):
        j = layer // 2
        if layer % 2 == 0:
            y = even_layer(x, positions, even_w_in[j], mla_q_norm[j], mla_kv_norm[j], mla_w_uq[j],
                           mla_w_ukv[j], s5_a_re[j], s5_a_im[j], s5_log_dt[j], s5_b_re[j], s5_b_im[j],
                           s5_c_re[j], s5_c_im[j], s5_d[j], s5_w_glu[j], s5_b_glu[j], even_w_out[j])
        else:
            y = odd_layer(x, odd_w_in[j], gla_w_gk2[j], gla_b_gk[j], gla_g_norm[j], odd_w_out[j])
        x = layer_norm(DEEPNORM_ALPHA * x + y, ln_g[layer], ln_b[layer])
    return x


_drawn_inputs = setup_inputs


def setup_inputs(seed=0):
    import zlib

    import numpy as np

    out = dict(_drawn_inputs(seed))
    spreads = {}
    factors = {'mla_q_norm': 8.0,
     'mla_kv_norm': 8.0,
     's5_a_re': 64.0,
     's5_a_im': 64.0,
     's5_log_dt': 64.0,
     's5_b_re': 64.0,
     's5_b_im': 64.0,
     's5_c_re': 64.0,
     's5_c_im': 64.0,
     's5_w_glu': 4.108,
     's5_b_glu': 200.0,
     'gla_b_gk': 8.0,
     'gla_g_norm': 94.928}
    for name, (base, spread) in spreads.items():
        noise = np.random.default_rng([zlib.crc32(name.encode()), seed]).standard_normal(out[name].shape)
        drawn = base * np.exp(spread * noise) if base else spread * noise
        out[name] = __import__('jax').numpy.asarray(drawn.astype(out[name].dtype))
    for name, factor in factors.items():
        out[name] = (out[name] * factor).astype(out[name].dtype)
    return out
```

```python
import math
from collections import defaultdict
from contextlib import ExitStack

import concourse.bass as bass
from concourse import mybir
import numpy as np

F32 = mybir.dt.float32
BF16 = mybir.dt.bfloat16
I32 = mybir.dt.int32
ALU = mybir.AluOpType
ACT = mybir.ActivationFunctionType
AX_X = mybir.AxisListType.X

P = 128
PI_BELOW = 3.1415925
TO_INT = 1.5 * 2 ** 23
TO_13_BITS = 1.5 * 2 ** 10


def two_pi_parts():
    first = 6.28125
    second = float(np.float32(round((2 * math.pi - first) * 2 ** 19) / 2 ** 19))
    return first, second, float(np.float32(2 * math.pi - first - second))


class PsumPlan:

    def __init__(self, new_sem):
        self.new_sem, self.sems, self.counts = new_sem, {}, defaultdict(int)
        self.last_on, self.jobs = {}, {}

    def give(self, job, *banks):
        if banks not in self.sems:
            name = "_".join(map(str, banks))
            self.sems[banks] = (self.new_sem(f"bank{name}_full"), self.new_sem(f"bank{name}_free"))
        nth = self.counts[banks] = self.counts[banks] + 1
        before = {self.last_on[b] for b in banks if b in self.last_on}
        self.jobs[job] = (banks, nth, before)
        for b in banks:
            self.last_on[b] = job

    def bank(self, job):
        return self.jobs[job][0][0]

    def full(self, job):
        return self.sems[self.jobs[job][0]][0]

    def free(self, job):
        return self.sems[self.jobs[job][0]][1]

    def claim(self, pe, job):
        for old in self.jobs[job][2]:
            pe.wait_ge(self.free(old), self.jobs[old][1])

    def filled(self, engine, job):
        engine.wait_ge(self.full(job), self.jobs[job][1])

    def drained(self, engine, job):
        engine.wait_ge(self.free(job), self.jobs[job][1])


class Steps:

    def __init__(self, engine, own, plan):
        self.engine, self.own, self.plan = engine, own, plan
        self.counts, self.last = defaultdict(int), None

    def __call__(self, ins, signal=None):
        signal = signal or self.own
        ins.then_inc(signal, 1)
        self.counts[signal.name] += 1
        self.last = (signal, self.counts[signal.name])
        self.settle()

    def frees(self, ins, job):
        ins.then_inc(self.plan.free(job), 1)
        self.last = (self.plan.free(job), self.plan.jobs[job][1])
        self.settle()

    def settle(self):
        self.engine.wait_ge(*self.last)


def hybrid_trunk(nc, x, positions, ln_g, ln_b, even_w_in, mla_q_norm, mla_kv_norm, mla_w_uq,
                 mla_w_ukv, s5_a_re, s5_a_im, s5_log_dt, s5_b_re, s5_b_im, s5_c_re, s5_c_im,
                 s5_d, s5_w_glu, s5_b_glu, even_w_out, odd_w_in, gla_w_gk2, gla_b_gk,
                 gla_g_norm, odd_w_out, out):
    S, D = x.shape[1:]
    NT, KD = S // P, D // P
    RQ, RKV = mla_q_norm.shape[1], mla_kv_norm.shape[1]
    H, NOPE, ROPE, VD = 8, 64, 32, 64
    HALF, QK = ROPE // 2, NOPE + ROPE
    G, NS = s5_a_re.shape[1:]
    GS = s5_b_re.shape[3]
    W5 = G * GS
    LC = P // GS
    NC5 = S // LC
    MIX = H * VD + W5
    NA = RQ + RKV + ROPE
    GH, GDK, GDV, GC = 4, 128, 256, 64
    GKW, GW, GR = GH * GDK, GH * GDV, gla_w_gk2.shape[1]
    NCH = S // GC
    ALPHA = float(np.float32(4 ** 0.25))
    SCALE = float(np.float32(QK ** -0.5))
    assert NC5 == P and G * GS == 256 and NT == 8 and RQ == 256 and RKV == P and D == 1024

    w_in0, w_in1 = even_w_in[0], odd_w_in[0]
    c_g0 = NA
    c_u = c_g0 + H * VD
    c_gs = c_u + W5
    c_gk = 2 * GKW + GW
    c_end0 = c_gs + W5

    with ExitStack() as ctx:
        def sem(name):
            return ctx.enter_context(nc.semaphore(name))

        base = (nc.sbuf_base + 31) // 32 * 32

        def at(name, offset, shape, dt=F32):
            return nc.alloc_sbuf_tensor_at(name, shape, dt, offset=base + offset * 4)

        cursor = [0]

        def own(name, shape, dt=F32):
            t = at(name, cursor[0], shape, dt)
            cursor[0] += (int(np.prod(shape[1:])) + 7) // 8 * 8
            return t

        ident = own("ident", [P, P])
        ident_b = own("ident_b", [P, P], BF16)
        causal_bias = own("causal_bias", [P, P], BF16)
        chunk_tri = own("chunk_tri", [P, GH, P], I32)
        sign = own("sign", [P, 2])
        eps = own("eps", [P, 2])
        norm_w = own("norm_w", [P, 3])
        pos_i = own("pos_i", [P, NT], I32)
        pos_f = own("pos_f", [P, NT])
        inv_freq = own("inv_freq", [P, HALF])
        rope_t = own("rope_t", [P, 4, NT, HALF])
        stat = own("stat", [P, 64])
        rsum = own("rsum", [P, 2, H])
        rinv = own("rinv", [P, 2, H])
        negmax = own("negmax", [P, 2])
        gla_c = own("gla_c", [P, 8])
        gk2 = own("gk2", [GR, GKW])
        o = cursor[0]
        rot = at("rot", o, [P, 3, 512])
        w_glu = at("w_glu", o + 1536, [P, 2, W5])
        ln_gb = at("ln_gb", o, [P, 2, D])
        cursor[0] += 2048

        RA = cursor[0]
        RB = RA + KD * S
        RC = RB + KD * c_end0
        RD = RC + 8192
        xT = at("xT", RA, [P, KD, S])
        kT = at("kT", RA, [QK, H, S])
        w_a = at("w_a", RB, [P, KD, NA])
        w_u = at("w_u", RB + 3328, [P, KD, W5])
        w_gs = at("w_gs", RB + 5376, [P, KD, W5])
        w_g = at("w_g", RB + 7424, [P, KD, H * VD])
        V = at("V", RC, [P, NT, H, VD])
        gate = at("gate", RC + 4096, [P, NT, H * VD])
        D1 = RD
        D2 = D1 + 3328
        D3 = D2 + 3072
        D4 = D3 + 2560
        D5 = D4 + 2048
        D6 = D5 + 768
        D7 = D6 + 2048
        RT = D7 + 2048
        cqkv = at("cqkv", D1, [P, NT, NA])
        prob = at("prob", D1, [P, 2, S])
        probT = at("probT", D1 + 2048, [P, 2, 512])
        cT = at("cT", D2, [P, 3, S])
        squared = at("squared", D2, [P, RQ + RKV])
        w_uq = at("w_uq", D3, [P, 2, H * QK])
        w_ukv = at("w_ukv", D3 + 1536, [P, 2, H, NOPE])
        x_ring = at("x_ring", D4, [P, 2, D])
        Kt = at("Kt", D4, [GS, G, LC, GS])
        kpeT = at("kpeT", D4, [QK, S])
        qTt = at("qTt", D4, [QK, 2, H, P])
        qt = at("qt", D5, [P, H, QK])
        gs5 = at("gs5", D6, [P, 2, S])
        U = at("U", D7, [P, G, LC, GS])
        UT = at("UT", D7, [P, G, NC5])
        Y5 = at("Y5", D1, [P, LC, G, GS])
        NTAB = LC + 1 + NC5
        tabA = at("tabA", RT, [P, G, NTAB])
        tabB = at("tabB", RT + G * NTAB, [P, G, NTAB])
        assert (RT + 2 * G * NTAB) * 4 <= nc.sbuf_usable_end - base, (RT + 2 * G * NTAB) * 4
        o = RC
        names = {}
        for name, shape, dt in (
            ("par", [G, 4, P], F32), ("dts", [G, 16], F32), ("dti", [G, 8], I32), ("parT", [P, 4, G], F32),
            ("sm", [P, 8, G], F32), ("ex", [P, 4, G * (LC + 1)], F32), ("exi", [P, G * (LC + 1)], I32),
            ("times", [P, NTAB], F32), ("BA", [P, G, GS], F32), ("BB", [P, G, GS], F32),
            ("crow", [P, 2, 2, P], F32), ("CA", [P, G, GS], F32),
            ("CB", [P, G, GS], F32), ("Dt", [GS, G], F32), ("DD", [GS, G, GS], F32),
        ):
            names[name] = at(name, o, shape, dt)
            o += (int(np.prod(shape[1:])) + 7) // 8 * 8
        assert o <= RC + 4096, o - RC
        par, dts, dti, parT, sm, ex, exi, times, BA, BB, crow, CA, CB, Dt, DD = names.values()
        NX = at("NX", RB, [P, G, LC + 1, GS])
        N2 = at("N2", RB + 2304, [P, G, LC, GS])
        M = at("M", RB + 4352, [P, G, LC, GS])
        TT = at("TT", RB + 4352, [P, G, P])
        work = at("work", RB + 6400, [P, 640])
        MT = at("MT", RB + 7424, [P, G, P])
        MTs = at("MTs", RB + 9472, [P, G, P])
        HC = at("HC", RB + 7424, [P, G, NC5])
        HS = at("HS", RB + 9472, [P, G, NC5])
        YT = at("YT", RB + 7424, [P, 2, S])
        OT = at("OT", RB + 7424, [P, H * VD // P, S])
        w_out0 = at("w_out0", RB, [P, MIX // P, D])
        SGL = at("SGL", D4, [P, 2, 512])
        Bst = at("Bst", D5, [P, G, GS])
        Bsw = at("Bsw", D5 + 256, [P, G, GS])
        LR = at("LR", RB + 7040, [P, G, LC + 1])
        LI = at("LI", RB + 7184, [P, G, LC + 1])
        mag8 = at("mag8", RB + 7328, [P, G])
        x_res = at("x_res", D1, [P, 2, D])
        zn = at("zn", D4, [P, 2, D])
        x1T = at("x1T", RA, [P, KD, S])
        w_ring = at("w_ring", RC, [P, 2, KD, 512])
        V1 = at("V1", RB, [P, NT, GW])
        dec = at("dec", RB + 8192, [P, 2, 2, 512])
        gkT = at("gkT", RB + 10240, [GR, S])
        E1 = RD
        QD = at("QD", E1, [P, GH, S])
        KI = at("KI", E1 + 4096, [P, GH, S])
        SG = at("SG", E1 + 8192, [P, NT, GW])
        E2 = E1 + 16384
        zb = at("zb", E2, [P, 2, 512])
        soft = at("soft", E2 + 1024, [P, 512])
        cum = at("cum", E2 + 1536, [P, 2, 512])
        resets = at("resets", E2 + 2560, [P, 512])
        ends = at("ends", E2 + 3072, [P, GH, NCH])
        w_gk = at("w_gk", E2 + 3136, [P, KD, GR])
        assert (E2 + 3136 + KD * GR) * 4 <= nc.sbuf_usable_end - base
        w_out1 = at("w_out1", RA, [P, KD, D])
        QD2 = at("QD2", RC, [P, GH, S])
        state = at("state", RC + 4096, [P, 2, GH, GDV])
        kTok = at("kTok", RC + 6144, [P, 2, GH, P])
        att = at("att", RC + 7168, [P, 2, GH, P])
        Y1 = at("Y1", RB + 8192, [P, GW])
        Y1T = at("Y1T", E2 + 1024, [P, KD, P])
        sq = at("sq", RB + 9216, [P, 256])
        zn1 = at("zn1", RB + 9472, [P, 2, D])
        x_res1 = at("x_res1", E2, [P, 1, D])

        vec_step, act_step, pool_step = sem("vec_step"), sem("act_step"), sem("pool_step")
        consts_set = sem("consts_set")
        x_loaded = [sem(f"x_loaded{s}") for s in range(2)]
        wa_loaded, wu_loaded, wgs_loaded, wg_loaded = map(sem, ("wa_loaded", "wu_loaded", "wgs_loaded", "wg_loaded"))
        small_loaded = sem("small_loaded")
        par_loaded, bc_loaded = sem("s5_par_loaded"), sem("s5_bc_loaded")
        mla_w_loaded, glu_w_loaded = sem("mla_w_loaded"), sem("glu_w_loaded")
        squares_done = sem("squares_done")
        latents_scaled = sem("latents_scaled")
        angles_set = sem("angles_set")
        sines_done = sem("sines_done")
        rope_set = sem("rope_set")
        keys_turned = sem("keys_turned")
        kpe_spread = sem("kpe_spread")
        pv_done = sem("pv_done")
        s5_par_set = sem("s5_par_set")
        s5_turns_set = sem("s5_turns_set")
        s5_phase_set = sem("s5_phase_set")
        s5_sin_set = sem("s5_sin_set")
        s5_cos_set = sem("s5_cos_set")
        s5_m_set, s5_b_set, s5_nx_set, s5_n2_set = map(sem, ("s5_m_set", "s5_b_set", "s5_nx_set", "s5_n2_set"))
        s5_d_added, s5_tt_zero, s5_tt_set = sem("s5_d_added"), sem("s5_tt_zero"), sem("s5_tt_set")
        s5_states_set = sem("s5_states_set")
        s5_out_set = sem("s5_out_set")
        q_turned = sem("q_turned")
        max_set, prob_set = sem("max_set"), sem("prob_set")
        gated = sem("gated")
        w_out0_loaded, ln0_loaded = sem("w_out0_loaded"), sem("ln0_loaded")
        xres_loaded = [sem(f"xres_loaded{s}") for s in range(2)]
        var_set, root_set, centred = sem("var_set"), sem("root_set"), sem("centred")
        x1_set = sem("x1_set")
        x1_stored = [sem(f"x1_stored{s}") for s in range(2)]
        w1_loaded = [sem(f"w1_loaded{s}") for s in range(2)]
        wgk_loaded = sem("wgk_loaded")
        soft_set, scanned, decay_set = sem("soft_set"), sem("scanned"), sem("decay_set")
        qk_set = sem("qk_set")
        w_out1_loaded, ln1_loaded = sem("w_out1_loaded"), sem("ln1_loaded")
        qd2_set, ms_set = sem("qd2_set"), sem("ms_set")
        x1_back = sem("x1_back")
        y_set = sem("y_set")
        y_stored = [sem(f"y_stored{s}") for s in range(2)]

        psum = ctx.enter_context(nc.psum_tensor("psum", [P, 8, 512], F32))
        x1_dram = nc.dram_tensor("x1_scratch", [S, D], F32, kind="Internal")
        x1_rows = x1_dram.ap() if not isinstance(x1_dram, bass.AP) else x1_dram

        plan = PsumPlan(sem)
        turn = [0]

        def ring(*job):
            plan.give(job, turn[0] % 8)
            turn[0] += 1

        for i in range(NT):
            ring("xT", i, 0)
            ring("xT", i, 1)
            if i:
                ring("ina", i - 1)
        ring("ina", NT - 1)
        ring("par")
        ring("crow")
        for t in range(LC):
            ring("inu", t)
        for m in range(2):
            for n in range(2):
                ring("ings", m, n)
        for q in range(4):
            ring("UT", q)
        for i in range(NT):
            ring("ing", i)
            ring("cT", i)
        for q in range(4):
            ring("MT", q)
        for q in range(4):
            ring("K", q)
        for q in range(4):
            ring("v", q)
            ring("vs", q)
        for p in range(H // 2):
            for n in range(2):
                ring("kp", p, n)
        for i in range(NT):
            ring("vp", i)
        for q in range(4):
            ring("y", q)
        for m in range(2):
            for n in range(2):
                ring("yT", m, n)
        for m in range(2):
            for n in range(2):
                ring("glu", m, n)

        heads = [(i, h) for i in range(NT) for h in range(H)]
        pt_jobs = {}
        count = 0
        for n, (i, h) in enumerate(heads):
            pt_jobs[i, h] = []
            for g in range(i // 4 + 1):
                pt_jobs[i, h].append((count, 4 * g, min(4, i + 1 - 4 * g)))
                count += 1

        def attention_steps():
            yield "q", 0
            yield "qT", 0
            yield "s", 0
            yield "s", 1
            for n, (i, h) in enumerate(heads):
                yield "pt", n
                if h == 1 and i + 1 < NT:
                    yield "q", i + 1
                if h == 3 and i + 1 < NT:
                    yield "qT", i + 1
                if n + 2 < len(heads):
                    yield "s", n + 2
                yield "av", n
                if h == 2 and i:
                    yield "OT", i - 1
            yield "OT", NT - 1

        for what, n in attention_steps():
            if what in ("q", "qT"):
                plan.give((what, n, 0), 6)
                plan.give((what, n, 1), 6)
            elif what == "s":
                plan.give(("s", n), 2 * (n % 2), 2 * (n % 2) + 1)
            elif what == "pt":
                for number, _, _ in pt_jobs[heads[n]]:
                    plan.give(("pt", number), 4 + number % 2)
            elif what == "av" and heads[n][1] == 0:
                plan.give(("o", heads[n][0]), 7)
            elif what == "OT":
                plan.give(("OT", n), 6)
        turn[0] = 0
        for i in range(NT):
            ring("z0", i, 0)
            ring("z0", i, 1)
            if i:
                ring("x1T", i - 1, 0)
                ring("x1T", i - 1, 1)
        ring("x1T", NT - 1, 0)
        ring("x1T", NT - 1, 1)
        for n in range(2):
            ring("gk", n)
        ring("gate", 0)
        for m in range(2 * GH):
            if m + 1 < 2 * GH:
                ring("gate", m + 1)
            ring("q1", m)
            ring("k1", m)
        for what in ("v1", "g1"):
            for c in range(2):
                for i in range(NT):
                    ring(what, c, i)

        def gla_steps():
            for i in range(NT + 1):
                if i < NT:
                    yield "kT1", i
                    yield "at", i
                    yield "ks", (i, 0)
                if i:
                    yield "yT1", i - 1
                    yield "z1", i - 1
                if i < NT:
                    yield "o", i
                    if i + 1 < NT:
                        yield "ks", (i, 1)

        for what, n in gla_steps():
            if what == "ks":
                ring("ks", *n, 0)
                ring("ks", *n, 1)
            elif what in ("kT1", "at"):
                ring(what, n)
            else:
                ring({"o": "o1"}.get(what, what), n, 0)
                ring({"o": "o1"}.get(what, what), n, 1)

        def bank(*job):
            return psum[:, plan.bank(job), :]

        def squares(act, step, i):
            plan.drained(act, ("ina", i))
            step(act.activation(squared[:, 0:RQ], cqkv[:, i, 0:RQ], ACT.Square, accum_out=stat[:, i:i + 1]))
            step(act.activation(squared[:, RQ:RQ + RKV], cqkv[:, i, RQ:RQ + RKV], ACT.Square,
                                accum_out=stat[:, 8 + i:9 + i]))

        def values_done(engine, number):
            n = next(n for n, key in enumerate(heads) if number in [j[0] for j in pt_jobs[key]])
            i, h = heads[n]
            if h == H - 1:
                plan.filled(engine, ("o", i))
            else:
                engine.wait_ge(pv_done, i * (H - 1) + h + 1)

        def copy_probs(engine, step, number, first, blocks):
            plan.filled(engine, ("pt", number))
            if number >= 2:
                values_done(engine, number - 2)
            dst, src = probT[:, number % 2, 0:blocks * P], bank("pt", number)[:, 0:blocks * P]
            ins = engine.activation(dst, src, ACT.Copy) if engine is nc.scalar else engine.tensor_copy(dst, src)
            step.frees(ins, ("pt", number))

        block = ctx.enter_context(nc.Block())

        @block.sync
        def _(sp):
            def rows(w, c0, c1):
                return w.rearrange("(k p) n -> p k n", p=P)[:, :, c0:c1]

            for i in range(NT):
                if i >= 2:
                    plan.filled(sp, ("xT", i - 2, 1))
                sp.dma_start(x_ring[:, i % 2, :], x[0, i * P:(i + 1) * P, :]).then_inc(x_loaded[i % 2], 16)
                if i == 1:
                    sp.dma_start(w_a[:, :, :], rows(w_in0, 0, NA)).then_inc(wa_loaded, 16)
                if i == 3:
                    sp.dma_start(w_u[:, :, :], rows(w_in0, c_u, c_u + W5)).then_inc(wu_loaded, 16)
                if i == 4:
                    sp.dma_start(w_gs[:, :, :], rows(w_in0, c_gs, c_gs + W5)).then_inc(wgs_loaded, 16)
                if i == 5:
                    sp.dma_start(w_g[:, :, :], rows(w_in0, c_g0, c_g0 + H * VD)).then_inc(wg_loaded, 16)
            sp.dma_start(w_uq[:, :, :], mla_w_uq[0].rearrange("(k p) n -> p k n", p=P)).then_inc(mla_w_loaded, 16)
            kv_cols = mla_w_ukv[0].rearrange("p (h s d) -> p s h d", h=H, s=2)
            for s in range(2):
                sp.dma_start(w_ukv[:, s, :, :], kv_cols[:, s, :, :]).then_inc(mla_w_loaded, 16)
            sp.dma_start(w_glu[:, :, :], s5_w_glu[0].rearrange("(k p) n -> p k n", p=P)).then_inc(glu_w_loaded, 16)
            sp.wait_ge(s5_tt_zero, 1)
            sp.wait_ge(s5_d_added, 1)
            for q in range(4):
                plan.drained(sp, ("K", q))
            for s in range(LC):
                sp.dma_start(TT[s * GS:(s + 1) * GS, :, s * GS:P],
                             Kt[:, :, 0:LC - s, :].rearrange("p g t h -> p g (t h)")).then_inc(s5_tt_set, 16)
            for i in range(NT):
                plan.drained(sp, ("cT", i))
            plan.filled(sp, ("ing", NT - 1))
            for h in range(H):
                sp.dma_start(kT[NOPE:QK, h, :], kpeT[NOPE:QK, :]).then_inc(kpe_spread, 16)
            plan.filled(sp, ("y", 3))
            sp.dma_start(w_out0[:, :, :], even_w_out[0].rearrange("(k p) n -> p k n", p=P)).then_inc(w_out0_loaded, 16)
            plan.filled(sp, ("o", NT - 1))
            plan.filled(sp, ("OT", NT - 1))
            sp.wait_ge(s5_out_set, 4)
            for n, w in enumerate((ln_g, ln_b)):
                sp.dma_start(ln_gb[:, n, :], w[0:1, :].partition_broadcast(P)).then_inc(ln0_loaded, 16)
            w1_pieces = [(0, 512), (GKW, GKW + 512), (2 * GKW, 2 * GKW + 512), (2 * GKW + 512, 2 * GKW + 1024),
                         (c_gk + GR, c_gk + GR + 512), (c_gk + GR + 512, c_gk + GR + 1024)]
            w1_last = [("q1", 7), ("k1", 7), ("v1", 0, NT - 1), ("v1", 1, NT - 1)]

            def w1_load(n):
                if n >= 2:
                    plan.filled(sp, w1_last[n - 2])
                sp.dma_start(w_ring[:, n % 2, :, :], rows(w_in1, *w1_pieces[n])).then_inc(w1_loaded[n % 2], 16)

            for i in range(NT):
                if i >= 2:
                    plan.drained(sp, ("z0", i - 2, 1))
                sp.dma_start(x_res[:, i % 2, :], x[0, i * P:(i + 1) * P, :]).then_inc(xres_loaded[i % 2], 16)
                if i < 2:
                    w1_load(i)
                if i >= 2:
                    sp.wait_ge(x1_set, i - 1)
                    sp.dma_start(x1_rows[(i - 2) * P:(i - 1) * P, :], zn[:, i % 2, :]).then_inc(x1_stored[i % 2], 16)
            for i in range(NT - 2, NT):
                sp.wait_ge(x1_set, i + 1)
                sp.dma_start(x1_rows[i * P:(i + 1) * P, :], zn[:, i % 2, :]).then_inc(x1_stored[i % 2], 16)
            sp.dma_start(w_gk[:, :, :], rows(w_in1, c_gk, c_gk + GR)).then_inc(wgk_loaded, 16)
            for n, w in enumerate((ln_g, ln_b)):
                sp.dma_start(ln_gb[:, n, :], w[1:2, :].partition_broadcast(P)).then_inc(ln1_loaded, 16)
            for n in range(2, 6):
                w1_load(n)
            plan.filled(sp, ("g1", 1, NT - 1))
            sp.dma_start(w_out1[:, :, :], odd_w_out[0].rearrange("(k p) n -> p k n", p=P)).then_inc(w_out1_loaded, 16)
            for s in range(2):
                sp.wait_ge(x1_stored[s], 16 * NT // 2)
            for i in range(NT):
                if i:
                    plan.drained(sp, ("z1", i - 1, 1))
                else:
                    plan.drained(sp, ("k1", 7))
                    sp.wait_ge(decay_set, 2 * GH)
                sp.dma_start(x_res1[:, 0, :], x1_rows[i * P:(i + 1) * P, :]).then_inc(x1_back, 16)
                if i:
                    sp.wait_ge(y_set, i)
                    sp.dma_start(out[0, (i - 1) * P:i * P, :], zn1[:, (i - 1) % 2, :]).then_inc(y_stored[(i - 1) % 2], 16)
            sp.wait_ge(y_set, NT)
            sp.dma_start(out[0, (NT - 1) * P:, :], zn1[:, (NT - 1) % 2, :]).then_inc(y_stored[(NT - 1) % 2], 16)
            for s in range(2):
                sp.wait_ge(y_stored[s], 16 * NT // 2)

        @block.gpsimd
        def _(pool):
            step = Steps(pool, pool_step, plan)
            step(pool.memset(ident[:, :], 0.0))
            step(pool.memset(ident_b[:, :], 0.0))
            step(pool.memset(causal_bias[:, :], 0.0))
            step(pool.memset(chunk_tri[:, :, :], 1))
            step(pool.memset(sign[:, :], 1.0))
            step(pool.memset(eps[:, 0:1], 1e-5))
            step(pool.memset(eps[:, 1:2], 1e-6))
            for j in range(HALF):
                step(pool.memset(inv_freq[:, j:j + 1],
                                 float(np.float32(10000.0) ** np.float32(-j / HALF))))
            step(pool.iota(times[:, 0:LC + 1], [[1, LC + 1]], base=0, channel_multiplier=0,
                           allow_small_or_imprecise_dtypes=True))
            step(pool.iota(times[:, LC + 1:NTAB], [[LC, NC5]], base=0, channel_multiplier=0,
                           allow_small_or_imprecise_dtypes=True))
            step.settle()
            step(pool.affine_select(out=ident[:, :], in_=ident[:, :], compare_op=ALU.not_equal, fill=1.0,
                                    base=0, pattern=[[-1, P]], channel_multiplier=1))
            step(pool.affine_select(out=ident_b[:, :], in_=ident_b[:, :], compare_op=ALU.not_equal, fill=1.0,
                                    base=0, pattern=[[-1, P]], channel_multiplier=1))
            step(pool.affine_select(out=causal_bias[:, :], in_=causal_bias[:, :], compare_op=ALU.is_ge,
                                    fill=-1e38, base=0, pattern=[[-1, P]], channel_multiplier=1))
            step(pool.affine_select(out=chunk_tri[:, :, :], in_=chunk_tri[:, :, :], compare_op=ALU.is_ge,
                                    fill=0.0, base=0, pattern=[[0, GH], [1, P]], channel_multiplier=-1))
            step.settle()
            step(pool.memset(chunk_tri[0:GC, :, GC:P], 0))
            step(pool.memset(sign[0:NS, 0:1], -1.0))
            step(pool.memset(sign[NS:P, 1:2], -1.0))
            step.settle()
            step(pool.memset(stat[:, :], 0.0), consts_set)

            pool.wait_ge(s5_turns_set, 1)
            hi = sm[:, 4, :].unsqueeze(2).to_broadcast([P, G, NTAB])
            lo = sm[:, 5, :].unsqueeze(2).to_broadcast([P, G, NTAB])
            tb = times[:, :].unsqueeze(1).to_broadcast([P, G, NTAB])
            step(pool.tensor_tensor(tabA[:, :, :], hi, tb, ALU.mult))
            step(pool.tensor_tensor(tabB[:, :, :], lo, tb, ALU.mult))
            step.settle()

            def drop_turns(signal=None):
                for g in range(0, G, 8):
                    w = rot[:, :, :].rearrange("p a b -> p (a b)")[:, 0:8 * NTAB].rearrange("p (g t) -> p g t", g=8)
                    part = tabA[:, g:g + 8, :]
                    step(pool.tensor_scalar(w, part, TO_INT, None, ALU.add))
                    step.settle()
                    step(pool.tensor_scalar(w, w, TO_INT, None, ALU.subtract))
                    step.settle()
                    step(pool.tensor_tensor(part, part, w, ALU.subtract), signal if g else None)
                    step.settle()

            drop_turns()
            step(pool.tensor_tensor(tabA[:, :, :], tabA[:, :, :], tabB[:, :, :], ALU.add))
            step.settle()
            drop_turns(s5_phase_set)

            def turn_pairs(x1, x2, cos, sin, t1, t2, t3, t4, last):
                step(pool.tensor_tensor(t1, x1, cos, ALU.mult))
                step(pool.tensor_tensor(t2, x2, sin, ALU.mult))
                step(pool.tensor_tensor(t3, x2, cos, ALU.mult))
                step(pool.tensor_tensor(t4, x1, sin, ALU.mult))
                step.settle()
                step(pool.tensor_tensor(x1, t1, t2, ALU.subtract))
                step(pool.tensor_tensor(x2, t3, t4, ALU.add), last)

            pool.wait_ge(rope_set, 1)
            for i in range(NT):
                plan.drained(pool, ("ina", i))
            temps = [rot[:, 0, 128 * j:128 * (j + 1)].rearrange("p (t r) -> p t r", r=HALF) for j in range(4)]
            k0 = RQ + RKV
            turn_pairs(cqkv[:, :, k0:k0 + HALF], cqkv[:, :, k0 + HALF:k0 + ROPE], rope_t[:, 2, :, :],
                       rope_t[:, 3, :, :], *temps, keys_turned)
            plan.filled(pool, ("MT", 3))
            step(pool.memset(TT[:, :, :], 0.0), s5_tt_zero)
            pool.wait_ge(s5_n2_set, 4)
            temps = [work[:, 128 * j:128 * (j + 1)].rearrange("p (h r) -> p h r", r=HALF) for j in range(4)]
            for i in range(NT):
                plan.drained(pool, ("q", i, 0))
                plan.drained(pool, ("q", i, 1))
                cos = rope_t[:, 2, i, :].unsqueeze(1).to_broadcast([P, H, HALF])
                sin = rope_t[:, 3, i, :].unsqueeze(1).to_broadcast([P, H, HALF])
                turn_pairs(qt[:, :, NOPE:NOPE + HALF], qt[:, :, NOPE + HALF:QK], cos, sin, *temps, q_turned)

            pool.wait_ge(ln0_loaded, 32)
            for i in range(NT):
                pool.wait_ge(centred, i + 1)
                z = zn[:, i % 2, :]
                step(pool.tensor_tensor(z, z, ln_gb[:, 0, :], ALU.mult))
                step.settle()
                step(pool.tensor_tensor(z, z, ln_gb[:, 1, :], ALU.add), x1_set)

            pool.wait_ge(ln1_loaded, 32)
            plan.filled(pool, ("g1", 1, NT - 1))
            pool.wait_ge(qk_set, 2 * GH)
            for i in range(NT + 1):
                if i < NT:
                    for c in range(2):
                        n = 2 * i + c
                        if n:
                            s = slice(n * GC, (n + 1) * GC)
                            step(pool.tensor_tensor(QD2[:, :, s], QD[:, :, s],
                                                    ends[:, :, n - 1:n].to_broadcast([P, GH, GC]), ALU.mult),
                                 qd2_set)
                if i:
                    pool.wait_ge(centred, NT + i)
                    z = zn1[:, (i - 1) % 2, :]
                    step(pool.tensor_tensor(z, z, ln_gb[:, 0, :], ALU.mult))
                    step.settle()
                    step(pool.tensor_tensor(z, z, ln_gb[:, 1, :], ALU.add), y_set)

        @block.scalar
        def _(act):
            step = Steps(act, act_step, plan)
            act.dma_start(pos_i[:, :], positions[0].rearrange("(t p) -> p t", p=P),
                          allow_slow_non_contiguous=True).then_inc(small_loaded, 16)
            act.dma_start(norm_w[:, 0:2], mla_q_norm[0].rearrange("(k p) -> p k", p=P),
                          allow_slow_non_contiguous=True).then_inc(small_loaded, 16)
            act.dma_start(norm_w[:, 2:3], mla_kv_norm[0].rearrange("(k p) -> p k", p=P),
                          allow_slow_non_contiguous=True).then_inc(small_loaded, 16)
            act.dma_start(gla_c[:, 0:4], gla_b_gk[0].rearrange("(k p) -> p k", p=P),
                          allow_slow_non_contiguous=True).then_inc(small_loaded, 16)
            act.dma_start(gla_c[:, 4:6], gla_g_norm[0].rearrange("(k p) -> p k", p=P),
                          allow_slow_non_contiguous=True).then_inc(small_loaded, 16)
            act.dma_start(gla_c[:, 6:8], s5_b_glu[0].rearrange("(k p) -> p k", p=P),
                          allow_slow_non_contiguous=True).then_inc(small_loaded, 16)
            act.dma_start(gk2[:, :], gla_w_gk2[0]).then_inc(small_loaded, 16)
            act.dma_start(Dt[:, :], s5_d[0].rearrange("(g h) -> h g", g=G),
                          allow_slow_non_contiguous=True).then_inc(bc_loaded, 16)
            for half in range(2):
                s = slice(half * NS, (half + 1) * NS)
                act.dma_start(par[:, 2, s], s5_a_re[0]).then_inc(par_loaded, 16)
                act.dma_start(par[:, 3, s], s5_a_im[0]).then_inc(par_loaded, 16)
            act.dma_start(dts[:, 0:1], s5_log_dt[0].rearrange("(g a) -> g a", a=1),
                          allow_slow_non_contiguous=True).then_inc(par_loaded, 16)
            re_im = (s5_b_re, s5_b_im)
            for half in range(2):
                s = slice(half * NS, (half + 1) * NS)
                act.dma_start(BA[s, :, :], re_im[half][0].rearrange("g p h -> p g h")).then_inc(bc_loaded, 16)
                act.dma_start(BB[s, :, :], re_im[1 - half][0].rearrange("g p h -> p g h")).then_inc(bc_loaded, 16)
            c_re_im = (s5_c_re, s5_c_im)
            for swap in range(2):
                for half in range(2):
                    src = c_re_im[half ^ swap][0].rearrange("(r g) h p -> (g h) r p", r=2)
                    act.dma_start(crow[:, swap, :, half * NS:(half + 1) * NS], src).then_inc(bc_loaded, 16)

            act.wait_ge(consts_set, 1)
            for i in range(NT):
                plan.filled(act, ("xT", i, 1))
                step.frees(act.activation(xT[:, 4:8, i * P:(i + 1) * P],
                                          bank("xT", i, 1).rearrange("p (k t) -> p k t", k=4), ACT.Copy),
                           ("xT", i, 1))
                if i:
                    squares(act, step, i - 1)
            squares(act, step, NT - 1)
            step.settle()
            step(act.activation(stat[:, 16:24], stat[:, 0:8], ACT.Sqrt, bias=eps[:, 1:2], scale=1.0 / RQ))
            step(act.activation(stat[:, 24:32], stat[:, 8:16], ACT.Sqrt, bias=eps[:, 1:2], scale=1.0 / RKV),
                 squares_done)
            for t in range(LC):
                plan.filled(act, ("inu", t))
                step.frees(act.activation(U[:, :, t, :], bank("inu", t)[:, 0:W5].rearrange("p (g h) -> p g h", g=G),
                                          ACT.Copy), ("inu", t))
            act.wait_ge(angles_set, 1)
            step(act.activation(rope_t[:, 3, :, :], rope_t[:, 0, :, :], ACT.Sin))
            step(act.activation(rope_t[:, 2, :, :], rope_t[:, 0, :, :], ACT.Sin, scale=0.5), sines_done)
            for m in range(2):
                for n in range(2):
                    plan.filled(act, ("ings", m, n))
                    step.frees(act.activation(gs5[:, m, n * 512:(n + 1) * 512], bank("ings", m, n), ACT.Silu),
                               ("ings", m, n))
            for i in range(NT):
                plan.filled(act, ("ing", i))
                step.frees(act.activation(gate[:, i, :], bank("ing", i), ACT.Silu), ("ing", i))
                if i == 0:
                    act.wait_ge(s5_phase_set, 1)
                    step(act.activation(tabB[:, :, :], tabA[:, :, :], ACT.Sin, scale=2 * PI_BELOW))
                    step.settle()
                    step(act.activation(tabA[:, :, :], tabA[:, :, :], ACT.Sin, scale=PI_BELOW), s5_sin_set)
            for q in range(4):
                plan.filled(act, ("K", q))
                step.frees(act.activation(Kt[:, 4 * q:4 * q + 4, :, :].rearrange("p g t h -> p (g t h)"),
                                          bank("K", q)[0:GS, :], ACT.Copy), ("K", q))
            act.wait_ge(s5_n2_set, 4)
            act.wait_ge(s5_d_added, 1)
            for i in range(NT):
                plan.filled(act, ("vp", i))
                step.frees(act.activation(V[:, i, :, :], bank("vp", i).rearrange("p (h d) -> p h d", h=H), ACT.Copy),
                           ("vp", i))
            for q in range(4):
                plan.filled(act, ("y", q))
                step.frees(act.activation(Y5[:, :, 4 * q:4 * q + 4, :],
                                          bank("y", q).rearrange("p (g t h) -> p t g h", g=4, t=LC),
                                          ACT.Gelu_apprx_tanh), ("y", q))
            act.wait_ge(small_loaded, 16 * 7)
            act.wait_ge(kpe_spread, 16 * H)
            act.wait_ge(s5_tt_set, 16 * LC)
            for k, (m, n) in enumerate((m, n) for m in range(2) for n in range(2)):
                plan.filled(act, ("glu", m, n))
                if k >= 2:
                    act.wait_ge(s5_out_set, k - 1)
                step.frees(act.activation(SGL[:, k % 2, :], bank("glu", m, n), ACT.Sigmoid, bias=gla_c[:, 6 + m:7 + m]),
                           ("glu", m, n))
            def exponentials(n):
                i, h = heads[n]
                w = (i + 1) * P
                scores = psum[:, 2 * (n % 2):2 * (n % 2) + 2, :].rearrange("p a b -> p (a b)")[:, 0:w]
                act.wait_ge(max_set, n + 1)
                if n >= 2:
                    plan.filled(act, ("pt", pt_jobs[heads[n - 2]][-1][0]))
                step.frees(act.activation(prob[:, n % 2, 0:w], scores, ACT.Exp, bias=negmax[:, n % 2:n % 2 + 1],
                                          accum_out=rsum[:, i % 2, h:h + 1]), ("s", n))

            for what, n in attention_steps():
                if what == "q":
                    for half in range(2):
                        plan.filled(act, ("q", n, half))
                        step.frees(act.activation(qt[:, 4 * half:4 * half + 4, :],
                                                  bank("q", n, half)[:, 0:4 * QK].rearrange("p (h d) -> p h d", h=4),
                                                  ACT.Copy, scale=SCALE), ("q", n, half))
                elif what == "s" and n == 0:
                    exponentials(0)
                elif what == "pt":
                    if n + 1 < len(heads):
                        exponentials(n + 1)
                    for number, first, blocks in pt_jobs[heads[n]][1:]:
                        copy_probs(act, step, number, first, blocks)
            for i in range(NT + 1):
                if i < NT:
                    act.wait_ge(var_set, i + 1)
                    step(act.activation(stat[:, 20:21], stat[:, 1:2], ACT.Sqrt, bias=eps[:, 0:1]), root_set)
                if i:
                    plan.filled(act, ("x1T", i - 1, 1))
                    step.frees(act.activation(x1T[:, 4:8, (i - 1) * P:i * P],
                                              bank("x1T", i - 1, 1).rearrange("p (k t) -> p k t", k=4), ACT.Copy),
                               ("x1T", i - 1, 1))
            for n in range(2):
                plan.filled(act, ("gk", n))
                step.frees(act.activation(gkT[:, n * 512:(n + 1) * 512], bank("gk", n)[0:GR, :], ACT.Copy), ("gk", n))
            for m in range(2 * GH + 1):
                if m < 2 * GH:
                    plan.filled(act, ("gate", m))
                    if m >= 2:
                        act.wait_ge(scanned, m - 1)
                    step.frees(act.activation(zb[:, m % 2, :], bank("gate", m), ACT.Identity,
                                              bias=gla_c[:, m // 2:m // 2 + 1]), ("gate", m))
                    step.settle()
                    if m:
                        act.wait_ge(scanned, m)
                    step(act.activation(soft[:, :], zb[:, m % 2, :], ACT.Abs))
                    step.settle()
                    step(act.activation(soft[:, :], soft[:, :], ACT.Exp, scale=-1.0))
                    step.settle()
                    step(act.activation(soft[:, :], soft[:, :], ACT.Ln, bias=1.0), soft_set)
                if m:
                    act.wait_ge(scanned, m)
                    if m >= 3:
                        act.wait_ge(qk_set, m - 2)
                    s = (m - 1) % 2
                    step(act.activation(dec[:, s, 0, :], cum[:, s, :], ACT.Exp, scale=1.0 / 16))
                    step(act.activation(dec[:, s, 1, :], cum[:, s, :], ACT.Exp, scale=-1.0 / 16), decay_set)
            for c in range(2):
                for i in range(NT):
                    plan.filled(act, ("v1", c, i))
                    step.frees(act.activation(V1[:, i, c * 512:(c + 1) * 512], bank("v1", c, i), ACT.Copy),
                               ("v1", c, i))
            for s in range(2):
                act.wait_ge(x1_stored[s], 16 * NT // 2)
            for c in range(2):
                for i in range(NT):
                    plan.filled(act, ("g1", c, i))
                    step.frees(act.activation(SG[:, i, c * 512:(c + 1) * 512], bank("g1", c, i), ACT.Silu),
                               ("g1", c, i))
            for what, i in gla_steps():
                if what == "kT1":
                    plan.filled(act, ("kT1", i))
                    if i >= 2:
                        plan.filled(act, ("ks", i - 2, 1, 1))
                    step.frees(act.activation(kTok[:, i % 2, :, :], bank("kT1", i).rearrange("p (h d) -> p h d", h=GH),
                                              ACT.Copy), ("kT1", i))
                elif what == "o":
                    for hp in range(2):
                        plan.filled(act, ("o1", i, hp))
                        for j in range(2):
                            step(act.activation(sq[:, :], bank("o1", i, hp)[:, j * GDV:(j + 1) * GDV], ACT.Square,
                                                accum_out=stat[:, 32 + 2 * hp + j:33 + 2 * hp + j]))
                            step.settle()
                    step(act.activation(stat[:, 40:44], stat[:, 32:36], ACT.Sqrt, bias=eps[:, 1:2], scale=1.0 / GDV),
                         ms_set)
                elif what == "z1":
                    act.wait_ge(var_set, NT + i + 1)
                    step(act.activation(stat[:, 20:21], stat[:, 1:2], ACT.Sqrt, bias=eps[:, 0:1]), root_set)

        @block.vector
        def _(vec):
            step = Steps(vec, vec_step, plan)
            C1, C2, C3 = two_pi_parts()
            INV_2PI = float(np.float32(1 / (2 * math.pi)))

            def serial(ins, signal=None):
                step(ins, signal)
                step.settle()

            def reduce_angle(angle, turns, signal=None):
                serial(vec.tensor_scalar(turns, angle, INV_2PI, TO_INT, ALU.mult, ALU.add))
                serial(vec.tensor_scalar(turns, turns, TO_INT, None, ALU.subtract))
                for part in (C1, C2, C3):
                    serial(vec.scalar_tensor_tensor(angle, turns, -part, angle, ALU.mult, ALU.add))
                serial(vec.tensor_scalar(angle, angle, PI_BELOW, -PI_BELOW, ALU.min, ALU.max), signal)

            def exact_exp(y, t, r, k_int):
                serial(vec.tensor_scalar(y, y, 88.8, -88.0, ALU.min, ALU.max))
                serial(vec.tensor_scalar(t, y, float(np.float32(1 / math.log(2))), TO_INT, ALU.mult, ALU.add))
                serial(vec.tensor_scalar(t, t, TO_INT, None, ALU.subtract))
                serial(vec.scalar_tensor_tensor(r, t, -0.693359375, y, ALU.mult, ALU.add))
                serial(vec.scalar_tensor_tensor(r, t, 2.12194440e-4, r, ALU.mult, ALU.add))
                serial(vec.tensor_scalar(y, r, 1.0 / math.factorial(7), None, ALU.mult))
                for k in range(6, 0, -1):
                    serial(vec.scalar_tensor_tensor(y, y, 1.0 / math.factorial(k), r, ALU.add, ALU.mult))
                serial(vec.tensor_scalar(t, t, 127.0, float(2 ** 23), ALU.add, ALU.mult))
                serial(vec.tensor_copy(k_int, t))
                serial(vec.scalar_tensor_tensor(y, y, 1.0, k_int.bitcast(F32), ALU.add, ALU.mult))

            def layer_norm(zt, res, job, i, tile_no):
                for n in range(2):
                    plan.filled(vec, (job, i, n))
                    s = slice(n * 512, (n + 1) * 512)
                    step.frees(vec.scalar_tensor_tensor(zt[:, s], res[:, s], ALPHA, bank(job, i, n),
                                                        ALU.mult, ALU.add), (job, i, n))
                    step.settle()
                    serial(vec.bn_stats(stat[:, 48 + 6 * n:54 + 6 * n], zt[:, s]))
                serial(vec.bn_aggr(stat[:, 0:2], stat[:, 48:60]), var_set)
                vec.wait_ge(root_set, tile_no + 1)
                serial(vec.reciprocal(stat[:, 21:22], stat[:, 20:21]))
                step(vec.tensor_scalar(zt, zt, stat[:, 0:1], stat[:, 21:22], ALU.subtract, ALU.mult), centred)

            vec.wait_ge(consts_set, 1)
            for i in range(NT + 1):
                if i < NT:
                    plan.filled(vec, ("xT", i, 0))
                    step.frees(vec.tensor_copy(xT[:, 0:4, i * P:(i + 1) * P],
                                               bank("xT", i, 0).rearrange("p (k t) -> p k t", k=4)), ("xT", i, 0))
                if i == 1:
                    vec.wait_ge(par_loaded, 16 * 5)
                    exact_exp(dts[:, 0:1], dts[:, 1:2], dts[:, 2:3], dti[:, 0:1])
                    step(vec.tensor_scalar(par[:, 0, :], par[:, 2, :], dts[:, 0:1], None, ALU.mult))
                    step(vec.tensor_scalar(par[:, 1, :], par[:, 3, :], dts[:, 0:1], None, ALU.mult), s5_par_set)
                if i:
                    plan.filled(vec, ("ina", i - 1))
                    step.frees(vec.tensor_copy(cqkv[:, i - 1, :], bank("ina", i - 1)[:, 0:NA]), ("ina", i - 1))
            vec.wait_ge(small_loaded, 16 * 7)
            serial(vec.tensor_copy(pos_f[:, :], pos_i[:, :]))
            serial(vec.tensor_tensor(rope_t[:, 0, :, :], pos_f[:, :].unsqueeze(2).to_broadcast([P, NT, HALF]),
                                     inv_freq[:, :].unsqueeze(1).to_broadcast([P, NT, HALF]), ALU.mult))
            reduce_angle(rope_t[:, 0, :, :], rope_t[:, 1, :, :], angles_set)
            plan.filled(vec, ("par",))
            step.frees(vec.tensor_copy(parT[:, :, :], bank("par")[:, 0:4 * G].rearrange("p (a g) -> p a g", a=4)),
                       ("par",))
            step.settle()
            serial(vec.tensor_copy(sm[:, 0, :], parT[:, 1, :]))
            reduce_angle(sm[:, 0, :], sm[:, 1, :])
            serial(vec.tensor_scalar(sm[:, 0, :], sm[:, 0, :], INV_2PI, None, ALU.mult))
            serial(vec.tensor_scalar(sm[:, 4, :], sm[:, 0, :], TO_13_BITS, None, ALU.add))
            serial(vec.tensor_scalar(sm[:, 4, :], sm[:, 4, :], TO_13_BITS, None, ALU.subtract))
            serial(vec.tensor_tensor(sm[:, 5, :], sm[:, 0, :], sm[:, 4, :], ALU.subtract), s5_turns_set)
            e4 = [ex[:, j, :].rearrange("p (g t) -> p g t", g=G) for j in range(4)]
            serial(vec.tensor_tensor(e4[0], parT[:, 0, :].unsqueeze(2).to_broadcast([P, G, LC + 1]),
                                     times[:, 0:LC + 1].unsqueeze(1).to_broadcast([P, G, LC + 1]), ALU.mult))
            exact_exp(ex[:, 0, :], ex[:, 1, :], ex[:, 2, :], exi[:, :])
            plan.filled(vec, ("crow",))
            cps = bank("crow").rearrange("p (s n) -> p s n", s=2)
            step(vec.tensor_scalar(CA[:, :, :].rearrange("p g h -> p (g h)"), cps[:, 0, :], sign[:, 1:2], None,
                                   ALU.mult))
            step.frees(vec.tensor_copy(CB[:, :, :].rearrange("p g h -> p (g h)"), cps[:, 1, :]), ("crow",))

            vec.wait_ge(squares_done, 1)
            serial(vec.reciprocal(stat[:, 32:48], stat[:, 16:32]))
            for i in range(NT):
                step(vec.tensor_scalar(cqkv[:, i, 0:RQ], cqkv[:, i, 0:RQ], stat[:, 32 + i:33 + i], None, ALU.mult))
                step(vec.tensor_scalar(cqkv[:, i, RQ:RQ + RKV], cqkv[:, i, RQ:RQ + RKV], stat[:, 40 + i:41 + i],
                                       None, ALU.mult), latents_scaled)
            vec.wait_ge(sines_done, 1)
            serial(vec.scalar_tensor_tensor(rope_t[:, 2, :, :], rope_t[:, 2, :, :], -2.0, rope_t[:, 2, :, :],
                                            ALU.mult, ALU.mult))
            serial(vec.tensor_scalar(rope_t[:, 2, :, :], rope_t[:, 2, :, :], 1.0, None, ALU.add), rope_set)
            for q in range(4):
                plan.filled(vec, ("UT", q))
                step.frees(vec.tensor_copy(UT[:, 4 * q:4 * q + 4, :].rearrange("p g c -> p (g c)"), bank("UT", q)),
                           ("UT", q))
            vec.wait_ge(s5_sin_set, 1)
            plan.filled(vec, ("ings", 1, 1))
            serial(vec.scalar_tensor_tensor(tabA[:, :, :], tabA[:, :, :], -2.0, tabA[:, :, :], ALU.mult, ALU.mult))
            powers = slice(0, LC + 1)
            step(vec.tensor_tensor(LR[:, :, :], e4[0], tabA[:, :, powers], ALU.mult))
            step(vec.tensor_tensor(LI[:, :, :], e4[0], tabB[:, :, powers], ALU.mult))
            step(vec.tensor_copy(mag8[:, :], e4[0][:, :, LC]))
            serial(vec.tensor_scalar(sm[:, 0, :], e4[0][:, :, 1], -1.0, None, ALU.add))
            nr, ni, ar, ai = sm[:, 0, :], LI[:, :, 1], parT[:, 2, :], parT[:, 3, :]
            serial(vec.tensor_tensor(nr, nr, LR[:, :, 1], ALU.add))
            step(vec.tensor_tensor(LR[:, :, :], LR[:, :, :], e4[0], ALU.add))
            step(vec.tensor_scalar(tabA[:, :, :], tabA[:, :, :], 1.0, None, ALU.add))
            den, t1, t2, zr, zi, zs = (sm[:, j, :] for j in (1, 2, 3, 4, 5, 6))
            step(vec.tensor_tensor(t1, ar, ar, ALU.mult))
            step(vec.tensor_tensor(t2, ai, ai, ALU.mult))
            step.settle()
            serial(vec.tensor_tensor(den, t1, t2, ALU.add))
            serial(vec.reciprocal(den, den))
            step(vec.tensor_tensor(t1, nr, ar, ALU.mult))
            step(vec.tensor_tensor(t2, ni, ai, ALU.mult))
            step.settle()
            serial(vec.tensor_tensor(zr, t1, t2, ALU.add))
            step(vec.tensor_tensor(t1, ni, ar, ALU.mult))
            step(vec.tensor_tensor(t2, nr, ai, ALU.mult))
            step.settle()
            serial(vec.tensor_tensor(zi, t1, t2, ALU.subtract))
            step(vec.tensor_tensor(zr, zr, den, ALU.mult))
            serial(vec.tensor_tensor(zi, zi, den, ALU.mult))
            serial(vec.tensor_scalar(zs, zi, sign[:, 0:1], None, ALU.mult))
            vec.wait_ge(bc_loaded, 16 * 9)
            wide = [P, G, GS]
            zr_b, zs_b = zr.unsqueeze(2).to_broadcast(wide), zs.unsqueeze(2).to_broadcast(wide)
            w0 = work[:, 0:G * GS].rearrange("p (g h) -> p g h", g=G)
            w1 = work[:, G * GS:2 * G * GS].rearrange("p (g h) -> p g h", g=G)
            step(vec.tensor_tensor(Bst[:, :, :], BA[:, :, :], zr_b, ALU.mult))
            step(vec.tensor_tensor(w0, BB[:, :, :], zs_b, ALU.mult))
            step(vec.tensor_tensor(Bsw[:, :, :], BB[:, :, :], zr_b, ALU.mult))
            step(vec.tensor_tensor(w1, BA[:, :, :], zs_b, ALU.mult))
            step.settle()
            step(vec.tensor_tensor(Bst[:, :, :], Bst[:, :, :], w0, ALU.add), s5_b_set)
            serial(vec.tensor_tensor(Bsw[:, :, :], Bsw[:, :, :], w1, ALU.subtract))

            def outer(dst, n, a, left, b, right, op, signal):
                for q in range(4):
                    g = slice(4 * q, 4 * q + 4)
                    shape = [P, 4, n, GS]
                    w = work[:, 0:4 * n * GS].rearrange("p (g t h) -> p g t h", g=4, t=n)
                    step(vec.tensor_tensor(dst[:, g, :, :], a[:, g, :].unsqueeze(3).to_broadcast(shape),
                                           left[:, g, :].unsqueeze(2).to_broadcast(shape), ALU.mult))
                    step(vec.tensor_tensor(w, b[:, g, :].unsqueeze(3).to_broadcast(shape),
                                           right[:, g, :].unsqueeze(2).to_broadcast(shape), ALU.mult))
                    step.settle()
                    step(vec.tensor_tensor(dst[:, g, :, :], dst[:, g, :, :], w, op), signal)

            LIs = ex[:, 1, :].rearrange("p (g t) -> p g t", g=G)
            serial(vec.tensor_scalar(LIs, LI[:, :, :], sign[:, 0:1], None, ALU.mult))
            for t in range(LC):
                j = LC - 1 - t
                a = LR[:, :, j].unsqueeze(2).to_broadcast(wide)
                b = LIs[:, :, j].unsqueeze(2).to_broadcast(wide)
                step(vec.tensor_tensor(M[:, :, t, :], Bst[:, :, :], a, ALU.mult))
                step(vec.tensor_tensor(w0 if t % 2 else w1, Bsw[:, :, :], b, ALU.mult))
                step.settle()
                step(vec.tensor_tensor(M[:, :, t, :], M[:, :, t, :], w0 if t % 2 else w1, ALU.add), s5_m_set)
            outer(NX, LC + 1, LR[:, :, :], CA, LI[:, :, :], CB, ALU.subtract, s5_nx_set)
            outer(N2, LC, LR[:, :, 1:LC + 1], CB, LI[:, :, 1:LC + 1], CA, ALU.add, s5_n2_set)
            for i in range(NT):
                plan.filled(vec, ("cT", i))
                s = slice(i * P, (i + 1) * P)
                step(vec.tensor_tensor(cT[:, :, s], bank("cT", i)[:, 0:384].rearrange("p (k t) -> p k t", k=3),
                                       norm_w[:, :].unsqueeze(2).to_broadcast([P, 3, P]), ALU.mult))
                step.frees(vec.tensor_copy(kpeT[NOPE:QK, s], bank("cT", i)[0:ROPE, 384:512]), ("cT", i))
            for q in range(4):
                plan.filled(vec, ("MT", q))
                if q == 0:
                    plan.filled(vec, ("ing", NT - 1))
                g = slice(4 * q, 4 * q + 4)
                src = bank("MT", q).rearrange("p (g s) -> p g s", g=4)
                step(vec.tensor_copy(MT[:, g, :], src))
                step(vec.tensor_copy(MTs[:, g, 0:NS], src[:, :, NS:P]))
                step.frees(vec.tensor_copy(MTs[:, g, NS:P], src[:, :, 0:NS]), ("MT", q))
            for q in range(4):
                plan.drained(vec, ("K", q))
            serial(vec.tensor_tensor(DD[:, :, :], ident[0:GS, 0:GS].unsqueeze(1).to_broadcast([GS, G, GS]),
                                     Dt[:, :].unsqueeze(2).to_broadcast([GS, G, GS]), ALU.mult))
            step(vec.tensor_tensor(Kt[:, :, 0, :], Kt[:, :, 0, :], DD[:, :, :], ALU.add), s5_d_added)
            for q in range(4):
                g = slice(4 * q, 4 * q + 4)
                cos = tabA[:, g, LC + 1:NTAB]
                sin = tabB[:, g, LC + 1:NTAB]
                w, v, h = (rot[:, j, :].rearrange("p (g c) -> p g c", g=4) for j in range(3))
                plan.filled(vec, ("v", q))
                step.frees(vec.tensor_tensor(w, bank("v", q).rearrange("p (g c) -> p g c", g=4), cos, ALU.mult),
                           ("v", q))
                plan.filled(vec, ("vs", q))
                step.frees(vec.tensor_tensor(v, bank("vs", q).rearrange("p (g c) -> p g c", g=4), sin, ALU.mult),
                           ("vs", q))
                step.settle()
                serial(vec.scalar_tensor_tensor(rot[:, 0, :], rot[:, 1, :], sign[:, 1:2], rot[:, 0, :],
                                                ALU.mult, ALU.add))
                for j in range(4):
                    step(vec.tensor_tensor_scan(h[:, j, :], mag8[:, 4 * q + j:4 * q + j + 1].to_broadcast([P, NC5]),
                                                w[:, j, :], 0.0, ALU.mult, ALU.add))
                step.settle()
                last = NC5 - 1
                step(vec.tensor_tensor(HC[:, g, 1:NC5], h[:, :, 0:last], cos[:, :, 0:last], ALU.mult))
                step(vec.scalar_tensor_tensor(HS[:, g, 1:NC5], h[:, :, 0:last], -1.0, sin[:, :, 0:last],
                                              ALU.mult, ALU.mult))
                step(vec.memset(HC[:, g, 0:1], 0.0))
                step(vec.memset(HS[:, g, 0:1], 0.0), s5_states_set)
            for p in range(H // 2):
                for n in range(2):
                    plan.filled(vec, ("kp", p, n))
                    s = slice(n * 512, (n + 1) * 512)
                    step(vec.tensor_copy(kT[0:NOPE, 2 * p, s], bank("kp", p, n)[0:NOPE, :]))
                    step.frees(vec.tensor_copy(kT[0:NOPE, 2 * p + 1, s], bank("kp", p, n)[NOPE:P, :]), ("kp", p, n))
            for m in range(2):
                for n in range(2):
                    plan.filled(vec, ("yT", m, n))
                    dst = YT[:, m, :].rearrange("p (c t) -> p t c", t=LC)[:, 4 * n:4 * n + 4, :]
                    step.frees(vec.tensor_copy(dst, bank("yT", m, n).rearrange("p (t c) -> p t c", t=4)),
                               ("yT", m, n))
            for k, (m, n) in enumerate((m, n) for m in range(2) for n in range(2)):
                plan.drained(vec, ("glu", m, n))
                s = slice(n * 512, (n + 1) * 512)
                serial(vec.tensor_tensor(SGL[:, k % 2, :], SGL[:, k % 2, :], YT[:, m, s], ALU.mult))
                step(vec.tensor_tensor(gs5[:, m, s], gs5[:, m, s], SGL[:, k % 2, :], ALU.mult), s5_out_set)
            for what, n in attention_steps():
                if what == "qT":
                    for half in range(2):
                        plan.filled(vec, ("qT", n, half))
                        step.frees(vec.tensor_copy(qTt[:, n % 2, 4 * half:4 * half + 4, :],
                                                   bank("qT", n, half)[0:QK, :].rearrange("p (h t) -> p h t", h=4)),
                                   ("qT", n, half))
                elif what == "s":
                    plan.filled(vec, ("s", n))
                    w = (heads[n][0] + 1) * P
                    scores = psum[:, 2 * (n % 2):2 * (n % 2) + 2, :].rearrange("p a b -> p (a b)")[:, 0:w]
                    step(vec.tensor_reduce(negmax[:, n % 2:n % 2 + 1], scores, AX_X, ALU.max, negate=True), max_set)
                elif what == "pt":
                    number, first, blocks = pt_jobs[heads[n]][0]
                    copy_probs(vec, step, number, first, blocks)
                elif what == "av" and heads[n][1] == H - 1:
                    i = heads[n][0]
                    plan.filled(vec, ("o", i))
                    plan.drained(vec, ("s", n))
                    serial(vec.reciprocal(rinv[:, i % 2, :], rsum[:, i % 2, :]))
                    o3 = rot[:, 0, :].rearrange("p (h d) -> p h d", h=H)
                    step.frees(vec.tensor_tensor(o3, bank("o", i).rearrange("p (h d) -> p h d", h=H),
                                                 rinv[:, i % 2, :].unsqueeze(2).to_broadcast([P, H, VD]), ALU.mult),
                               ("o", i))
                    step.settle()
                    step(vec.tensor_tensor(gate[:, i, :], gate[:, i, :], rot[:, 0, :], ALU.mult), gated)
                elif what == "OT":
                    plan.filled(vec, ("OT", n))
                    step.frees(vec.tensor_copy(OT[:, :, n * P:(n + 1) * P],
                                               bank("OT", n).rearrange("p (k t) -> p k t", k=4)), ("OT", n))
            for i in range(NT + 1):
                if i < NT:
                    vec.wait_ge(xres_loaded[i % 2], 16 * (i // 2 + 1))
                    if i >= 2:
                        vec.wait_ge(x1_stored[i % 2], 16 * (i // 2))
                    layer_norm(zn[:, i % 2, :], x_res[:, i % 2, :], "z0", i, i)
                if i:
                    plan.filled(vec, ("x1T", i - 1, 0))
                    step.frees(vec.tensor_copy(x1T[:, 0:4, (i - 1) * P:i * P],
                                               bank("x1T", i - 1, 0).rearrange("p (k t) -> p k t", k=4)),
                               ("x1T", i - 1, 0))
            step(vec.memset(resets[:, :], 1.0))
            step.settle()
            serial(vec.memset(resets[:, :].rearrange("p (c t) -> p c t", t=GC)[:, :, 0:1], 0.0))
            for m in range(2 * GH + 1):
                if m < 2 * GH:
                    vec.wait_ge(soft_set, m + 1)
                    z = zb[:, m % 2, :]
                    serial(vec.scalar_tensor_tensor(z, z, 0.0, soft[:, :], ALU.min, ALU.subtract))
                    if m >= 2:
                        vec.wait_ge(decay_set, m - 1)
                    step(vec.tensor_tensor_scan(cum[:, m % 2, :], resets[:, :], z, 0.0, ALU.mult, ALU.add), scanned)
                if m:
                    j = m - 1
                    h, n = j // 2, j % 2
                    s = slice(n * 512, (n + 1) * 512)
                    vec.wait_ge(decay_set, m)
                    plan.filled(vec, ("q1", j))
                    step.frees(vec.scalar_tensor_tensor(QD[:, h, s], bank("q1", j), GDK ** -0.5, dec[:, j % 2, 0, :],
                                                        ALU.mult, ALU.mult), ("q1", j))
                    plan.filled(vec, ("k1", j))
                    step.frees(vec.tensor_tensor(KI[:, h, s], bank("k1", j), dec[:, j % 2, 1, :], ALU.mult),
                               ("k1", j))
                    step(vec.tensor_copy(ends[:, h, 8 * n:8 * n + 8],
                                         dec[:, j % 2, 0, :].rearrange("p (c t) -> p c t", t=GC)[:, :, GC - 1]),
                         qk_set)
            for what, i in gla_steps():
                if what == "at":
                    plan.filled(vec, ("at", i))
                    if i == 0:
                        serial(vec.memset(att[:, :, :, :], 0.0))
                    step.frees(vec.copy_predicated(att[:, i % 2, :, :], chunk_tri[:, :, :],
                                                   bank("at", i).rearrange("p (h c) -> p h c", h=GH)), ("at", i))
                elif what == "ks":
                    n = 2 * i[0] + i[1]
                    for hp in range(2):
                        plan.filled(vec, ("ks", *i, hp))
                        for j in range(2):
                            h = 2 * hp + j
                            src = bank("ks", *i, hp)[:, j * GDV:(j + 1) * GDV]
                            if n == 0:
                                ins = vec.tensor_copy(state[:, 0, h, :], src)
                            else:
                                ins = vec.scalar_tensor_tensor(state[:, n % 2, h, :], state[:, (n - 1) % 2, h, :],
                                                               ends[:, h, n - 1:n], src, ALU.mult, ALU.add)
                            if j:
                                step.frees(ins, ("ks", *i, hp))
                            else:
                                step(ins)
                    step.settle()
                elif what == "o":
                    vec.wait_ge(ms_set, i + 1)
                    if i:
                        plan.filled(vec, ("yT1", i - 1, 1))
                    serial(vec.reciprocal(stat[:, 44:48], stat[:, 40:44]))
                    for hp in range(2):
                        for j in range(2):
                            h = 2 * hp + j
                            s = slice(h * GDV, (h + 1) * GDV)
                            ins = vec.scalar_tensor_tensor(Y1[:, s], bank("o1", i, hp)[:, j * GDV:(j + 1) * GDV],
                                                           stat[:, 44 + h:45 + h], SG[:, i, s], ALU.mult, ALU.mult)
                            if j:
                                step.frees(ins, ("o1", i, hp))
                            else:
                                step(ins)
                elif what == "yT1":
                    for half in range(2):
                        plan.filled(vec, ("yT1", i, half))
                        if i and half == 0:
                            plan.filled(vec, ("z1", i - 1, 1))
                        src = bank("yT1", i, half).rearrange("p (a b t) -> p a b t", a=2, b=2)
                        gn = gla_c[:, 4:6].unsqueeze(1).unsqueeze(3).to_broadcast([P, 2, 2, P])
                        dst = Y1T[:, 4 * half:4 * half + 4, :].rearrange("p (a b) t -> p a b t", b=2)
                        step.frees(vec.tensor_tensor(dst, src, gn, ALU.mult), ("yT1", i, half))
                elif what == "z1":
                    vec.wait_ge(x1_back, 16 * (i + 1))
                    if i >= 2:
                        vec.wait_ge(y_stored[i % 2], 16 * (i // 2))
                    layer_norm(zn1[:, i % 2, :], x_res1[:, 0, :], "z1", i, NT + i)

        @block.tensor
        def _(pe):
            def group(job, out, pairs, last=True):
                for k, (lhsT, rhs) in enumerate(pairs):
                    mm = pe.matmul(out, lhsT, rhs, start=(k == 0), stop=(k == len(pairs) - 1))
                if last:
                    mm.then_inc(plan.full(job), 1)

            def turned(job, blocks, identity=ident):
                plan.claim(pe, job)
                for k, (block_in, rows) in enumerate(blocks):
                    cols = block_in.shape[0]
                    mm = pe.transpose(bank(*job)[0:rows, k * P:k * P + cols], block_in, identity[0:cols, 0:cols])
                mm.then_inc(plan.full(job), 1)

            pe.wait_ge(consts_set, 1)
            for i in range(NT + 1):
                if i < NT:
                    pe.wait_ge(x_loaded[i % 2], 16 * (i // 2 + 1))
                    for half in range(2):
                        turned(("xT", i, half), [(x_ring[:, i % 2, k * P:(k + 1) * P], P)
                                                 for k in range(4 * half, 4 * half + 4)])
                if i:
                    j = i - 1
                    if j == 0:
                        pe.wait_ge(wa_loaded, 16)
                    plan.drained(pe, ("xT", j, 0))
                    plan.drained(pe, ("xT", j, 1))
                    plan.claim(pe, ("ina", j))
                    group(("ina", j), bank("ina", j)[:, 0:NA],
                          [(xT[:, k, j * P:(j + 1) * P], w_a[:, k, :]) for k in range(KD)])
            pe.wait_ge(s5_par_set, 1)
            plan.claim(pe, ("par",))
            for j in range(4):
                mm = pe.transpose(bank("par")[:, j * G:(j + 1) * G], par[:, j, :], ident[0:G, 0:G])
            mm.then_inc(plan.full(("par",)), 1)
            pe.wait_ge(bc_loaded, 16 * 9)
            turned(("crow",), [(crow[:, s, r, :], P) for s in range(2) for r in range(2)])
            pe.wait_ge(wu_loaded, 16)
            xs = xT[:, :, :].rearrange("p k (c t) -> p k t c", t=LC)
            for t in range(LC):
                plan.claim(pe, ("inu", t))
                group(("inu", t), bank("inu", t)[:, 0:W5], [(xs[:, k, t, :], w_u[:, k, :]) for k in range(KD)])
            pe.wait_ge(wgs_loaded, 16)
            for m in range(2):
                for n in range(2):
                    plan.claim(pe, ("ings", m, n))
                    group(("ings", m, n), bank("ings", m, n),
                          [(w_gs[:, k, m * P:(m + 1) * P], xT[:, k, n * 512:(n + 1) * 512]) for k in range(KD)])
            for t in range(LC):
                plan.drained(pe, ("inu", t))
            for q in range(4):
                turned(("UT", q), [(U[:, g, :, :].rearrange("p t h -> p (t h)"), P) for g in range(4 * q, 4 * q + 4)])
            pe.wait_ge(wg_loaded, 16)
            for i in range(NT):
                plan.claim(pe, ("ing", i))
                group(("ing", i), bank("ing", i), [(xT[:, k, i * P:(i + 1) * P], w_g[:, k, :]) for k in range(KD)])
                if i == 0:
                    pe.wait_ge(latents_scaled, NT)
                    pe.wait_ge(keys_turned, 1)
                turned(("cT", i), [(cqkv[:, i, 0:P], P), (cqkv[:, i, P:2 * P], P), (cqkv[:, i, 2 * P:3 * P], P),
                                   (cqkv[:, i, 3 * P:NA], ROPE)])
            pe.wait_ge(s5_m_set, LC)
            for q in range(4):
                turned(("MT", q), [(M[:, g, :, :].rearrange("p t h -> p (t h)"), P) for g in range(4 * q, 4 * q + 4)])
            pe.wait_ge(s5_b_set, 1)
            pe.wait_ge(s5_nx_set, 4)
            for q in range(4):
                plan.claim(pe, ("K", q))
                for j in range(4):
                    g = 4 * q + j
                    group(("K", q), bank("K", q)[0:GS, j * P:(j + 1) * P],
                          [(Bst[:, g, :], NX[:, g, 0:LC, :].rearrange("p t h -> p (t h)"))], last=(j == 3))
            for q in range(4):
                plan.drained(pe, ("UT", q))
                plan.drained(pe, ("MT", q))
                for name, mat in (("v", MT), ("vs", MTs)):
                    plan.claim(pe, (name, q))
                    for j in range(4):
                        g = 4 * q + j
                        group((name, q), bank(name, q)[:, j * P:(j + 1) * P], [(mat[:, g, :], UT[:, g, :])],
                              last=(j == 3))
            pe.wait_ge(mla_w_loaded, 48)
            for i in range(NT):
                plan.drained(pe, ("cT", i))
            for p in range(H // 2):
                for n in range(2):
                    plan.claim(pe, ("kp", p, n))
                    group(("kp", p, n), bank("kp", p, n),
                          [(w_ukv[:, 0, 2 * p:2 * p + 2, :].rearrange("p h d -> p (h d)"), cT[:, 2, n * 512:(n + 1) * 512])])
            for i in range(NT):
                plan.claim(pe, ("vp", i))
                group(("vp", i), bank("vp", i), [(cT[:, 2, i * P:(i + 1) * P], w_ukv[:, 1, :, :].rearrange("p h d -> p (h d)"))])
            pe.wait_ge(s5_tt_set, 16 * LC)
            pe.wait_ge(s5_n2_set, 4)
            for q in range(4):
                pe.wait_ge(s5_states_set, q + 1)
                plan.claim(pe, ("y", q))
                for j in range(4):
                    g = 4 * q + j
                    group(("y", q), bank("y", q)[:, j * P:(j + 1) * P],
                          [(UT[:, g, :], TT[:, g, :]),
                           (HC[:, g, :], NX[:, g, 1:LC + 1, :].rearrange("p t h -> p (t h)")),
                           (HS[:, g, :], N2[:, g, :, :].rearrange("p t h -> p (t h)"))], last=(j == 3))
            for q in range(4):
                plan.drained(pe, ("y", q))
            for m in range(2):
                for n in range(2):
                    turned(("yT", m, n), [(Y5[:, t, 8 * m:8 * m + 8, :].rearrange("p g h -> p (g h)"), P) for t in range(4 * n, 4 * n + 4)])
            pe.wait_ge(glu_w_loaded, 16)
            for m in range(2):
                for n in range(2):
                    plan.drained(pe, ("yT", m, n))
            for m in range(2):
                for n in range(2):
                    plan.claim(pe, ("glu", m, n))
                    group(("glu", m, n), bank("glu", m, n),
                          [(w_glu[:, k, m * P:(m + 1) * P], YT[:, k, n * 512:(n + 1) * 512]) for k in range(2)])
            for p in range(H // 2):
                for n in range(2):
                    plan.drained(pe, ("kp", p, n))
            for i in range(NT):
                plan.drained(pe, ("vp", i))
            pe.wait_ge(kpe_spread, 16 * H)
            for what, n in attention_steps():
                if what == "q":
                    for half in range(2):
                        plan.claim(pe, ("q", n, half))
                        cols = slice(4 * half * QK, 4 * (half + 1) * QK)
                        group(("q", n, half), bank("q", n, half)[:, 0:4 * QK],
                              [(cT[:, k, n * P:(n + 1) * P], w_uq[:, k, cols]) for k in range(2)])
                elif what == "qT":
                    pe.wait_ge(q_turned, n + 1)
                    for half in range(2):
                        turned(("qT", n, half), [(qt[:, h, :], QK) for h in range(4 * half, 4 * half + 4)])
                elif what == "s":
                    i, h = heads[n]
                    if h == 0:
                        plan.drained(pe, ("qT", i, 0))
                        plan.drained(pe, ("qT", i, 1))
                    plan.claim(pe, ("s", n))
                    slot = 2 * (n % 2)
                    w = (i + 1) * P
                    for part in range((w + 511) // 512):
                        c0, c1 = part * 512, min(w, part * 512 + 512)
                        diag = c1 == w
                        mm = pe.matmul(psum[:, slot + part, 0:c1 - c0], qTt[:, i % 2, h, :], kT[:, h, c0:c1],
                                       start=True, stop=not diag, skip_group_check=diag)
                        if diag:
                            mm = pe.matmul(psum[:, slot + part, c1 - c0 - P:c1 - c0], ident_b[:, :],
                                           causal_bias[:, :], start=False, stop=True, skip_group_check=True)
                    mm.then_inc(plan.full(("s", n)), 1)
                elif what == "pt":
                    plan.drained(pe, ("s", n))
                    for number, first, blocks in pt_jobs[heads[n]]:
                        turned(("pt", number), [(prob[:, n % 2, (first + b) * P:(first + b + 1) * P], P)
                                                for b in range(blocks)])
                elif what == "av":
                    i, h = heads[n]
                    if h == 0:
                        plan.claim(pe, ("o", i))
                    pairs = []
                    for number, first, blocks in pt_jobs[i, h]:
                        plan.drained(pe, ("pt", number))
                        pairs += [(probT[:, number % 2, b * P:(b + 1) * P], V[:, first + b, h, :])
                                  for b in range(blocks)]
                    for k, (lhsT, rhs) in enumerate(pairs):
                        mm = pe.matmul(bank("o", i)[:, h * VD:(h + 1) * VD], lhsT, rhs, start=(k == 0),
                                       stop=(k == len(pairs) - 1))
                    mm.then_inc(plan.full(("o", i)) if h == H - 1 else pv_done, 1)
                elif what == "OT":
                    pe.wait_ge(gated, n + 1)
                    turned(("OT", n), [(gate[:, n, k * P:(k + 1) * P], P) for k in range(4)])
            pe.wait_ge(w_out0_loaded, 16)
            pe.wait_ge(s5_out_set, 4)
            for i in range(NT + 1):
                if i < NT:
                    plan.drained(pe, ("OT", i))
                    for n in range(2):
                        plan.claim(pe, ("z0", i, n))
                        ts, cs = slice(i * P, (i + 1) * P), slice(n * 512, (n + 1) * 512)
                        group(("z0", i, n), bank("z0", i, n),
                              [(OT[:, k, ts] if k < 4 else gs5[:, k - 4, ts], w_out0[:, k, cs]) for k in range(6)])
                if i:
                    pe.wait_ge(x1_set, i)
                    for half in range(2):
                        turned(("x1T", i - 1, half), [(zn[:, (i - 1) % 2, k * P:(k + 1) * P], P)
                                                      for k in range(4 * half, 4 * half + 4)])
            for i in range(NT):
                for half in range(2):
                    plan.drained(pe, ("x1T", i, half))
            pe.wait_ge(wgk_loaded, 16)
            for n in range(2):
                plan.claim(pe, ("gk", n))
                group(("gk", n), bank("gk", n)[0:GR, :],
                      [(w_gk[:, k, :], x1T[:, k, n * 512:(n + 1) * 512]) for k in range(KD)])
            pe.wait_ge(small_loaded, 16 * 7)

            def gate_z(m):
                h, n = m // 2, m % 2
                plan.drained(pe, ("gk", n))
                plan.claim(pe, ("gate", m))
                group(("gate", m), bank("gate", m), [(gk2[:, h * P:(h + 1) * P], gkT[:, n * 512:(n + 1) * 512])])

            gate_z(0)
            pe.wait_ge(w1_loaded[0], 16)
            pe.wait_ge(w1_loaded[1], 16)
            for m in range(2 * GH):
                h, n = m // 2, m % 2
                if m + 1 < 2 * GH:
                    gate_z(m + 1)
                for slot, name in enumerate(("q1", "k1")):
                    plan.claim(pe, (name, m))
                    group((name, m), bank(name, m),
                          [(w_ring[:, slot, k, h * P:(h + 1) * P], x1T[:, k, n * 512:(n + 1) * 512])
                           for k in range(KD)])
            for which, name in enumerate(("v1", "g1")):
                for c in range(2):
                    pe.wait_ge(w1_loaded[c], 16 * (which + 2))
                    for i in range(NT):
                        plan.claim(pe, (name, c, i))
                        group((name, c, i), bank(name, c, i),
                              [(x1T[:, k, i * P:(i + 1) * P], w_ring[:, c, k, :]) for k in range(KD)])
            for c in range(2):
                for i in range(NT):
                    plan.drained(pe, ("v1", c, i))
            for what, i in gla_steps():
                if what == "kT1":
                    turned(("kT1", i), [(KI[:, h, i * P:(i + 1) * P], P) for h in range(GH)])
                elif what == "at":
                    plan.claim(pe, ("at", i))
                    for h in range(GH):
                        s = slice(i * P, (i + 1) * P)
                        group(("at", i), bank("at", i)[:, h * P:(h + 1) * P], [(KI[:, h, s], QD[:, h, s])],
                              last=(h == GH - 1))
                elif what == "ks":
                    t, c = i
                    if c == 0:
                        plan.drained(pe, ("kT1", t))
                    rows = slice(c * GC, (c + 1) * GC)
                    for hp in range(2):
                        plan.claim(pe, ("ks", *i, hp))
                        for j in range(2):
                            h = 2 * hp + j
                            group(("ks", *i, hp), bank("ks", *i, hp)[:, j * GDV:(j + 1) * GDV],
                                  [(kTok[rows, t % 2, h, :], V1[rows, t, h * GDV:(h + 1) * GDV])], last=(j == 1))
                elif what == "o":
                    plan.drained(pe, ("at", i))
                    plan.drained(pe, ("ks", i, 0, 0))
                    plan.drained(pe, ("ks", i, 0, 1))
                    pe.wait_ge(qd2_set, 2 * i + 1)
                    for hp in range(2):
                        plan.claim(pe, ("o1", i, hp))
                        for j in range(2):
                            h = 2 * hp + j
                            cols = slice(j * GDV, (j + 1) * GDV)
                            mm = pe.matmul(bank("o1", i, hp)[:, cols], att[:, i % 2, h, :],
                                           V1[:, i, h * GDV:(h + 1) * GDV], start=True, stop=False,
                                           skip_group_check=True)
                            for c in range(2):
                                n = 2 * i + c
                                if n:
                                    mm = pe.matmul(psum[c * GC:(c + 1) * GC, plan.bank(("o1", i, hp)), cols],
                                                   QD2[:, h, n * GC:(n + 1) * GC], state[:, (n - 1) % 2, h, :],
                                                   start=False, stop=True, skip_group_check=True)
                        mm.then_inc(plan.full(("o1", i, hp)), 1)
                elif what == "yT1":
                    plan.drained(pe, ("o1", i, 0))
                    plan.drained(pe, ("o1", i, 1))
                    for half in range(2):
                        turned(("yT1", i, half), [(Y1[:, k * P:(k + 1) * P], P) for k in range(4 * half, 4 * half + 4)])
                elif what == "z1":
                    if i == 0:
                        pe.wait_ge(w_out1_loaded, 16)
                    plan.drained(pe, ("yT1", i, 0))
                    plan.drained(pe, ("yT1", i, 1))
                    for n in range(2):
                        plan.claim(pe, ("z1", i, n))
                        group(("z1", i, n), bank("z1", i, n),
                              [(Y1T[:, k, :], w_out1[:, k, n * 512:(n + 1) * 512]) for k in range(KD)])


_OUT = ("out_dram", (1, 1024, 1024))


def kernel(**inputs):
    import concourse.bacc as bacc
    from concourse.bass_utils import run_bass_kernel_spmd

    nc = bacc.Bacc("TRN2", target_bir_lowering=False, num_devices=1)
    arrays, args = {}, {}
    for name, value in inputs.items():
        a = np.ascontiguousarray(value)
        arrays[f"{name}_dram"] = a
        args[name] = nc.dram_tensor(f"{name}_dram", a.shape, mybir.dt.from_np(a.dtype), kind="ExternalInput").ap()
    args["out"] = nc.dram_tensor(_OUT[0], _OUT[1], F32, kind="ExternalOutput").ap()
    hybrid_trunk(nc, **args)
    return run_bass_kernel_spmd(nc, [arrays], core_ids=[0]).results[0][_OUT[0]]
```

```python
import math
from collections import defaultdict
from contextlib import ExitStack

import concourse.bass as bass
from concourse import mybir
import numpy as np

F32 = mybir.dt.float32
BF16 = mybir.dt.bfloat16
F32R = mybir.dt.float32r
I32 = mybir.dt.int32
ALU = mybir.AluOpType
ACT = mybir.ActivationFunctionType
AX_X = mybir.AxisListType.X

P = 128
PI_BELOW = 3.1415925
TO_INT = 1.5 * 2 ** 23
TO_13_BITS = 1.5 * 2 ** 10


def two_pi_parts():
    first = 6.28125
    second = float(np.float32(round((2 * math.pi - first) * 2 ** 19) / 2 ** 19))
    return first, second, float(np.float32(2 * math.pi - first - second))


class PsumPlan:

    def __init__(self, new_sem):
        self.new_sem, self.sems, self.counts = new_sem, {}, defaultdict(int)
        self.last_on, self.jobs = {}, {}

    def give(self, job, *banks):
        if banks not in self.sems:
            name = "_".join(map(str, banks))
            self.sems[banks] = (self.new_sem(f"bank{name}_full"), self.new_sem(f"bank{name}_free"))
        nth = self.counts[banks] = self.counts[banks] + 1
        before = {self.last_on[b] for b in banks if b in self.last_on}
        self.jobs[job] = (banks, nth, before)
        for b in banks:
            self.last_on[b] = job

    def bank(self, job):
        return self.jobs[job][0][0]

    def full(self, job):
        return self.sems[self.jobs[job][0]][0]

    def free(self, job):
        return self.sems[self.jobs[job][0]][1]

    def claim(self, pe, job):
        for old in self.jobs[job][2]:
            pe.wait_ge(self.free(old), self.jobs[old][1])

    def filled(self, engine, job):
        engine.wait_ge(self.full(job), self.jobs[job][1])

    def drained(self, engine, job):
        engine.wait_ge(self.free(job), self.jobs[job][1])


class Steps:

    def __init__(self, engine, own, plan):
        self.engine, self.own, self.plan = engine, own, plan
        self.counts, self.last = defaultdict(int), None

    def __call__(self, ins, signal=None):
        signal = signal or self.own
        ins.then_inc(signal, 1)
        self.counts[signal.name] += 1
        self.last = (signal, self.counts[signal.name])
        self.settle()

    def frees(self, ins, job):
        ins.then_inc(self.plan.free(job), 1)
        self.last = (self.plan.free(job), self.plan.jobs[job][1])
        self.settle()

    def settle(self):
        self.engine.wait_ge(*self.last)


def hybrid_trunk(nc, x, positions, ln_g, ln_b, even_w_in, mla_q_norm, mla_kv_norm, mla_w_uq,
                 mla_w_ukv, s5_a_re, s5_a_im, s5_log_dt, s5_b_re, s5_b_im, s5_c_re, s5_c_im,
                 s5_d, s5_w_glu, s5_b_glu, even_w_out, odd_w_in, gla_w_gk2, gla_b_gk,
                 gla_g_norm, odd_w_out, out):
    S, D = x.shape[1:]
    NT, KD = S // P, D // P
    RQ, RKV = mla_q_norm.shape[1], mla_kv_norm.shape[1]
    H, NOPE, ROPE, VD = 8, 64, 32, 64
    HALF, QK = ROPE // 2, NOPE + ROPE
    G, NS = s5_a_re.shape[1:]
    GS = s5_b_re.shape[3]
    W5 = G * GS
    LC = P // GS
    NC5 = S // LC
    MIX = H * VD + W5
    NA = RQ + RKV + ROPE
    GH, GDK, GDV, GC = 4, 128, 256, 64
    GKW, GW, GR = GH * GDK, GH * GDV, gla_w_gk2.shape[1]
    NCH = S // GC
    ALPHA = float(np.float32(4 ** 0.25))
    SCALE = float(np.float32(QK ** -0.5))
    assert NC5 == P and G * GS == 256 and NT == 8 and RQ == 256 and RKV == P and D == 1024

    w_in0, w_in1 = even_w_in[0], odd_w_in[0]
    c_g0 = NA
    c_u = c_g0 + H * VD
    c_gs = c_u + W5
    c_gk = 2 * GKW + GW
    c_end0 = c_gs + W5

    with ExitStack() as ctx:
        def sem(name):
            return ctx.enter_context(nc.semaphore(name))

        base = (nc.sbuf_base + 31) // 32 * 32

        def at(name, offset, shape, dt=F32):
            return nc.alloc_sbuf_tensor_at(name, shape, dt, offset=base + offset * 4)

        cursor = [0]

        def own(name, shape, dt=F32):
            t = at(name, cursor[0], shape, dt)
            cursor[0] += (int(np.prod(shape[1:])) + 7) // 8 * 8
            return t

        ident = own("ident", [P, P])
        ident_b = own("ident_b", [P, P], BF16)
        causal_bias = own("causal_bias", [P, P], BF16)
        tile_tri = own("tile_tri", [P, GH, P], I32)
        sign = own("sign", [P, 2])
        eps = own("eps", [P, 2])
        norm_w = own("norm_w", [P, 3])
        pos_i = own("pos_i", [P, NT], I32)
        pos_f = own("pos_f", [P, NT])
        inv_freq = own("inv_freq", [P, HALF])
        rope_at = cursor[0]
        rope_t = own("rope_t", [P, 4, NT, HALF])
        stat = own("stat", [P, 64])
        rsum = own("rsum", [P, 2, H])
        rinv = own("rinv", [P, 2, H])
        negmax = own("negmax", [P, 4])
        gla_c = own("gla_c", [P, 8])
        gk2_at = cursor[0]
        gk2 = own("gk2", [GR, GKW])
        o = cursor[0]
        rot = at("rot", o, [P, 3, 512])
        w_glu = at("w_glu", o + 1536, [P, 2, W5])
        ln_gb = at("ln_gb", o, [P, 2, D])
        cursor[0] += 2048

        RA = cursor[0]
        RB = RA + KD * S
        RC = RB + KD * c_end0
        RD = RC + 8192
        xT = at("xT", RA, [P, KD, S])
        kT = at("kT", RA, [QK, H, S])
        w_a = at("w_a", RB, [P, KD, NA])
        w_u = at("w_u", RB + 3328, [P, KD, W5])
        w_gs = at("w_gs", RB + 5376, [P, KD, W5])
        w_g = at("w_g", RB + 7424, [P, KD, H * VD])
        V = at("V", RC, [P, NT, H, VD])
        gate = at("gate", RC + 4096, [P, NT, H * VD])
        D1 = RD
        D2 = D1 + 3328
        D3 = D2 + 3072
        D4 = D3 + 2560
        D5 = D4 + 2048
        D6 = D5 + 768
        D7 = D6 + 2048
        RT = D7 + 2048
        cqkv = at("cqkv", D1, [P, NT, NA])
        prob = at("prob", D1, [P, 2 * S])
        probT = at("probT", RD + 17920, [P, 4, 512])
        cT = at("cT", D2, [P, 3, S])
        squared = at("squared", D2, [P, RQ + RKV])
        w_uq = at("w_uq", D3, [P, 2, H * QK])
        w_ukv = at("w_ukv", D3 + 1536, [P, 2, H, NOPE])
        x_ring = at("x_ring", D4, [P, 2, D])
        Kt = at("Kt", D4, [GS, G, LC, GS])
        kpeT = at("kpeT", D4, [QK, S])
        qTt = at("qTt", D4, [QK, 2, H, P])
        qt = at("qt", D5, [P, H, QK])
        gs5 = at("gs5", D6, [P, 2, S])
        U = at("U", D7, [P, G, LC, GS])
        UT = at("UT", D7, [P, G, NC5])
        Y5 = at("Y5", D1, [P, LC, G, GS])
        NTAB = LC + 1 + NC5
        tabA = at("tabA", RT, [P, G, NTAB])
        tabB = at("tabB", RT + G * NTAB, [P, G, NTAB])
        assert (RT + 2 * G * NTAB) * 4 <= nc.sbuf_usable_end - base, (RT + 2 * G * NTAB) * 4
        o = RC
        names = {}
        for name, shape, dt in (
            ("par", [G, 4, P], F32), ("dts", [G, 16], F32), ("dti", [G, 8], I32), ("parT", [P, 4, G], F32),
            ("sm", [P, 8, G], F32), ("ex", [P, 4, G * (LC + 1)], F32), ("exi", [P, G * (LC + 1)], I32),
            ("times", [P, NTAB], F32), ("BA", [P, G, GS], F32), ("BB", [P, G, GS], F32),
            ("crow", [P, 2, 2, P], F32), ("CA", [P, G, GS], F32),
            ("CB", [P, G, GS], F32), ("Dt", [GS, G], F32), ("DD", [GS, G, GS], F32),
        ):
            names[name] = at(name, o, shape, dt)
            o += (int(np.prod(shape[1:])) + 7) // 8 * 8
        assert o <= RC + 4096, o - RC
        par, dts, dti, parT, sm, ex, exi, times, BA, BB, crow, CA, CB, Dt, DD = names.values()
        NX = at("NX", RB, [P, G, LC + 1, GS])
        N2 = at("N2", RB + 2304, [P, G, LC, GS])
        M = at("M", RB + 4352, [P, G, LC, GS])
        TT = at("TT", RB + 4352, [P, G, P])
        work = at("work", RB + 6400, [P, 640])
        MT = at("MT", RB + 7424, [P, G, P])
        MTs = at("MTs", RB + 9472, [P, G, P])
        HC = at("HC", RB + 7424, [P, G, NC5])
        HS = at("HS", RB + 9472, [P, G, NC5])
        YT = at("YT", RB + 7424, [P, 2, S])
        OT = at("OT", RB + 7424, [P, H * VD // P, S])
        w_out0 = at("w_out0", RB, [P, MIX // P, D])
        SGL = at("SGL", D4, [P, 2, 512])
        Bst = at("Bst", D5, [P, G, GS])
        Bsw = at("Bsw", D5 + 256, [P, G, GS])
        LR = at("LR", RB + 7040, [P, G, LC + 1])
        LI = at("LI", RB + 7184, [P, G, LC + 1])
        mag8 = at("mag8", RB + 7328, [P, G])
        x_res = at("x_res", D1, [P, 2, D])
        zn = at("zn", D1 + 2048, [P, 2, D])
        x1T_hi = at("x1T_hi", RA, [P, KD, S], F32R)
        x1T_lo = at("x1T_lo", RC, [P, KD, S], F32R)
        QD = at("QD", RB, [P, GH, S])
        KI = at("KI", RB + 4096, [P, GH, S])
        dec = at("dec", RB + 8192, [P, 2, 2, 512])
        gkT = at("gkT", RB + 10240, [GR, S])
        V1 = at("V1", RD, [P, NT, GW])
        SG = at("SG", RD + 8192, [P, NT, GW])
        E2 = RD + 16384

        def split_pair(name, offset, shape):
            size = int(np.prod(shape[1:]))
            return (at(name + "_raw", offset, shape), at(name + "_hi", offset + size, shape, F32R),
                    at(name + "_lo", offset, shape, F32R))

        wqk = [split_pair(f"wqk{s}", RD + (4096, 13824)[s], [P, KD, 2, P]) for s in range(2)]
        wv = [split_pair(f"wv{s}", RD + 8192 + 1024 * s, [P, 512]) for s in range(4)]
        wg = [split_pair(f"wg{s}", RB + 8192 + 1024 * s, [P, 512]) for s in range(3)]
        zb = at("zb", RD + 17920, [P, 2, 512])
        soft = at("soft", RD + 18944, [P, 512])
        cum = at("cum", RD + 19456, [P, 2, 512])
        w_gk = split_pair("w_gk", E2 + 4096, [P, KD, GR])
        ends = at("ends", E2 + 4096 + 2 * KD * GR, [P, GH, NCH])
        resets = at("resets", RD + 12288, [P, 512])
        two_ends = at("two_ends", E2 + 4096 + 2 * KD * GR + 64, [P, GH, NT])
        assert (E2 + 4096 + 2 * KD * GR + 96) * 4 <= nc.sbuf_usable_end - base
        w_out1 = (at("w_out1_raw", RC, [P, KD, D]), at("w_out1_hi", RA, [P, KD, D], F32R),
                  at("w_out1_lo", RC, [P, KD, D], F32R))
        state = at("state", RB + 8192, [P, 2, GH, GDV])
        QS = at("QS", RB + 10240, [P, 2, GH, P])
        KS = [at(f"KS{s}", (rope_at, gk2_at)[s], [P, GH, P]) for s in range(2)]
        sq = at("sq", RB + 11264, [P, 256])
        kTok = at("kTok", E2, [P, 2, GH, P])
        att = at("att", E2 + 1024, [P, 2, GH, P])
        Y1T = [[at(f"Y1T{s}_{part}", (E2 + 2048, RB)[s] + 1024 * n, [P, KD, P], F32R)
                for n, part in enumerate(("hi", "lo"))] for s in range(2)]

        vec_step, act_step, pool_step = sem("vec_step"), sem("act_step"), sem("pool_step")
        consts_set = sem("consts_set")
        x_loaded = [sem(f"x_loaded{s}") for s in range(2)]
        wa_loaded, wu_loaded, wgs_loaded, wg_loaded = map(sem, ("wa_loaded", "wu_loaded", "wgs_loaded", "wg_loaded"))
        small_loaded = sem("small_loaded")
        par_loaded, bc_loaded = sem("s5_par_loaded"), sem("s5_bc_loaded")
        mla_w_loaded, glu_w_loaded = sem("mla_w_loaded"), sem("glu_w_loaded")
        squares_done = sem("squares_done")
        latents_scaled = sem("latents_scaled")
        angles_set = sem("angles_set")
        sines_done = sem("sines_done")
        rope_set = sem("rope_set")
        keys_turned = sem("keys_turned")
        kpe_spread = sem("kpe_spread")
        pv_done = sem("pv_done")
        s5_par_set = sem("s5_par_set")
        s5_turns_set = sem("s5_turns_set")
        s5_phase_set = sem("s5_phase_set")
        s5_sin_set = sem("s5_sin_set")
        s5_cos_set = sem("s5_cos_set")
        s5_m_set, s5_b_set, s5_nx_set, s5_n2_set = map(sem, ("s5_m_set", "s5_b_set", "s5_nx_set", "s5_n2_set"))
        s5_d_added, s5_tt_zero, s5_tt_set = sem("s5_d_added"), sem("s5_tt_zero"), sem("s5_tt_set")
        s5_states_set = sem("s5_states_set")
        s5_out_set = sem("s5_out_set")
        q_turned = sem("q_turned")
        max_set, prob_set = sem("max_set"), sem("prob_set")
        gated = sem("gated")
        w_out0_loaded, ln0_loaded = sem("w_out0_loaded"), sem("ln0_loaded")
        xres_loaded = [sem(f"xres_loaded{s}") for s in range(2)]
        var_set, root_set, centred = sem("var_set"), sem("root_set"), sem("centred")
        x1_set = sem("x1_set")
        x1_stored = [sem(f"x1_stored{s}") for s in range(2)]
        x1_hi_set = sem("x1_hi_set")
        wgk_loaded = sem("wgk_loaded")
        wqk_loaded = [sem(f"wqk_loaded{s}") for s in range(2)]
        wgk_split, wqk_split = sem("wgk_split"), sem("wqk_split")
        slices = {"v1": wv, "g1": wg}
        slice_loaded = {name: [sem(f"{name}_slice_loaded{s}") for s in range(len(ring_))]
                        for name, ring_ in slices.items()}
        slice_split = {name: sem(f"{name}_slice_split") for name in slices}
        slice_used = {name: sem(f"{name}_slice_used") for name in slices}
        soft_set, scanned, decay_set = sem("soft_set"), sem("scanned"), sem("decay_set")
        qk_set = sem("qk_set")
        w_out1_loaded, ln1_loaded = [sem(f"w_out1_loaded{q}") for q in range(4)], sem("ln1_loaded")
        w_out1_hi_set, w_out1_split = sem("w_out1_hi_set"), sem("w_out1_split")
        two_ends_set = sem("two_ends_set")
        ks_set, qs_set, ms_set = sem("ks_set"), sem("qs_set"), sem("ms_set")
        yT1_hi_set = sem("yT1_hi_set")
        x1_back = [sem(f"x1_back{s}") for s in range(4)]
        y_set = sem("y_set")
        y_stored = [sem(f"y_stored{s}") for s in range(2)]

        psum = ctx.enter_context(nc.psum_tensor("psum", [P, 8, 512], F32))
        x1_dram = nc.dram_tensor("x1_scratch", [S, D], F32, kind="Internal")
        x1_rows = x1_dram.ap() if not isinstance(x1_dram, bass.AP) else x1_dram

        plan = PsumPlan(sem)
        turn = [0]

        def ring(*job):
            plan.give(job, turn[0] % 8)
            turn[0] += 1

        for i in range(NT):
            ring("xT", i, 0)
            ring("xT", i, 1)
            if i:
                ring("ina", i - 1)
        ring("ina", NT - 1)
        ring("par")
        ring("crow")
        for t in range(LC):
            ring("inu", t)
        for m in range(2):
            for n in range(2):
                ring("ings", m, n)
        for q in range(4):
            ring("UT", q)
        for i in range(NT):
            ring("ing", i)
            ring("cT", i)
        for q in range(4):
            ring("MT", q)
        for q in range(4):
            ring("K", q)
        for q in range(4):
            ring("v", q)
            ring("vs", q)
        for p in range(H // 2):
            for n in range(2):
                ring("kp", p, n)
        for i in range(NT):
            ring("vp", i)
        for q in range(4):
            ring("y", q)
        for m in range(2):
            for n in range(2):
                ring("yT", m, n)
        for m in range(2):
            for n in range(2):
                ring("glu", m, n)

        heads = [(i, h) for i in range(NT) for h in range(H)]
        pt_jobs = {}
        count = 0
        for n, (i, h) in enumerate(heads):
            pt_jobs[i, h] = []
            for g in range(i // 4 + 1):
                pt_jobs[i, h].append((count, 4 * g, min(4, i + 1 - 4 * g)))
                count += 1

        SHORT = [n for n, (i, h) in enumerate(heads) if i < 4]

        def score_banks(n):
            return (n % 4,) if n in SHORT else (2 * (n % 2), 2 * (n % 2) + 1)

        def scores(n):
            i, b0, w = heads[n][0], score_banks(n)[0], (heads[n][0] + 1) * P
            return psum[:, b0:b0 + len(score_banks(n)), :].rearrange("p a b -> p (a b)")[:, 0:w], b0 * 512

        def attention_steps():
            yield "q", 0
            yield "qT", 0
            for n in range(4):
                yield "s", n
            for n, (i, h) in enumerate(heads):
                yield "pt", n
                if h == 0 and i + 1 < NT:
                    yield "q", i + 1
                if h == 3 and i + 1 < NT:
                    yield "qT", i + 1
                if n + 4 in SHORT:
                    yield "s", n + 4
                if n + 2 < len(heads) and n + 2 not in SHORT:
                    yield "s", n + 2
                if n:
                    yield "av", n - 1
                if h == 3 and i:
                    yield "OT", i - 1
            yield "av", len(heads) - 1
            yield "OT", NT - 1

        for what, n in attention_steps():
            if what in ("q", "qT"):
                plan.give((what, n, 0), 6)
                plan.give((what, n, 1), 6)
            elif what == "s":
                plan.give(("s", n), *score_banks(n))
            elif what == "pt":
                for number, _, _ in pt_jobs[heads[n]]:
                    plan.give(("pt", number), 4 + number % 2)
            elif what == "av" and heads[n][1] == 0:
                plan.give(("o", heads[n][0]), 7)
            elif what == "OT":
                plan.give(("OT", n), 6)
        turn[0] = 0
        for i in range(NT):
            ring("z0", i, 0)
            ring("z0", i, 1)
            if i:
                ring("x1T", i - 1, 0)
                ring("x1T", i - 1, 1)
        ring("x1T", NT - 1, 0)
        ring("x1T", NT - 1, 1)
        for n in range(2):
            ring("gk", n)
        ring("gate", 0)
        for m in range(2 * GH):
            if m + 1 < 2 * GH:
                ring("gate", m + 1)
            ring("q1", m)
            ring("k1", m)
        for what in ("v1", "g1"):
            for c in range(2):
                for i in range(NT):
                    ring(what, c, i)

        LAG = 3

        def gla_steps():
            yield "kT1", 0
            yield "at", 0
            for i in range(NT + LAG):
                if i + 1 < NT:
                    yield "kT1", i + 1
                    yield "at", i + 1
                if i < NT:
                    if i >= LAG:
                        yield "z1", i - LAG
                    if i >= LAG - 1:
                        yield "yT1", i - LAG + 1
                    if i + 1 < NT:
                        yield "ks", i
                    yield "o", i
                else:
                    if i - LAG + 1 < NT:
                        yield "yT1", i - LAG + 1
                    yield "z1", i - LAG

        def y1t_slot(i):
            return int(i == NT - LAG + 1)

        def y1t_free(engine, i):
            before = [j for j in range(i) if y1t_slot(j) == y1t_slot(i)]
            if before:
                plan.filled(engine, ("z1", before[-1], 1))

        for what, n in gla_steps():
            if what in ("kT1", "at"):
                ring(what, n)
            else:
                ring({"o": "o1"}.get(what, what), n, 0)
                ring({"o": "o1"}.get(what, what), n, 1)

        def await_slice(engine, name, n):
            c, k = divmod(n, KD)
            if k == KD - 1:
                plan.filled(engine, (name, c, NT - 1))
            else:
                engine.wait_ge(slice_used[name], c * (KD - 1) + k + 1)

        def bank(*job):
            return psum[:, plan.bank(job), :]

        def squares(act, step, i):
            plan.drained(act, ("ina", i))
            step(act.activation(squared[:, 0:RQ], cqkv[:, i, 0:RQ], ACT.Square, accum_out=stat[:, i:i + 1]))
            step(act.activation(squared[:, RQ:RQ + RKV], cqkv[:, i, RQ:RQ + RKV], ACT.Square,
                                accum_out=stat[:, 8 + i:9 + i]))

        def values_done(engine, number):
            n = next(n for n, key in enumerate(heads) if number in [j[0] for j in pt_jobs[key]])
            i, h = heads[n]
            if h == H - 1:
                plan.filled(engine, ("o", i))
            else:
                engine.wait_ge(pv_done, i * (H - 1) + h + 1)

        def copy_probs(engine, step, number, first, blocks):
            plan.filled(engine, ("pt", number))
            if number >= 4:
                values_done(engine, number - 4)
            dst, src = probT[:, number % 4, 0:blocks * P], bank("pt", number)[:, 0:blocks * P]
            ins = engine.activation(dst, src, ACT.Copy) if engine is nc.scalar else engine.tensor_copy(dst, src)
            step.frees(ins, ("pt", number))

        block = ctx.enter_context(nc.Block())

        @block.sync
        def _(sp):
            def rows(w, c0, c1):
                return w.rearrange("(k p) n -> p k n", p=P)[:, :, c0:c1]

            for i in range(NT):
                if i >= 2:
                    plan.filled(sp, ("xT", i - 2, 1))
                sp.dma_start(x_ring[:, i % 2, :], x[0, i * P:(i + 1) * P, :]).then_inc(x_loaded[i % 2], 16)
                if i == 1:
                    sp.dma_start(w_a[:, :, :], rows(w_in0, 0, NA)).then_inc(wa_loaded, 16)
                if i == 3:
                    sp.dma_start(w_u[:, :, :], rows(w_in0, c_u, c_u + W5)).then_inc(wu_loaded, 16)
                if i == 4:
                    sp.dma_start(w_gs[:, :, :], rows(w_in0, c_gs, c_gs + W5)).then_inc(wgs_loaded, 16)
                if i == 5:
                    sp.dma_start(w_g[:, :, :], rows(w_in0, c_g0, c_g0 + H * VD)).then_inc(wg_loaded, 16)
            sp.dma_start(w_uq[:, :, :], mla_w_uq[0].rearrange("(k p) n -> p k n", p=P)).then_inc(mla_w_loaded, 16)
            kv_cols = mla_w_ukv[0].rearrange("p (h s d) -> p s h d", h=H, s=2)
            for s in range(2):
                sp.dma_start(w_ukv[:, s, :, :], kv_cols[:, s, :, :]).then_inc(mla_w_loaded, 16)
            sp.dma_start(w_glu[:, :, :], s5_w_glu[0].rearrange("(k p) n -> p k n", p=P)).then_inc(glu_w_loaded, 16)
            sp.wait_ge(s5_tt_zero, 1)
            sp.wait_ge(s5_d_added, 1)
            for q in range(4):
                plan.drained(sp, ("K", q))
            for s in range(LC):
                sp.dma_start(TT[s * GS:(s + 1) * GS, :, s * GS:P],
                             Kt[:, :, 0:LC - s, :].rearrange("p g t h -> p g (t h)")).then_inc(s5_tt_set, 16)
            for i in range(NT):
                plan.drained(sp, ("cT", i))
            plan.filled(sp, ("ing", NT - 1))
            for h in range(H):
                sp.dma_start(kT[NOPE:QK, h, :], kpeT[NOPE:QK, :]).then_inc(kpe_spread, 16)
            plan.filled(sp, ("y", 3))
            sp.dma_start(w_out0[:, :, :], even_w_out[0].rearrange("(k p) n -> p k n", p=P)).then_inc(w_out0_loaded, 16)
            sp.dma_start(w_gk[0][:, :, :], rows(w_in1, c_gk, c_gk + GR)).then_inc(wgk_loaded, 16)

            def wqk_load(h):
                for n in range(2):
                    sp.dma_start(wqk[h % 2][0][:, :, n, :],
                                 rows(w_in1, n * GKW + h * P, n * GKW + (h + 1) * P)).then_inc(wqk_loaded[h % 2], 16)

            for q in range(4):
                plan.drained(sp, ("v", q))
            sp.wait_ge(s5_states_set, 4)
            plan.filled(sp, ("q", NT - 1, 1))
            wqk_load(0)
            wqk_load(1)
            plan.filled(sp, ("o", NT - 1))
            plan.filled(sp, ("OT", NT - 1))
            sp.wait_ge(s5_out_set, 4)
            for n, w in enumerate((ln_g, ln_b)):
                sp.dma_start(ln_gb[:, n, :], w[0:1, :].partition_broadcast(P)).then_inc(ln0_loaded, 16)
            for i in range(NT):
                if i >= 2:
                    plan.drained(sp, ("z0", i - 2, 1))
                sp.dma_start(x_res[:, i % 2, :], x[0, i * P:(i + 1) * P, :]).then_inc(xres_loaded[i % 2], 16)
                if i >= 2:
                    sp.wait_ge(x1_set, i - 1)
                    sp.dma_start(x1_rows[(i - 2) * P:(i - 1) * P, :], zn[:, i % 2, :]).then_inc(x1_stored[i % 2], 16)
            for i in range(NT - 2, NT):
                sp.wait_ge(x1_set, i + 1)
                sp.dma_start(x1_rows[i * P:(i + 1) * P, :], zn[:, i % 2, :]).then_inc(x1_stored[i % 2], 16)
            for n, w in enumerate((ln_g, ln_b)):
                sp.dma_start(ln_gb[:, n, :], w[1:2, :].partition_broadcast(P)).then_inc(ln1_loaded, 16)

            def slice_load(name, n):
                ring_ = slices[name]
                slot, (c, k) = n % len(ring_), divmod(n, KD)
                if n >= len(ring_):
                    await_slice(sp, name, n - len(ring_))
                c0 = {"v1": 2 * GKW, "g1": c_gk + GR}[name] + c * 512
                sp.dma_start(ring_[slot][0][:, :], w_in1[k * P:(k + 1) * P, c0:c0 + 512]).then_inc(
                    slice_loaded[name][slot], 16)

            plan.filled(sp, ("z0", NT - 1, 1))
            for n in range(4):
                slice_load("v1", n)
            for h in range(2, GH):
                plan.filled(sp, ("k1", 2 * (h - 2) + 1))
                wqk_load(h)
            for n in range(4, 2 * KD):
                if n == 6:
                    plan.filled(sp, ("k1", 2 * GH - 1))
                    sp.wait_ge(qk_set, 2 * GH)
                    for g in range(3):
                        slice_load("g1", g)
                slice_load("v1", n)
            for n in range(3, 2 * KD):
                slice_load("g1", n)
            plan.filled(sp, ("g1", 1, NT - 1))
            for q in range(4):
                sp.dma_start(w_out1[0][:, 2 * q:2 * q + 2, :],
                             odd_w_out[0].rearrange("(k p) n -> p k n", p=P)[:, 2 * q:2 * q + 2, :]).then_inc(
                    w_out1_loaded[q], 16)
            for s in range(2):
                sp.wait_ge(x1_stored[s], 16 * NT // 2)
            for i in range(NT + LAG):
                if i >= LAG:
                    j = i - LAG
                    sp.wait_ge(y_set, j + 1)
                    sp.dma_start(out[0, j * P:(j + 1) * P, :], SG[:, j, :]).then_inc(y_stored[j % 2], 16)
                if i < NT:
                    plan.filled(sp, ("o1", i, 1))
                    sp.dma_start(V1[:, i, :], x1_rows[i * P:(i + 1) * P, :]).then_inc(x1_back[i % 4], 16)
            for s in range(2):
                sp.wait_ge(y_stored[s], 16 * NT // 2)

        @block.gpsimd
        def _(pool):
            step = Steps(pool, pool_step, plan)
            step(pool.memset(ident[:, :], 0.0))
            step(pool.memset(ident_b[:, :], 0.0))
            step(pool.memset(causal_bias[:, :], 0.0))
            step(pool.memset(tile_tri[:, :, :], 1))
            step(pool.memset(sign[:, :], 1.0))
            step(pool.memset(eps[:, 0:1], 1e-5))
            step(pool.memset(eps[:, 1:2], 1e-6))
            for j in range(HALF):
                step(pool.memset(inv_freq[:, j:j + 1],
                                 float(np.float32(10000.0) ** np.float32(-j / HALF))))
            step(pool.iota(times[:, 0:LC + 1], [[1, LC + 1]], base=0, channel_multiplier=0,
                           allow_small_or_imprecise_dtypes=True))
            step(pool.iota(times[:, LC + 1:NTAB], [[LC, NC5]], base=0, channel_multiplier=0,
                           allow_small_or_imprecise_dtypes=True))
            step.settle()
            step(pool.affine_select(out=ident[:, :], in_=ident[:, :], compare_op=ALU.not_equal, fill=1.0,
                                    base=0, pattern=[[-1, P]], channel_multiplier=1))
            step(pool.affine_select(out=ident_b[:, :], in_=ident_b[:, :], compare_op=ALU.not_equal, fill=1.0,
                                    base=0, pattern=[[-1, P]], channel_multiplier=1))
            step(pool.affine_select(out=causal_bias[:, :], in_=causal_bias[:, :], compare_op=ALU.is_ge,
                                    fill=-1e38, base=0, pattern=[[-1, P]], channel_multiplier=1))
            step(pool.affine_select(out=tile_tri[:, :, :], in_=tile_tri[:, :, :], compare_op=ALU.is_ge,
                                    fill=0.0, base=0, pattern=[[0, GH], [1, P]], channel_multiplier=-1))
            step.settle()
            step(pool.memset(sign[0:NS, 0:1], -1.0))
            step(pool.memset(sign[NS:P, 1:2], -1.0))
            step.settle()
            step(pool.memset(stat[:, :], 0.0), consts_set)

            pool.wait_ge(s5_turns_set, 1)
            hi = sm[:, 4, :].unsqueeze(2).to_broadcast([P, G, NTAB])
            lo = sm[:, 5, :].unsqueeze(2).to_broadcast([P, G, NTAB])
            tb = times[:, :].unsqueeze(1).to_broadcast([P, G, NTAB])
            step(pool.tensor_tensor(tabA[:, :, :], hi, tb, ALU.mult))
            step(pool.tensor_tensor(tabB[:, :, :], lo, tb, ALU.mult))
            step.settle()

            def drop_turns(signal=None):
                for g in range(0, G, 8):
                    w = rot[:, :, :].rearrange("p a b -> p (a b)")[:, 0:8 * NTAB].rearrange("p (g t) -> p g t", g=8)
                    part = tabA[:, g:g + 8, :]
                    step(pool.tensor_scalar(w, part, TO_INT, None, ALU.add))
                    step.settle()
                    step(pool.tensor_scalar(w, w, TO_INT, None, ALU.subtract))
                    step.settle()
                    step(pool.tensor_tensor(part, part, w, ALU.subtract), signal if g else None)
                    step.settle()

            drop_turns()
            step(pool.tensor_tensor(tabA[:, :, :], tabA[:, :, :], tabB[:, :, :], ALU.add))
            step.settle()
            drop_turns(s5_phase_set)

            def turn_pairs(x1, x2, cos, sin, t1, t2, t3, t4, last):
                step(pool.tensor_tensor(t1, x1, cos, ALU.mult))
                step(pool.tensor_tensor(t2, x2, sin, ALU.mult))
                step(pool.tensor_tensor(t3, x2, cos, ALU.mult))
                step(pool.tensor_tensor(t4, x1, sin, ALU.mult))
                step.settle()
                step(pool.tensor_tensor(x1, t1, t2, ALU.subtract))
                step(pool.tensor_tensor(x2, t3, t4, ALU.add), last)

            pool.wait_ge(rope_set, 1)
            for i in range(NT):
                plan.drained(pool, ("ina", i))
            temps = [rot[:, 0, 128 * j:128 * (j + 1)].rearrange("p (t r) -> p t r", r=HALF) for j in range(4)]
            k0 = RQ + RKV
            turn_pairs(cqkv[:, :, k0:k0 + HALF], cqkv[:, :, k0 + HALF:k0 + ROPE], rope_t[:, 2, :, :],
                       rope_t[:, 3, :, :], *temps, keys_turned)
            plan.filled(pool, ("MT", 3))
            step(pool.memset(TT[:, :, :], 0.0), s5_tt_zero)
            pool.wait_ge(s5_n2_set, 4)
            temps = [work[:, 128 * j:128 * (j + 1)].rearrange("p (h r) -> p h r", r=HALF) for j in range(4)]
            for i in range(NT):
                plan.drained(pool, ("q", i, 0))
                plan.drained(pool, ("q", i, 1))
                cos = rope_t[:, 2, i, :].unsqueeze(1).to_broadcast([P, H, HALF])
                sin = rope_t[:, 3, i, :].unsqueeze(1).to_broadcast([P, H, HALF])
                turn_pairs(qt[:, :, NOPE:NOPE + HALF], qt[:, :, NOPE + HALF:QK], cos, sin, *temps, q_turned)

            def split(raw, hi, lo, signal):
                step(pool.tensor_copy(hi, raw))
                step(pool.tensor_tensor(lo, raw, hi.bitcast(F32), ALU.subtract), signal)

            def wqk_split_head(h):
                pool.wait_ge(wqk_loaded[h % 2], 32 * (h // 2 + 1))
                for k in range(0, KD, 4):
                    split(*(t[:, k:k + 4, :, :].rearrange("p k n c -> p k (n c)") for t in wqk[h % 2]), wqk_split)

            def slice_split_at(name, n):
                ring_ = slices[name]
                pool.wait_ge(slice_loaded[name][n % len(ring_)], 16 * (n // len(ring_) + 1))
                split(*(t[:, :] for t in ring_[n % len(ring_)]), slice_split[name])

            pool.wait_ge(wgk_loaded, 16)
            split(*(t[:, :, :] for t in w_gk), wgk_split)
            for h in range(2):
                wqk_split_head(h)

            pool.wait_ge(ln0_loaded, 32)
            for i in range(NT):
                pool.wait_ge(centred, i + 1)
                z = zn[:, i % 2, :]
                step(pool.tensor_tensor(z, z, ln_gb[:, 0, :], ALU.mult))
                step(pool.tensor_tensor(z, z, ln_gb[:, 1, :], ALU.add), x1_set)
            for n in range(4):
                slice_split_at("v1", n)
            for h in range(2, GH):
                wqk_split_head(h)
            for name, first in (("v1", 4), ("g1", 0)):
                for n in range(first, 2 * KD):
                    slice_split_at(name, n)

            pool.wait_ge(two_ends_set, 1)
            plan.filled(pool, ("gate", 2 * GH - 1))

            def keys_at_end(i):
                if i >= 2:
                    plan.filled(pool, ("at", i - 2))
                first, second = slice(2 * i * GC, (2 * i + 1) * GC), slice((2 * i + 1) * GC, (2 * i + 2) * GC)
                step(pool.tensor_tensor(KS[i % 2][:, :, 0:GC], KI[:, :, first],
                                        ends[:, :, 2 * i:2 * i + 1].to_broadcast([P, GH, GC]), ALU.mult))
                step(pool.tensor_copy(KS[i % 2][:, :, GC:P], KI[:, :, second]), ks_set)

            keys_at_end(0)
            keys_at_end(1)
            pool.wait_ge(ln1_loaded, 32)
            for i in range(NT + LAG):
                if i + 2 < NT:
                    keys_at_end(i + 2)
                if i == 0:
                    plan.filled(pool, ("g1", 1, NT - 1))
                if 1 <= i < NT:
                    if i >= 3:
                        plan.filled(pool, ("o1", i - 2, 1))
                    for c, decays in enumerate((ends[:, :, 2 * i - 1:2 * i], two_ends[:, :, i:i + 1])):
                        step(pool.tensor_tensor(QS[:, i % 2, :, c * GC:(c + 1) * GC],
                                                QD[:, :, i * P + c * GC:i * P + (c + 1) * GC],
                                                decays.to_broadcast([P, GH, GC]), ALU.mult), qs_set if c else None)
                if i >= LAG:
                    j = i - LAG
                    pool.wait_ge(centred, NT + j + 1)
                    z = SG[:, j, :]
                    step(pool.tensor_tensor(z, z, ln_gb[:, 0, :], ALU.mult))
                    step(pool.tensor_tensor(z, z, ln_gb[:, 1, :], ALU.add), y_set)

        @block.scalar
        def _(act):
            step = Steps(act, act_step, plan)
            act.dma_start(pos_i[:, :], positions[0].rearrange("(t p) -> p t", p=P),
                          allow_slow_non_contiguous=True).then_inc(small_loaded, 16)
            act.dma_start(norm_w[:, 0:2], mla_q_norm[0].rearrange("(k p) -> p k", p=P),
                          allow_slow_non_contiguous=True).then_inc(small_loaded, 16)
            act.dma_start(norm_w[:, 2:3], mla_kv_norm[0].rearrange("(k p) -> p k", p=P),
                          allow_slow_non_contiguous=True).then_inc(small_loaded, 16)
            act.dma_start(gla_c[:, 0:4], gla_b_gk[0].rearrange("(k p) -> p k", p=P),
                          allow_slow_non_contiguous=True).then_inc(small_loaded, 16)
            act.dma_start(gla_c[:, 4:6], gla_g_norm[0].rearrange("(k p) -> p k", p=P),
                          allow_slow_non_contiguous=True).then_inc(small_loaded, 16)
            act.dma_start(gla_c[:, 6:8], s5_b_glu[0].rearrange("(k p) -> p k", p=P),
                          allow_slow_non_contiguous=True).then_inc(small_loaded, 16)
            act.dma_start(gk2[:, :], gla_w_gk2[0]).then_inc(small_loaded, 16)
            act.dma_start(Dt[:, :], s5_d[0].rearrange("(g h) -> h g", g=G),
                          allow_slow_non_contiguous=True).then_inc(bc_loaded, 16)
            for half in range(2):
                s = slice(half * NS, (half + 1) * NS)
                act.dma_start(par[:, 2, s], s5_a_re[0]).then_inc(par_loaded, 16)
                act.dma_start(par[:, 3, s], s5_a_im[0]).then_inc(par_loaded, 16)
            act.dma_start(dts[:, 0:1], s5_log_dt[0].rearrange("(g a) -> g a", a=1),
                          allow_slow_non_contiguous=True).then_inc(par_loaded, 16)
            re_im = (s5_b_re, s5_b_im)
            for half in range(2):
                s = slice(half * NS, (half + 1) * NS)
                act.dma_start(BA[s, :, :], re_im[half][0].rearrange("g p h -> p g h")).then_inc(bc_loaded, 16)
                act.dma_start(BB[s, :, :], re_im[1 - half][0].rearrange("g p h -> p g h")).then_inc(bc_loaded, 16)
            c_re_im = (s5_c_re, s5_c_im)
            for swap in range(2):
                for half in range(2):
                    src = c_re_im[half ^ swap][0].rearrange("(r g) h p -> (g h) r p", r=2)
                    act.dma_start(crow[:, swap, :, half * NS:(half + 1) * NS], src).then_inc(bc_loaded, 16)

            act.wait_ge(consts_set, 1)
            for i in range(NT):
                plan.filled(act, ("xT", i, 1))
                step.frees(act.activation(xT[:, 4:8, i * P:(i + 1) * P],
                                          bank("xT", i, 1).rearrange("p (k t) -> p k t", k=4), ACT.Copy),
                           ("xT", i, 1))
                if i:
                    squares(act, step, i - 1)
            squares(act, step, NT - 1)
            step.settle()
            step(act.activation(stat[:, 16:24], stat[:, 0:8], ACT.Sqrt, bias=eps[:, 1:2], scale=1.0 / RQ))
            step(act.activation(stat[:, 24:32], stat[:, 8:16], ACT.Sqrt, bias=eps[:, 1:2], scale=1.0 / RKV),
                 squares_done)
            for t in range(LC):
                plan.filled(act, ("inu", t))
                step.frees(act.activation(U[:, :, t, :], bank("inu", t)[:, 0:W5].rearrange("p (g h) -> p g h", g=G),
                                          ACT.Copy), ("inu", t))
            act.wait_ge(angles_set, 1)
            step(act.activation(rope_t[:, 3, :, :], rope_t[:, 0, :, :], ACT.Sin))
            step(act.activation(rope_t[:, 2, :, :], rope_t[:, 0, :, :], ACT.Sin, scale=0.5), sines_done)
            for m in range(2):
                for n in range(2):
                    plan.filled(act, ("ings", m, n))
                    step.frees(act.activation(gs5[:, m, n * 512:(n + 1) * 512], bank("ings", m, n), ACT.Silu),
                               ("ings", m, n))
            for i in range(NT):
                plan.filled(act, ("ing", i))
                step.frees(act.activation(gate[:, i, :], bank("ing", i), ACT.Silu), ("ing", i))
                if i == 0:
                    act.wait_ge(s5_phase_set, 1)
                    step(act.activation(tabB[:, :, :], tabA[:, :, :], ACT.Sin, scale=2 * PI_BELOW))
                    step.settle()
                    step(act.activation(tabA[:, :, :], tabA[:, :, :], ACT.Sin, scale=PI_BELOW), s5_sin_set)
            for q in range(4):
                plan.filled(act, ("K", q))
                step.frees(act.activation(Kt[:, 4 * q:4 * q + 4, :, :].rearrange("p g t h -> p (g t h)"),
                                          bank("K", q)[0:GS, :], ACT.Copy), ("K", q))
            act.wait_ge(s5_n2_set, 4)
            act.wait_ge(s5_d_added, 1)
            for i in range(NT):
                plan.filled(act, ("vp", i))
                step.frees(act.activation(V[:, i, :, :], bank("vp", i).rearrange("p (h d) -> p h d", h=H), ACT.Copy),
                           ("vp", i))
            for q in range(4):
                plan.filled(act, ("y", q))
                step.frees(act.activation(Y5[:, :, 4 * q:4 * q + 4, :],
                                          bank("y", q).rearrange("p (g t h) -> p t g h", g=4, t=LC),
                                          ACT.Gelu_apprx_tanh), ("y", q))
            act.wait_ge(small_loaded, 16 * 7)
            act.wait_ge(kpe_spread, 16 * H)
            act.wait_ge(s5_tt_set, 16 * LC)
            for k, (m, n) in enumerate((m, n) for m in range(2) for n in range(2)):
                plan.filled(act, ("glu", m, n))
                if k >= 2:
                    act.wait_ge(s5_out_set, k - 1)
                step.frees(act.activation(SGL[:, k % 2, :], bank("glu", m, n), ACT.Sigmoid, bias=gla_c[:, 6 + m:7 + m]),
                           ("glu", m, n))
            def exponentials(n):
                i, h = heads[n]
                src, place = scores(n)
                act.wait_ge(max_set, n + 1)
                before = n - (4 if n in SHORT else 2)
                if before >= 0:
                    plan.filled(act, ("pt", pt_jobs[heads[before]][-1][0]))
                step.frees(act.activation(prob[:, place:place + (i + 1) * P], src, ACT.Exp, bias=negmax[:, n % 4:n % 4 + 1],
                                          accum_out=rsum[:, i % 2, h:h + 1]), ("s", n))

            for what, n in attention_steps():
                if what == "q":
                    for half in range(2):
                        plan.filled(act, ("q", n, half))
                        step.frees(act.activation(qt[:, 4 * half:4 * half + 4, :],
                                                  bank("q", n, half)[:, 0:4 * QK].rearrange("p (h d) -> p h d", h=4),
                                                  ACT.Copy, scale=SCALE), ("q", n, half))
                elif what == "s" and n == 0:
                    exponentials(0)
                elif what == "pt":
                    if n + 1 < len(heads):
                        exponentials(n + 1)
                    for number, first, blocks in pt_jobs[heads[n]][1:]:
                        copy_probs(act, step, number, first, blocks)
            for i in range(NT + 1):
                if i < NT:
                    act.wait_ge(var_set, i + 1)
                    step(act.activation(stat[:, 20:21], stat[:, 1:2], ACT.Sqrt, bias=eps[:, 0:1]), root_set)
                if i:
                    for half in range(2):
                        plan.filled(act, ("x1T", i - 1, half))
                        step(act.activation(x1T_hi[:, 4 * half:4 * half + 4, (i - 1) * P:i * P],
                                            bank("x1T", i - 1, half).rearrange("p (k t) -> p k t", k=4), ACT.Copy),
                             x1_hi_set)
            for n in range(2):
                plan.filled(act, ("gk", n))
                step.frees(act.activation(gkT[:, n * 512:(n + 1) * 512], bank("gk", n)[0:GR, :], ACT.Copy), ("gk", n))
            for m in range(2 * GH + 1):
                if m < 2 * GH:
                    plan.filled(act, ("gate", m))
                    if m >= 2:
                        act.wait_ge(scanned, m - 1)
                    step.frees(act.activation(zb[:, m % 2, :], bank("gate", m), ACT.Identity,
                                              bias=gla_c[:, m // 2:m // 2 + 1]), ("gate", m))
                    step.settle()
                    if m:
                        act.wait_ge(scanned, m)
                    step(act.activation(soft[:, :], zb[:, m % 2, :], ACT.Abs))
                    step.settle()
                    step(act.activation(soft[:, :], soft[:, :], ACT.Exp, scale=-1.0))
                    step.settle()
                    step(act.activation(soft[:, :], soft[:, :], ACT.Ln, bias=1.0), soft_set)
                if m:
                    act.wait_ge(scanned, m)
                    if m >= 3:
                        act.wait_ge(qk_set, m - 2)
                    s = (m - 1) % 2
                    step(act.activation(dec[:, s, 0, :], cum[:, s, :], ACT.Exp, scale=1.0 / 16))
                    step(act.activation(dec[:, s, 1, :], cum[:, s, :], ACT.Exp, scale=-1.0 / 16), decay_set)
            for s in range(2):
                act.wait_ge(x1_stored[s], 16 * NT // 2)
            for c in range(2):
                for i in range(NT):
                    plan.filled(act, ("v1", c, i))
                    step.frees(act.activation(V1[:, i, c * 512:(c + 1) * 512], bank("v1", c, i), ACT.Copy),
                               ("v1", c, i))
            for c in range(2):
                for i in range(NT):
                    plan.filled(act, ("g1", c, i))
                    step.frees(act.activation(SG[:, i, c * 512:(c + 1) * 512], bank("g1", c, i), ACT.Silu),
                               ("g1", c, i))
            for what, i in gla_steps():
                if what == "kT1":
                    plan.filled(act, ("kT1", i))
                    if i >= 2:
                        plan.filled(act, ("ks", i - 2, 1))
                    step.frees(act.activation(kTok[:, i % 2, :, :], bank("kT1", i).rearrange("p (h d) -> p h d", h=GH),
                                              ACT.Copy), ("kT1", i))
                elif what == "o":
                    for hp in range(2):
                        plan.filled(act, ("o1", i, hp))
                        for j in range(2):
                            step(act.activation(sq[:, :], bank("o1", i, hp)[:, j * GDV:(j + 1) * GDV], ACT.Square,
                                                accum_out=stat[:, 32 + 2 * hp + j:33 + 2 * hp + j]))
                            step.settle()
                    r = 36 + 4 * (i % 2)
                    step(act.activation(stat[:, r:r + 4], stat[:, 32:36], ACT.Sqrt, bias=eps[:, 1:2], scale=1.0 / GDV),
                         ms_set)
                    if i < 2:
                        for k in range(4 * i, 4 * i + 4):
                            act.wait_ge(w_out1_loaded[k // 2], 16)
                            step(act.activation(w_out1[1][:, k, :], w_out1[0][:, k, :], ACT.Copy,
                                                scale=gla_c[:, 4 + k % 2:5 + k % 2]), w_out1_hi_set)
                elif what == "yT1":
                    for half in range(2):
                        plan.filled(act, ("yT1", i, half))
                        if half == 0:
                            y1t_free(act, i)
                        step(act.activation(Y1T[y1t_slot(i)][0][:, 4 * half:4 * half + 4, :],
                                            bank("yT1", i, half).rearrange("p (k t) -> p k t", k=4), ACT.Copy),
                             yT1_hi_set)
                elif what == "z1":
                    act.wait_ge(var_set, NT + i + 1)
                    step(act.activation(stat[:, 20:21], stat[:, 1:2], ACT.Sqrt, bias=eps[:, 0:1]), root_set)

        @block.vector
        def _(vec):
            step = Steps(vec, vec_step, plan)
            C1, C2, C3 = two_pi_parts()
            INV_2PI = float(np.float32(1 / (2 * math.pi)))

            def serial(ins, signal=None):
                step(ins, signal)
                step.settle()

            def reduce_angle(angle, turns, signal=None):
                serial(vec.tensor_scalar(turns, angle, INV_2PI, TO_INT, ALU.mult, ALU.add))
                serial(vec.tensor_scalar(turns, turns, TO_INT, None, ALU.subtract))
                for part in (C1, C2, C3):
                    serial(vec.scalar_tensor_tensor(angle, turns, -part, angle, ALU.mult, ALU.add))
                serial(vec.tensor_scalar(angle, angle, PI_BELOW, -PI_BELOW, ALU.min, ALU.max), signal)

            def exact_exp(y, t, r, k_int):
                serial(vec.tensor_scalar(y, y, 88.8, -88.0, ALU.min, ALU.max))
                serial(vec.tensor_scalar(t, y, float(np.float32(1 / math.log(2))), TO_INT, ALU.mult, ALU.add))
                serial(vec.tensor_scalar(t, t, TO_INT, None, ALU.subtract))
                serial(vec.scalar_tensor_tensor(r, t, -0.693359375, y, ALU.mult, ALU.add))
                serial(vec.scalar_tensor_tensor(r, t, 2.12194440e-4, r, ALU.mult, ALU.add))
                serial(vec.tensor_scalar(y, r, 1.0 / math.factorial(7), None, ALU.mult))
                for k in range(6, 0, -1):
                    serial(vec.scalar_tensor_tensor(y, y, 1.0 / math.factorial(k), r, ALU.add, ALU.mult))
                serial(vec.tensor_scalar(t, t, 127.0, float(2 ** 23), ALU.add, ALU.mult))
                serial(vec.tensor_copy(k_int, t))
                serial(vec.scalar_tensor_tensor(y, y, 1.0, k_int.bitcast(F32), ALU.add, ALU.mult))

            def layer_norm(zt, res, job, i, tile_no):
                for n in range(2):
                    plan.filled(vec, (job, i, n))
                    s = slice(n * 512, (n + 1) * 512)
                    step.frees(vec.scalar_tensor_tensor(zt[:, s], res[:, s], ALPHA, bank(job, i, n),
                                                        ALU.mult, ALU.add), (job, i, n))
                    step.settle()
                    serial(vec.bn_stats(stat[:, 48 + 6 * n:54 + 6 * n], zt[:, s]))
                serial(vec.bn_aggr(stat[:, 0:2], stat[:, 48:60]), var_set)
                vec.wait_ge(root_set, tile_no + 1)
                serial(vec.reciprocal(stat[:, 21:22], stat[:, 20:21]))
                step(vec.tensor_scalar(zt, zt, stat[:, 0:1], stat[:, 21:22], ALU.subtract, ALU.mult), centred)

            vec.wait_ge(consts_set, 1)
            for i in range(NT + 1):
                if i < NT:
                    plan.filled(vec, ("xT", i, 0))
                    step.frees(vec.tensor_copy(xT[:, 0:4, i * P:(i + 1) * P],
                                               bank("xT", i, 0).rearrange("p (k t) -> p k t", k=4)), ("xT", i, 0))
                if i == 1:
                    vec.wait_ge(par_loaded, 16 * 5)
                    exact_exp(dts[:, 0:1], dts[:, 1:2], dts[:, 2:3], dti[:, 0:1])
                    step(vec.tensor_scalar(par[:, 0, :], par[:, 2, :], dts[:, 0:1], None, ALU.mult))
                    step(vec.tensor_scalar(par[:, 1, :], par[:, 3, :], dts[:, 0:1], None, ALU.mult), s5_par_set)
                if i:
                    plan.filled(vec, ("ina", i - 1))
                    step.frees(vec.tensor_copy(cqkv[:, i - 1, :], bank("ina", i - 1)[:, 0:NA]), ("ina", i - 1))
            vec.wait_ge(small_loaded, 16 * 7)
            serial(vec.tensor_copy(pos_f[:, :], pos_i[:, :]))
            serial(vec.tensor_tensor(rope_t[:, 0, :, :], pos_f[:, :].unsqueeze(2).to_broadcast([P, NT, HALF]),
                                     inv_freq[:, :].unsqueeze(1).to_broadcast([P, NT, HALF]), ALU.mult))
            reduce_angle(rope_t[:, 0, :, :], rope_t[:, 1, :, :], angles_set)
            plan.filled(vec, ("par",))
            step.frees(vec.tensor_copy(parT[:, :, :], bank("par")[:, 0:4 * G].rearrange("p (a g) -> p a g", a=4)),
                       ("par",))
            step.settle()
            serial(vec.tensor_copy(sm[:, 0, :], parT[:, 1, :]))
            reduce_angle(sm[:, 0, :], sm[:, 1, :])
            serial(vec.tensor_scalar(sm[:, 0, :], sm[:, 0, :], INV_2PI, None, ALU.mult))
            serial(vec.tensor_scalar(sm[:, 4, :], sm[:, 0, :], TO_13_BITS, None, ALU.add))
            serial(vec.tensor_scalar(sm[:, 4, :], sm[:, 4, :], TO_13_BITS, None, ALU.subtract))
            serial(vec.tensor_tensor(sm[:, 5, :], sm[:, 0, :], sm[:, 4, :], ALU.subtract), s5_turns_set)
            e4 = [ex[:, j, :].rearrange("p (g t) -> p g t", g=G) for j in range(4)]
            serial(vec.tensor_tensor(e4[0], parT[:, 0, :].unsqueeze(2).to_broadcast([P, G, LC + 1]),
                                     times[:, 0:LC + 1].unsqueeze(1).to_broadcast([P, G, LC + 1]), ALU.mult))
            exact_exp(ex[:, 0, :], ex[:, 1, :], ex[:, 2, :], exi[:, :])
            plan.filled(vec, ("crow",))
            cps = bank("crow").rearrange("p (s n) -> p s n", s=2)
            step(vec.tensor_scalar(CA[:, :, :].rearrange("p g h -> p (g h)"), cps[:, 0, :], sign[:, 1:2], None,
                                   ALU.mult))
            step.frees(vec.tensor_copy(CB[:, :, :].rearrange("p g h -> p (g h)"), cps[:, 1, :]), ("crow",))

            vec.wait_ge(squares_done, 1)
            serial(vec.reciprocal(stat[:, 32:48], stat[:, 16:32]))
            for i in range(NT):
                step(vec.tensor_scalar(cqkv[:, i, 0:RQ], cqkv[:, i, 0:RQ], stat[:, 32 + i:33 + i], None, ALU.mult))
                step(vec.tensor_scalar(cqkv[:, i, RQ:RQ + RKV], cqkv[:, i, RQ:RQ + RKV], stat[:, 40 + i:41 + i],
                                       None, ALU.mult), latents_scaled)
            vec.wait_ge(sines_done, 1)
            serial(vec.scalar_tensor_tensor(rope_t[:, 2, :, :], rope_t[:, 2, :, :], -2.0, rope_t[:, 2, :, :],
                                            ALU.mult, ALU.mult))
            serial(vec.tensor_scalar(rope_t[:, 2, :, :], rope_t[:, 2, :, :], 1.0, None, ALU.add), rope_set)
            for q in range(4):
                plan.filled(vec, ("UT", q))
                step.frees(vec.tensor_copy(UT[:, 4 * q:4 * q + 4, :].rearrange("p g c -> p (g c)"), bank("UT", q)),
                           ("UT", q))
            vec.wait_ge(s5_sin_set, 1)
            plan.filled(vec, ("ings", 1, 1))
            serial(vec.scalar_tensor_tensor(tabA[:, :, :], tabA[:, :, :], -2.0, tabA[:, :, :], ALU.mult, ALU.mult))
            powers = slice(0, LC + 1)
            step(vec.tensor_tensor(LR[:, :, :], e4[0], tabA[:, :, powers], ALU.mult))
            step(vec.tensor_tensor(LI[:, :, :], e4[0], tabB[:, :, powers], ALU.mult))
            step(vec.tensor_copy(mag8[:, :], e4[0][:, :, LC]))
            serial(vec.tensor_scalar(sm[:, 0, :], e4[0][:, :, 1], -1.0, None, ALU.add))
            nr, ni, ar, ai = sm[:, 0, :], LI[:, :, 1], parT[:, 2, :], parT[:, 3, :]
            serial(vec.tensor_tensor(nr, nr, LR[:, :, 1], ALU.add))
            step(vec.tensor_tensor(LR[:, :, :], LR[:, :, :], e4[0], ALU.add))
            step(vec.tensor_scalar(tabA[:, :, :], tabA[:, :, :], 1.0, None, ALU.add))
            den, t1, t2, zr, zi, zs = (sm[:, j, :] for j in (1, 2, 3, 4, 5, 6))
            step(vec.tensor_tensor(t1, ar, ar, ALU.mult))
            step(vec.tensor_tensor(t2, ai, ai, ALU.mult))
            step.settle()
            serial(vec.tensor_tensor(den, t1, t2, ALU.add))
            serial(vec.reciprocal(den, den))
            step(vec.tensor_tensor(t1, nr, ar, ALU.mult))
            step(vec.tensor_tensor(t2, ni, ai, ALU.mult))
            step.settle()
            serial(vec.tensor_tensor(zr, t1, t2, ALU.add))
            step(vec.tensor_tensor(t1, ni, ar, ALU.mult))
            step(vec.tensor_tensor(t2, nr, ai, ALU.mult))
            step.settle()
            serial(vec.tensor_tensor(zi, t1, t2, ALU.subtract))
            step(vec.tensor_tensor(zr, zr, den, ALU.mult))
            serial(vec.tensor_tensor(zi, zi, den, ALU.mult))
            serial(vec.tensor_scalar(zs, zi, sign[:, 0:1], None, ALU.mult))
            vec.wait_ge(bc_loaded, 16 * 9)
            wide = [P, G, GS]
            zr_b, zs_b = zr.unsqueeze(2).to_broadcast(wide), zs.unsqueeze(2).to_broadcast(wide)
            w0 = work[:, 0:G * GS].rearrange("p (g h) -> p g h", g=G)
            w1 = work[:, G * GS:2 * G * GS].rearrange("p (g h) -> p g h", g=G)
            step(vec.tensor_tensor(Bst[:, :, :], BA[:, :, :], zr_b, ALU.mult))
            step(vec.tensor_tensor(w0, BB[:, :, :], zs_b, ALU.mult))
            step(vec.tensor_tensor(Bsw[:, :, :], BB[:, :, :], zr_b, ALU.mult))
            step(vec.tensor_tensor(w1, BA[:, :, :], zs_b, ALU.mult))
            step.settle()
            step(vec.tensor_tensor(Bst[:, :, :], Bst[:, :, :], w0, ALU.add), s5_b_set)
            serial(vec.tensor_tensor(Bsw[:, :, :], Bsw[:, :, :], w1, ALU.subtract))

            def outer(dst, n, a, left, b, right, op, signal):
                for q in range(4):
                    g = slice(4 * q, 4 * q + 4)
                    shape = [P, 4, n, GS]
                    w = work[:, 0:4 * n * GS].rearrange("p (g t h) -> p g t h", g=4, t=n)
                    step(vec.tensor_tensor(dst[:, g, :, :], a[:, g, :].unsqueeze(3).to_broadcast(shape),
                                           left[:, g, :].unsqueeze(2).to_broadcast(shape), ALU.mult))
                    step(vec.tensor_tensor(w, b[:, g, :].unsqueeze(3).to_broadcast(shape),
                                           right[:, g, :].unsqueeze(2).to_broadcast(shape), ALU.mult))
                    step.settle()
                    step(vec.tensor_tensor(dst[:, g, :, :], dst[:, g, :, :], w, op), signal)

            LIs = ex[:, 1, :].rearrange("p (g t) -> p g t", g=G)
            serial(vec.tensor_scalar(LIs, LI[:, :, :], sign[:, 0:1], None, ALU.mult))
            for t in range(LC):
                j = LC - 1 - t
                a = LR[:, :, j].unsqueeze(2).to_broadcast(wide)
                b = LIs[:, :, j].unsqueeze(2).to_broadcast(wide)
                step(vec.tensor_tensor(M[:, :, t, :], Bst[:, :, :], a, ALU.mult))
                step(vec.tensor_tensor(w0 if t % 2 else w1, Bsw[:, :, :], b, ALU.mult))
                step.settle()
                step(vec.tensor_tensor(M[:, :, t, :], M[:, :, t, :], w0 if t % 2 else w1, ALU.add), s5_m_set)
            outer(NX, LC + 1, LR[:, :, :], CA, LI[:, :, :], CB, ALU.subtract, s5_nx_set)
            outer(N2, LC, LR[:, :, 1:LC + 1], CB, LI[:, :, 1:LC + 1], CA, ALU.add, s5_n2_set)
            for i in range(NT):
                plan.filled(vec, ("cT", i))
                s = slice(i * P, (i + 1) * P)
                step(vec.tensor_tensor(cT[:, :, s], bank("cT", i)[:, 0:384].rearrange("p (k t) -> p k t", k=3),
                                       norm_w[:, :].unsqueeze(2).to_broadcast([P, 3, P]), ALU.mult))
                step.frees(vec.tensor_copy(kpeT[NOPE:QK, s], bank("cT", i)[0:ROPE, 384:512]), ("cT", i))
            for q in range(4):
                plan.filled(vec, ("MT", q))
                if q == 0:
                    plan.filled(vec, ("ing", NT - 1))
                g = slice(4 * q, 4 * q + 4)
                src = bank("MT", q).rearrange("p (g s) -> p g s", g=4)
                step(vec.tensor_copy(MT[:, g, :], src))
                step(vec.tensor_copy(MTs[:, g, 0:NS], src[:, :, NS:P]))
                step.frees(vec.tensor_copy(MTs[:, g, NS:P], src[:, :, 0:NS]), ("MT", q))
            for q in range(4):
                plan.drained(vec, ("K", q))
            serial(vec.tensor_tensor(DD[:, :, :], ident[0:GS, 0:GS].unsqueeze(1).to_broadcast([GS, G, GS]),
                                     Dt[:, :].unsqueeze(2).to_broadcast([GS, G, GS]), ALU.mult))
            step(vec.tensor_tensor(Kt[:, :, 0, :], Kt[:, :, 0, :], DD[:, :, :], ALU.add), s5_d_added)
            for q in range(4):
                g = slice(4 * q, 4 * q + 4)
                cos = tabA[:, g, LC + 1:NTAB]
                sin = tabB[:, g, LC + 1:NTAB]
                w, v, h = (rot[:, j, :].rearrange("p (g c) -> p g c", g=4) for j in range(3))
                plan.filled(vec, ("v", q))
                step.frees(vec.tensor_tensor(w, bank("v", q).rearrange("p (g c) -> p g c", g=4), cos, ALU.mult),
                           ("v", q))
                plan.filled(vec, ("vs", q))
                step.frees(vec.tensor_tensor(v, bank("vs", q).rearrange("p (g c) -> p g c", g=4), sin, ALU.mult),
                           ("vs", q))
                step.settle()
                serial(vec.scalar_tensor_tensor(rot[:, 0, :], rot[:, 1, :], sign[:, 1:2], rot[:, 0, :],
                                                ALU.mult, ALU.add))
                for j in range(4):
                    step(vec.tensor_tensor_scan(h[:, j, :], mag8[:, 4 * q + j:4 * q + j + 1].to_broadcast([P, NC5]),
                                                w[:, j, :], 0.0, ALU.mult, ALU.add))
                step.settle()
                last = NC5 - 1
                step(vec.tensor_tensor(HC[:, g, 1:NC5], h[:, :, 0:last], cos[:, :, 0:last], ALU.mult))
                step(vec.scalar_tensor_tensor(HS[:, g, 1:NC5], h[:, :, 0:last], -1.0, sin[:, :, 0:last],
                                              ALU.mult, ALU.mult))
                step(vec.memset(HC[:, g, 0:1], 0.0))
                step(vec.memset(HS[:, g, 0:1], 0.0), s5_states_set)
            for p in range(H // 2):
                for n in range(2):
                    plan.filled(vec, ("kp", p, n))
                    s = slice(n * 512, (n + 1) * 512)
                    step(vec.tensor_copy(kT[0:NOPE, 2 * p, s], bank("kp", p, n)[0:NOPE, :]))
                    step.frees(vec.tensor_copy(kT[0:NOPE, 2 * p + 1, s], bank("kp", p, n)[NOPE:P, :]), ("kp", p, n))
            for m in range(2):
                for n in range(2):
                    plan.filled(vec, ("yT", m, n))
                    dst = YT[:, m, :].rearrange("p (c t) -> p t c", t=LC)[:, 4 * n:4 * n + 4, :]
                    step.frees(vec.tensor_copy(dst, bank("yT", m, n).rearrange("p (t c) -> p t c", t=4)),
                               ("yT", m, n))
            for k, (m, n) in enumerate((m, n) for m in range(2) for n in range(2)):
                plan.drained(vec, ("glu", m, n))
                s = slice(n * 512, (n + 1) * 512)
                serial(vec.tensor_tensor(SGL[:, k % 2, :], SGL[:, k % 2, :], YT[:, m, s], ALU.mult))
                step(vec.tensor_tensor(gs5[:, m, s], gs5[:, m, s], SGL[:, k % 2, :], ALU.mult), s5_out_set)
            for what, n in attention_steps():
                if what == "qT":
                    for half in range(2):
                        plan.filled(vec, ("qT", n, half))
                        step.frees(vec.tensor_copy(qTt[:, n % 2, 4 * half:4 * half + 4, :],
                                                   bank("qT", n, half)[0:QK, :].rearrange("p (h t) -> p h t", h=4)),
                                   ("qT", n, half))
                elif what == "s":
                    plan.filled(vec, ("s", n))
                    step(vec.tensor_reduce(negmax[:, n % 4:n % 4 + 1], scores(n)[0], AX_X, ALU.max, negate=True), max_set)
                elif what == "pt":
                    number, first, blocks = pt_jobs[heads[n]][0]
                    copy_probs(vec, step, number, first, blocks)
                elif what == "av" and heads[n][1] == H - 1:
                    i = heads[n][0]
                    plan.filled(vec, ("o", i))
                    plan.drained(vec, ("s", n))
                    serial(vec.reciprocal(rinv[:, i % 2, :], rsum[:, i % 2, :]))
                    o3 = rot[:, 0, :].rearrange("p (h d) -> p h d", h=H)
                    step.frees(vec.tensor_tensor(o3, bank("o", i).rearrange("p (h d) -> p h d", h=H),
                                                 rinv[:, i % 2, :].unsqueeze(2).to_broadcast([P, H, VD]), ALU.mult),
                               ("o", i))
                    step.settle()
                    step(vec.tensor_tensor(gate[:, i, :], gate[:, i, :], rot[:, 0, :], ALU.mult), gated)
                elif what == "OT":
                    plan.filled(vec, ("OT", n))
                    step.frees(vec.tensor_copy(OT[:, :, n * P:(n + 1) * P],
                                               bank("OT", n).rearrange("p (k t) -> p k t", k=4)), ("OT", n))
            for i in range(NT + 1):
                if i < NT:
                    vec.wait_ge(xres_loaded[i % 2], 16 * (i // 2 + 1))
                    if i >= 2:
                        vec.wait_ge(x1_stored[i % 2], 16 * (i // 2))
                    layer_norm(zn[:, i % 2, :], x_res[:, i % 2, :], "z0", i, i)
                if i:
                    for half in range(2):
                        vec.wait_ge(x1_hi_set, 2 * (i - 1) + half + 1)
                        at_ = (slice(None), slice(4 * half, 4 * half + 4), slice((i - 1) * P, i * P))
                        step.frees(vec.tensor_tensor(x1T_lo[at_], bank("x1T", i - 1, half).rearrange("p (k t) -> p k t", k=4),
                                                     x1T_hi[at_].bitcast(F32), ALU.subtract), ("x1T", i - 1, half))
            step(vec.memset(resets[:, :], 1.0))
            step.settle()
            serial(vec.memset(resets[:, :].rearrange("p (c t) -> p c t", t=GC)[:, :, 0:1], 0.0))
            for m in range(2 * GH + 1):
                if m < 2 * GH:
                    vec.wait_ge(soft_set, m + 1)
                    z = zb[:, m % 2, :]
                    serial(vec.scalar_tensor_tensor(z, z, 0.0, soft[:, :], ALU.min, ALU.subtract))
                    if m >= 2:
                        vec.wait_ge(decay_set, m - 1)
                    step(vec.tensor_tensor_scan(cum[:, m % 2, :], resets[:, :], z, 0.0, ALU.mult, ALU.add), scanned)
                if m:
                    j = m - 1
                    h, n = j // 2, j % 2
                    s = slice(n * 512, (n + 1) * 512)
                    vec.wait_ge(decay_set, m)
                    plan.filled(vec, ("q1", j))
                    step.frees(vec.scalar_tensor_tensor(QD[:, h, s], bank("q1", j), GDK ** -0.5, dec[:, j % 2, 0, :],
                                                        ALU.mult, ALU.mult), ("q1", j))
                    plan.filled(vec, ("k1", j))
                    step.frees(vec.tensor_tensor(KI[:, h, s], bank("k1", j), dec[:, j % 2, 1, :], ALU.mult),
                               ("k1", j))
                    step(vec.tensor_copy(ends[:, h, 8 * n:8 * n + 8],
                                         dec[:, j % 2, 0, :].rearrange("p (c t) -> p c t", t=GC)[:, :, GC - 1]),
                         qk_set)
            step(vec.tensor_tensor(two_ends[:, :, 1:NT], ends[:, :, 1:NCH - 1:2], ends[:, :, 2:NCH:2], ALU.mult),
                 two_ends_set)
            step(vec.memset(att[:, :, :, :], 0.0))
            for what, i in gla_steps():
                if what == "at":
                    plan.filled(vec, ("at", i))
                    if i >= 2:
                        plan.filled(vec, ("o1", i - 2, 1))
                    step.frees(vec.copy_predicated(att[:, i % 2, :, :], tile_tri[:, :, :],
                                                   bank("at", i).rearrange("p (h c) -> p h c", h=GH)), ("at", i))
                elif what == "ks":
                    for hp in range(2):
                        plan.filled(vec, ("ks", i, hp))
                        for j in range(2):
                            h = 2 * hp + j
                            src = bank("ks", i, hp)[:, j * GDV:(j + 1) * GDV]
                            if i == 0:
                                ins = vec.tensor_copy(state[:, 0, h, :], src)
                            else:
                                ins = vec.scalar_tensor_tensor(state[:, i % 2, h, :], state[:, (i - 1) % 2, h, :],
                                                               two_ends[:, h, i:i + 1], src, ALU.mult, ALU.add)
                            if j:
                                step.frees(ins, ("ks", i, hp))
                            else:
                                step(ins)
                    step.settle()
                elif what == "o":
                    vec.wait_ge(ms_set, i + 1)
                    serial(vec.reciprocal(stat[:, 44:48], stat[:, 36 + 4 * (i % 2):40 + 4 * (i % 2)]))
                    for hp in range(2):
                        for j in range(2):
                            h = 2 * hp + j
                            s = slice(h * GDV, (h + 1) * GDV)
                            ins = vec.scalar_tensor_tensor(SG[:, i, s], bank("o1", i, hp)[:, j * GDV:(j + 1) * GDV],
                                                           stat[:, 44 + h:45 + h], SG[:, i, s], ALU.mult, ALU.mult)
                            if j:
                                step.frees(ins, ("o1", i, hp))
                            else:
                                step(ins)
                    if i < 2:
                        for k in range(4 * i, 4 * i + 4):
                            vec.wait_ge(w_out1_hi_set, k + 1)
                            step(vec.scalar_tensor_tensor(w_out1[2][:, k, :], w_out1[0][:, k, :],
                                                          gla_c[:, 4 + k % 2:5 + k % 2],
                                                          w_out1[1][:, k, :].bitcast(F32), ALU.mult, ALU.subtract),
                                 w_out1_split)
                elif what == "yT1":
                    for half in range(2):
                        vec.wait_ge(yT1_hi_set, 2 * i + half + 1)
                        ks = slice(4 * half, 4 * half + 4)
                        hi, lo = Y1T[y1t_slot(i)]
                        step.frees(vec.tensor_tensor(lo[:, ks, :],
                                                     bank("yT1", i, half).rearrange("p (k t) -> p k t", k=4),
                                                     hi[:, ks, :].bitcast(F32), ALU.subtract), ("yT1", i, half))
                elif what == "z1":
                    vec.wait_ge(x1_back[i % 4], 16 * (i // 4 + 1))
                    layer_norm(SG[:, i, :], V1[:, i, :], "z1", i, NT + i)

        @block.tensor
        def _(pe):
            def group(job, out, pairs, last=True):
                for k, (lhsT, rhs) in enumerate(pairs):
                    mm = pe.matmul(out, lhsT, rhs, start=(k == 0), stop=(k == len(pairs) - 1))
                if last:
                    mm.then_inc(plan.full(job), 1)

            def turned(job, blocks, identity=ident):
                plan.claim(pe, job)
                for k, (block_in, rows) in enumerate(blocks):
                    cols = block_in.shape[0]
                    mm = pe.transpose(bank(*job)[0:rows, k * P:k * P + cols], block_in, identity[0:cols, 0:cols])
                mm.then_inc(plan.full(job), 1)

            def split_pairs(pairs):
                return [pair for (a_hi, a_lo), (b_hi, b_lo) in pairs
                        for pair in ((a_hi, b_hi), (a_hi, b_lo), (a_lo, b_hi))]

            pe.wait_ge(consts_set, 1)
            for i in range(NT + 1):
                if i < NT:
                    pe.wait_ge(x_loaded[i % 2], 16 * (i // 2 + 1))
                    for half in range(2):
                        turned(("xT", i, half), [(x_ring[:, i % 2, k * P:(k + 1) * P], P)
                                                 for k in range(4 * half, 4 * half + 4)])
                if i:
                    j = i - 1
                    if j == 0:
                        pe.wait_ge(wa_loaded, 16)
                    plan.drained(pe, ("xT", j, 0))
                    plan.drained(pe, ("xT", j, 1))
                    plan.claim(pe, ("ina", j))
                    group(("ina", j), bank("ina", j)[:, 0:NA],
                          [(xT[:, k, j * P:(j + 1) * P], w_a[:, k, :]) for k in range(KD)])
            pe.wait_ge(s5_par_set, 1)
            plan.claim(pe, ("par",))
            for j in range(4):
                mm = pe.transpose(bank("par")[:, j * G:(j + 1) * G], par[:, j, :], ident[0:G, 0:G])
            mm.then_inc(plan.full(("par",)), 1)
            pe.wait_ge(bc_loaded, 16 * 9)
            turned(("crow",), [(crow[:, s, r, :], P) for s in range(2) for r in range(2)])
            pe.wait_ge(wu_loaded, 16)
            xs = xT[:, :, :].rearrange("p k (c t) -> p k t c", t=LC)
            for t in range(LC):
                plan.claim(pe, ("inu", t))
                group(("inu", t), bank("inu", t)[:, 0:W5], [(xs[:, k, t, :], w_u[:, k, :]) for k in range(KD)])
            pe.wait_ge(wgs_loaded, 16)
            for m in range(2):
                for n in range(2):
                    plan.claim(pe, ("ings", m, n))
                    group(("ings", m, n), bank("ings", m, n),
                          [(w_gs[:, k, m * P:(m + 1) * P], xT[:, k, n * 512:(n + 1) * 512]) for k in range(KD)])
            for t in range(LC):
                plan.drained(pe, ("inu", t))
            for q in range(4):
                turned(("UT", q), [(U[:, g, :, :].rearrange("p t h -> p (t h)"), P) for g in range(4 * q, 4 * q + 4)])
            pe.wait_ge(wg_loaded, 16)
            for i in range(NT):
                plan.claim(pe, ("ing", i))
                group(("ing", i), bank("ing", i), [(xT[:, k, i * P:(i + 1) * P], w_g[:, k, :]) for k in range(KD)])
                if i == 0:
                    pe.wait_ge(latents_scaled, NT)
                    pe.wait_ge(keys_turned, 1)
                turned(("cT", i), [(cqkv[:, i, 0:P], P), (cqkv[:, i, P:2 * P], P), (cqkv[:, i, 2 * P:3 * P], P),
                                   (cqkv[:, i, 3 * P:NA], ROPE)])
            pe.wait_ge(s5_m_set, LC)
            for q in range(4):
                turned(("MT", q), [(M[:, g, :, :].rearrange("p t h -> p (t h)"), P) for g in range(4 * q, 4 * q + 4)])
            pe.wait_ge(s5_b_set, 1)
            pe.wait_ge(s5_nx_set, 4)
            for q in range(4):
                plan.claim(pe, ("K", q))
                for j in range(4):
                    g = 4 * q + j
                    group(("K", q), bank("K", q)[0:GS, j * P:(j + 1) * P],
                          [(Bst[:, g, :], NX[:, g, 0:LC, :].rearrange("p t h -> p (t h)"))], last=(j == 3))
            for q in range(4):
                plan.drained(pe, ("UT", q))
                plan.drained(pe, ("MT", q))
                for name, mat in (("v", MT), ("vs", MTs)):
                    plan.claim(pe, (name, q))
                    for j in range(4):
                        g = 4 * q + j
                        group((name, q), bank(name, q)[:, j * P:(j + 1) * P], [(mat[:, g, :], UT[:, g, :])],
                              last=(j == 3))
            pe.wait_ge(mla_w_loaded, 48)
            for i in range(NT):
                plan.drained(pe, ("cT", i))
            for p in range(H // 2):
                for n in range(2):
                    plan.claim(pe, ("kp", p, n))
                    group(("kp", p, n), bank("kp", p, n),
                          [(w_ukv[:, 0, 2 * p:2 * p + 2, :].rearrange("p h d -> p (h d)"), cT[:, 2, n * 512:(n + 1) * 512])])
            for i in range(NT):
                plan.claim(pe, ("vp", i))
                group(("vp", i), bank("vp", i), [(cT[:, 2, i * P:(i + 1) * P], w_ukv[:, 1, :, :].rearrange("p h d -> p (h d)"))])
            pe.wait_ge(s5_tt_set, 16 * LC)
            pe.wait_ge(s5_n2_set, 4)
            for q in range(4):
                pe.wait_ge(s5_states_set, q + 1)
                plan.claim(pe, ("y", q))
                for j in range(4):
                    g = 4 * q + j
                    group(("y", q), bank("y", q)[:, j * P:(j + 1) * P],
                          [(UT[:, g, :], TT[:, g, :]),
                           (HC[:, g, :], NX[:, g, 1:LC + 1, :].rearrange("p t h -> p (t h)")),
                           (HS[:, g, :], N2[:, g, :, :].rearrange("p t h -> p (t h)"))], last=(j == 3))
            for q in range(4):
                plan.drained(pe, ("y", q))
            for m in range(2):
                for n in range(2):
                    turned(("yT", m, n), [(Y5[:, t, 8 * m:8 * m + 8, :].rearrange("p g h -> p (g h)"), P) for t in range(4 * n, 4 * n + 4)])
            pe.wait_ge(glu_w_loaded, 16)
            for m in range(2):
                for n in range(2):
                    plan.drained(pe, ("yT", m, n))
            for m in range(2):
                for n in range(2):
                    plan.claim(pe, ("glu", m, n))
                    group(("glu", m, n), bank("glu", m, n),
                          [(w_glu[:, k, m * P:(m + 1) * P], YT[:, k, n * 512:(n + 1) * 512]) for k in range(2)])
            for p in range(H // 2):
                for n in range(2):
                    plan.drained(pe, ("kp", p, n))
            for i in range(NT):
                plan.drained(pe, ("vp", i))
            pe.wait_ge(kpe_spread, 16 * H)
            for what, n in attention_steps():
                if what == "q":
                    for half in range(2):
                        plan.claim(pe, ("q", n, half))
                        cols = slice(4 * half * QK, 4 * (half + 1) * QK)
                        group(("q", n, half), bank("q", n, half)[:, 0:4 * QK],
                              [(cT[:, k, n * P:(n + 1) * P], w_uq[:, k, cols]) for k in range(2)])
                elif what == "qT":
                    pe.wait_ge(q_turned, n + 1)
                    for half in range(2):
                        turned(("qT", n, half), [(qt[:, h, :], QK) for h in range(4 * half, 4 * half + 4)])
                elif what == "s":
                    i, h = heads[n]
                    if h == 0:
                        plan.drained(pe, ("qT", i, 0))
                        plan.drained(pe, ("qT", i, 1))
                    plan.claim(pe, ("s", n))
                    slot = score_banks(n)[0]
                    w = (i + 1) * P
                    for part in range((w + 511) // 512):
                        c0, c1 = part * 512, min(w, part * 512 + 512)
                        diag = c1 == w
                        mm = pe.matmul(psum[:, slot + part, 0:c1 - c0], qTt[:, i % 2, h, :], kT[:, h, c0:c1],
                                       start=True, stop=not diag, skip_group_check=diag)
                        if diag:
                            mm = pe.matmul(psum[:, slot + part, c1 - c0 - P:c1 - c0], ident_b[:, :],
                                           causal_bias[:, :], start=False, stop=True, skip_group_check=True)
                    mm.then_inc(plan.full(("s", n)), 1)
                elif what == "pt":
                    plan.drained(pe, ("s", n))
                    for number, first, blocks in pt_jobs[heads[n]]:
                        place = scores(n)[1] + first * P
                        turned(("pt", number), [(prob[:, place + b * P:place + (b + 1) * P], P)
                                                for b in range(blocks)])
                elif what == "av":
                    i, h = heads[n]
                    if h == 0:
                        plan.claim(pe, ("o", i))
                    pairs = []
                    for number, first, blocks in pt_jobs[i, h]:
                        plan.drained(pe, ("pt", number))
                        pairs += [(probT[:, number % 4, b * P:(b + 1) * P], V[:, first + b, h, :])
                                  for b in range(blocks)]
                    for k, (lhsT, rhs) in enumerate(pairs):
                        mm = pe.matmul(bank("o", i)[:, h * VD:(h + 1) * VD], lhsT, rhs, start=(k == 0),
                                       stop=(k == len(pairs) - 1))
                    mm.then_inc(plan.full(("o", i)) if h == H - 1 else pv_done, 1)
                elif what == "OT":
                    pe.wait_ge(gated, n + 1)
                    turned(("OT", n), [(gate[:, n, k * P:(k + 1) * P], P) for k in range(4)])
            pe.wait_ge(w_out0_loaded, 16)
            pe.wait_ge(s5_out_set, 4)
            for i in range(NT + 1):
                if i < NT:
                    plan.drained(pe, ("OT", i))
                    for n in range(2):
                        plan.claim(pe, ("z0", i, n))
                        ts, cs = slice(i * P, (i + 1) * P), slice(n * 512, (n + 1) * 512)
                        group(("z0", i, n), bank("z0", i, n),
                              [(OT[:, k, ts] if k < 4 else gs5[:, k - 4, ts], w_out0[:, k, cs]) for k in range(6)])
                if i:
                    pe.wait_ge(x1_set, i)
                    for half in range(2):
                        turned(("x1T", i - 1, half), [(zn[:, (i - 1) % 2, k * P:(k + 1) * P], P)
                                                      for k in range(4 * half, 4 * half + 4)])
            for i in range(NT):
                for half in range(2):
                    plan.drained(pe, ("x1T", i, half))
            x1T = (x1T_hi, x1T_lo)
            pe.wait_ge(wgk_split, 1)
            for n in range(2):
                plan.claim(pe, ("gk", n))
                group(("gk", n), bank("gk", n)[0:GR, :],
                      split_pairs([([w[:, k, :] for w in w_gk[1:]], [x_[:, k, n * 512:(n + 1) * 512] for x_ in x1T])
                                   for k in range(KD)]))
            pe.wait_ge(small_loaded, 16 * 7)

            def gate_z(m):
                h, n = m // 2, m % 2
                plan.drained(pe, ("gk", n))
                plan.claim(pe, ("gate", m))
                group(("gate", m), bank("gate", m), [(gk2[:, h * P:(h + 1) * P], gkT[:, n * 512:(n + 1) * 512])])

            gate_z(0)
            for m in range(2 * GH):
                h, n = m // 2, m % 2
                if m + 1 < 2 * GH:
                    gate_z(m + 1)
                pe.wait_ge(wqk_split, 2 * (h + 1))
                for side, name in enumerate(("q1", "k1")):
                    plan.claim(pe, (name, m))
                    group((name, m), bank(name, m),
                          split_pairs([([w[:, k, side, :] for w in wqk[h % 2][1:]],
                                        [x_[:, k, n * 512:(n + 1) * 512] for x_ in x1T]) for k in range(KD)]))
            for name, ring_ in slices.items():
                for c in range(2):
                    for k in range(KD):
                        n = c * KD + k
                        pe.wait_ge(slice_split[name], n + 1)
                        w = [w_[:, :] for w_ in ring_[n % len(ring_)][1:]]
                        for i in range(NT):
                            if k == 0:
                                plan.claim(pe, (name, c, i))
                            pairs = split_pairs([([x_[:, k, i * P:(i + 1) * P] for x_ in x1T], w)])
                            for j, (lhsT, rhs) in enumerate(pairs):
                                mm = pe.matmul(bank(name, c, i), lhsT, rhs, start=(k == 0 and j == 0),
                                               stop=(k == KD - 1 and j == len(pairs) - 1))
                            if k == KD - 1:
                                mm.then_inc(plan.full((name, c, i)), 1)
                        if k < KD - 1:
                            mm.then_inc(slice_used[name], 1)
            for c in range(2):
                for i in range(NT):
                    plan.drained(pe, ("v1", c, i))
            for what, i in gla_steps():
                if what == "kT1":
                    pe.wait_ge(ks_set, i + 1)
                    turned(("kT1", i), [(KS[i % 2][:, h, :], P) for h in range(GH)])
                elif what == "at":
                    plan.claim(pe, ("at", i))
                    for h in range(GH):
                        for c, keys in enumerate((KI[:, h, i * P:(i + 1) * P], KS[i % 2][:, h, :])):
                            c0 = c * GC
                            group(("at", i), bank("at", i)[:, h * P + c0:h * P + c0 + GC],
                                  [(keys, QD[:, h, i * P + c0:i * P + c0 + GC])], last=(h == GH - 1 and c == 1))
                elif what == "ks":
                    plan.drained(pe, ("kT1", i))
                    for hp in range(2):
                        plan.claim(pe, ("ks", i, hp))
                        for j in range(2):
                            h = 2 * hp + j
                            group(("ks", i, hp), bank("ks", i, hp)[:, j * GDV:(j + 1) * GDV],
                                  [(kTok[:, i % 2, h, :], V1[:, i, h * GDV:(h + 1) * GDV])], last=(j == 1))
                elif what == "o":
                    plan.drained(pe, ("at", i))
                    if i:
                        plan.drained(pe, ("ks", i - 1, 0))
                        plan.drained(pe, ("ks", i - 1, 1))
                        pe.wait_ge(qs_set, i)
                    for hp in range(2):
                        plan.claim(pe, ("o1", i, hp))
                        for j in range(2):
                            h = 2 * hp + j
                            group(("o1", i, hp), bank("o1", i, hp)[:, j * GDV:(j + 1) * GDV],
                                  [(att[:, i % 2, h, :], V1[:, i, h * GDV:(h + 1) * GDV])]
                                  + ([(QS[:, i % 2, h, :], state[:, (i - 1) % 2, h, :])] if i else []), last=(j == 1))
                elif what == "yT1":
                    plan.drained(pe, ("o1", i, 0))
                    plan.drained(pe, ("o1", i, 1))
                    for half in range(2):
                        turned(("yT1", i, half), [(SG[:, i, k * P:(k + 1) * P], P) for k in range(4 * half, 4 * half + 4)])
                elif what == "z1":
                    if i == 0:
                        pe.wait_ge(w_out1_split, KD)
                    plan.drained(pe, ("yT1", i, 0))
                    plan.drained(pe, ("yT1", i, 1))
                    for n in range(2):
                        plan.claim(pe, ("z1", i, n))
                        group(("z1", i, n), bank("z1", i, n),
                              split_pairs([([y[:, k, :] for y in Y1T[y1t_slot(i)]],
                                            [w[:, k, n * 512:(n + 1) * 512] for w in w_out1[1:]])
                                           for k in range(KD)]))


_OUT = ("out_dram", (1, 1024, 1024))


def kernel(**inputs):
    import concourse.bacc as bacc
    from concourse.bass_utils import run_bass_kernel_spmd

    nc = bacc.Bacc("TRN2", target_bir_lowering=False, num_devices=1)
    arrays, args = {}, {}
    for name, value in inputs.items():
        a = np.ascontiguousarray(value)
        arrays[f"{name}_dram"] = a
        args[name] = nc.dram_tensor(f"{name}_dram", a.shape, mybir.dt.from_np(a.dtype), kind="ExternalInput").ap()
    args["out"] = nc.dram_tensor(_OUT[0], _OUT[1], F32, kind="ExternalOutput").ap()
    hybrid_trunk(nc, **args)
    return run_bass_kernel_spmd(nc, [arrays], core_ids=[0]).results[0][_OUT[0]]
```

```python
import math
from collections import defaultdict
from contextlib import ExitStack

import concourse.bass as bass
from concourse import mybir
import numpy as np

F32 = mybir.dt.float32
BF16 = mybir.dt.bfloat16
F32R = mybir.dt.float32r
I32 = mybir.dt.int32
ALU = mybir.AluOpType
ACT = mybir.ActivationFunctionType
AX_X = mybir.AxisListType.X

P = 128
PI_BELOW = 3.1415925
TO_INT = 1.5 * 2 ** 23
TO_13_BITS = 1.5 * 2 ** 10


def two_pi_parts():
    first = 6.28125
    second = float(np.float32(round((2 * math.pi - first) * 2 ** 19) / 2 ** 19))
    return first, second, float(np.float32(2 * math.pi - first - second))


class PsumPlan:

    def __init__(self, new_sem):
        self.new_sem, self.sems, self.counts = new_sem, {}, defaultdict(int)
        self.last_on, self.jobs = {}, {}

    def give(self, job, *banks):
        if banks not in self.sems:
            name = "_".join(map(str, banks))
            self.sems[banks] = (self.new_sem(f"bank{name}_full"), self.new_sem(f"bank{name}_free"))
        nth = self.counts[banks] = self.counts[banks] + 1
        before = {self.last_on[b] for b in banks if b in self.last_on}
        self.jobs[job] = (banks, nth, before)
        for b in banks:
            self.last_on[b] = job

    def bank(self, job):
        return self.jobs[job][0][0]

    def full(self, job):
        return self.sems[self.jobs[job][0]][0]

    def free(self, job):
        return self.sems[self.jobs[job][0]][1]

    def claim(self, pe, job):
        for old in self.jobs[job][2]:
            pe.wait_ge(self.free(old), self.jobs[old][1])

    def filled(self, engine, job):
        engine.wait_ge(self.full(job), self.jobs[job][1])

    def drained(self, engine, job):
        engine.wait_ge(self.free(job), self.jobs[job][1])


class Steps:

    def __init__(self, engine, own, plan):
        self.engine, self.own, self.plan = engine, own, plan
        self.counts, self.last = defaultdict(int), None

    def __call__(self, ins, signal=None):
        signal = signal or self.own
        ins.then_inc(signal, 1)
        self.counts[signal.name] += 1
        self.last = (signal, self.counts[signal.name])
        self.settle()

    def frees(self, ins, job):
        ins.then_inc(self.plan.free(job), 1)
        self.last = (self.plan.free(job), self.plan.jobs[job][1])
        self.settle()

    def settle(self):
        self.engine.wait_ge(*self.last)


def hybrid_trunk(nc, x, positions, ln_g, ln_b, even_w_in, mla_q_norm, mla_kv_norm, mla_w_uq,
                 mla_w_ukv, s5_a_re, s5_a_im, s5_log_dt, s5_b_re, s5_b_im, s5_c_re, s5_c_im,
                 s5_d, s5_w_glu, s5_b_glu, even_w_out, odd_w_in, gla_w_gk2, gla_b_gk,
                 gla_g_norm, odd_w_out, out):
    S, D = x.shape[1:]
    NT, KD = S // P, D // P
    RQ, RKV = mla_q_norm.shape[1], mla_kv_norm.shape[1]
    H, NOPE, ROPE, VD = 8, 64, 32, 64
    HALF, QK = ROPE // 2, NOPE + ROPE
    G, NS = s5_a_re.shape[1:]
    GS = s5_b_re.shape[3]
    W5 = G * GS
    LC = P // GS
    NC5 = S // LC
    MIX = H * VD + W5
    NA = RQ + RKV + ROPE
    GH, GDK, GDV, GC = 4, 128, 256, 64
    GKW, GW, GR = GH * GDK, GH * GDV, gla_w_gk2.shape[1]
    NCH = S // GC
    ALPHA = float(np.float32(4 ** 0.25))
    SCALE = float(np.float32(QK ** -0.5))
    assert NC5 == P and G * GS == 256 and NT == 8 and RQ == 256 and RKV == P and D == 1024

    w_in0, w_in1 = even_w_in[0], odd_w_in[0]
    c_g0 = NA
    c_u = c_g0 + H * VD
    c_gs = c_u + W5
    c_gk = 2 * GKW + GW
    c_end0 = c_gs + W5

    with ExitStack() as ctx:
        def sem(name):
            return ctx.enter_context(nc.semaphore(name))

        base = (nc.sbuf_base + 31) // 32 * 32

        def at(name, offset, shape, dt=F32):
            return nc.alloc_sbuf_tensor_at(name, shape, dt, offset=base + offset * 4)

        cursor = [0]

        def own(name, shape, dt=F32):
            t = at(name, cursor[0], shape, dt)
            cursor[0] += (int(np.prod(shape[1:])) + 7) // 8 * 8
            return t

        ident = own("ident", [P, P])
        ident_b = own("ident_b", [P, P], BF16)
        causal_bias = own("causal_bias", [P, P], BF16)
        tile_tri = own("tile_tri", [P, GH, P], I32)
        sign = own("sign", [P, 2])
        eps = own("eps", [P, 2])
        norm_w = own("norm_w", [P, 3])
        pos_i = own("pos_i", [P, NT], I32)
        pos_f = own("pos_f", [P, NT])
        inv_freq = own("inv_freq", [P, HALF])
        rope_at = cursor[0]
        rope_t = own("rope_t", [P, 4, NT, HALF])
        stat = own("stat", [P, 64])
        rsum = own("rsum", [P, 2, H])
        rinv = own("rinv", [P, 2, H])
        negmax = own("negmax", [P, 4])
        gla_c = own("gla_c", [P, 8])
        gk2_at = cursor[0]
        gk2 = own("gk2", [GR, GKW])
        o = cursor[0]
        rot = at("rot", o, [P, 3, 512])
        w_glu = at("w_glu", o + 1536, [P, 2, W5])
        ln_gb = at("ln_gb", o, [P, 2, D])
        cursor[0] += 2048

        RA = cursor[0]
        RB = RA + KD * S
        RC = RB + KD * c_end0
        RD = RC + 8192
        def split_pair(name, offset, shape):
            size = int(np.prod(shape[1:]))
            return (at(name + "_raw", offset, shape), at(name + "_hi", offset + size, shape, F32R),
                    at(name + "_lo", offset, shape, F32R))

        xT_hi = at("xT_hi", RA, [P, KD, S], F32R)
        kT = at("kT", RA, [QK, H, S])
        x_ring = at("x_ring", RB, [P, 4, D])
        V = at("V", RC, [P, NT, H, VD])
        gate = at("gate", RC + 4096, [P, NT, H * VD])
        D1 = RD
        D2 = D1 + 3328
        D3 = D2 + 3072
        D4 = D3 + 2560
        D5 = D4 + 2048
        D6 = D5 + 768
        D7 = D6 + 2048
        RT = D7 + 2048
        cqkv = at("cqkv", D1, [P, NT, NA])
        prob = at("prob", D1, [P, 2 * S])
        probT = at("probT", RD + 17920, [P, 4, 512])
        cT = at("cT", D2, [P, 3, S])
        squared = at("squared", RB + 10496, [P, RQ + RKV])
        key_temps = at("key_temps", RB + 10880, [P, 4, NT * HALF])
        w_uq = at("w_uq", D3, [P, 2, H * QK])
        w_ukv = at("w_ukv", D3 + 1536, [P, 2, H, NOPE])
        wg0 = [split_pair(f"wg0_{s}", RB + (4096 + 1024 * s) % 7168, [P, 512]) for s in range(7)]
        wa = [split_pair(f"wa{s}", D3 + 2 * NA * s, [P, NA]) for s in range(3)]
        wug = [split_pair(f"wug{s}", o, [P, 512]) for s, o in enumerate((D6, D6 + 1024, D3, D3 + 1024))]
        xT_lo_parts = [at(f"xT_lo{n}", o, [P, b - a, S], F32R) for n, (a, b, o) in enumerate(
            ((0, 2, RB + 7424), (2, 4, D4), (4, 7, D2), (7, 8, RB + 9472)))]
        xT_lo = [t[:, k, :] for t in xT_lo_parts for k in range(t.shape[1])]
        Kt = at("Kt", D4, [GS, G, LC, GS])
        kpeT = at("kpeT", D4, [QK, S])
        qTt = at("qTt", D4, [QK, 2, H, P])
        qt = at("qt", D5, [P, H, QK])
        gs5 = at("gs5", D6, [P, 2, S])
        U = at("U", D7, [P, G, LC, GS])
        UT = at("UT", D7, [P, G, NC5])
        Y5 = at("Y5", D1, [P, LC, G, GS])
        NTAB = LC + 1 + NC5
        tabA = at("tabA", RT, [P, G, NTAB])
        tabB = at("tabB", RT + G * NTAB, [P, G, NTAB])
        assert (RT + 2 * G * NTAB) * 4 <= nc.sbuf_usable_end - base, (RT + 2 * G * NTAB) * 4
        o = RC
        names = {}
        for name, shape, dt in (
            ("par", [G, 4, P], F32), ("dts", [G, 16], F32), ("dti", [G, 8], I32), ("parT", [P, 4, G], F32),
            ("sm", [P, 8, G], F32), ("ex", [P, 4, G * (LC + 1)], F32), ("exi", [P, G * (LC + 1)], I32),
            ("times", [P, NTAB], F32), ("BA", [P, G, GS], F32), ("BB", [P, G, GS], F32),
            ("crow", [P, 2, 2, P], F32), ("CA", [P, G, GS], F32),
            ("CB", [P, G, GS], F32), ("Dt", [GS, G], F32), ("DD", [GS, G, GS], F32),
        ):
            names[name] = at(name, o, shape, dt)
            o += (int(np.prod(shape[1:])) + 7) // 8 * 8
        assert o <= RC + 4096, o - RC
        par, dts, dti, parT, sm, ex, exi, times, BA, BB, crow, CA, CB, Dt, DD = names.values()
        NX = at("NX", RB, [P, G, LC + 1, GS])
        N2 = at("N2", RB + 2304, [P, G, LC, GS])
        M = at("M", RB + 4352, [P, G, LC, GS])
        TT = at("TT", RB + 4352, [P, G, P])
        work = at("work", RB + 6400, [P, 640])
        turn_work = at("turn_work", RB + 4352, [P, 8 * NTAB])
        MT = at("MT", RB + 7424, [P, G, P])
        YT = at("YT", RB + 7424, [P, 2, S])
        OT = at("OT", RB + 7424, [P, H * VD // P, S])
        w_out0 = at("w_out0", RB, [P, MIX // P, D])
        SGL = at("SGL", D7, [P, 4, 512])
        Bst = at("Bst", D5, [P, G, GS])
        Bsw = at("Bsw", D5 + 256, [P, G, GS])
        LR = at("LR", RB + 7040, [P, G, LC + 1])
        LI = at("LI", RB + 7184, [P, G, LC + 1])
        mag8 = at("mag8", RB + 7328, [P, G])
        x_res = at("x_res", D1, [P, 2, D])
        zn = at("zn", D1 + 2048, [P, 2, D])
        x1T_hi = at("x1T_hi", RA, [P, KD, S], F32R)
        x1T_lo = at("x1T_lo", RC, [P, KD, S], F32R)
        QD = at("QD", RB, [P, GH, S])
        KI = at("KI", RB + 4096, [P, GH, S])
        dec = at("dec", RB + 8192, [P, 2, 2, 512])
        gkT = at("gkT", RB + 10240, [GR, S])
        V1 = at("V1", RD, [P, NT, GW])
        SG = at("SG", RD + 8192, [P, NT, GW])
        E2 = RD + 16384

        wqk = [split_pair(f"wqk{s}", RD + (4096, 13824)[s], [P, KD, 2, P]) for s in range(2)]
        wv = [split_pair(f"wv{s}", RD + 8192 + 1024 * s, [P, 512]) for s in range(4)]
        wg = [split_pair(f"wg{s}", RB + 8192 + 1024 * s, [P, 512]) for s in range(3)]
        zb = at("zb", RD + 17920, [P, 2, 512])
        soft = at("soft", RD + 12800, [P, 2, 512])
        cum = at("cum", RD + 19456, [P, 2, 512])
        w_gk = split_pair("w_gk", E2 + 4096, [P, KD, GR])
        ends = at("ends", E2 + 4096 + 2 * KD * GR, [P, GH, NCH])
        resets = at("resets", RD + 12288, [P, 512])
        two_ends = at("two_ends", E2 + 4096 + 2 * KD * GR + 64, [P, GH, NT])
        assert (E2 + 4096 + 2 * KD * GR + 96) * 4 <= nc.sbuf_usable_end - base
        w_out1 = (at("w_out1_raw", RC, [P, KD, D]), at("w_out1_hi", RA, [P, KD, D], F32R),
                  at("w_out1_lo", RC, [P, KD, D], F32R))
        state = at("state", RB + 8192, [P, 2, GH, GDV])
        QS = at("QS", RB + 10240, [P, 2, GH, P])
        KS = [at(f"KS{s}", (rope_at, gk2_at)[s], [P, GH, P]) for s in range(2)]
        sq = at("sq", RB + 11264, [P, 256])
        kTok = at("kTok", E2, [P, 2, GH, P])
        att = at("att", E2 + 1024, [P, 2, GH, P])
        Y1T = [[at(f"Y1T{s}_{part}", (E2 + 2048, RB)[s] + 1024 * n, [P, KD, P], F32R)
                for n, part in enumerate(("hi", "lo"))] for s in range(2)]

        vec_step, act_step, pool_step = sem("vec_step"), sem("act_step"), sem("pool_step")
        ident_set = sem("ident_set")
        consts_set = sem("consts_set")
        x_loaded = [sem(f"x_loaded{s}") for s in range(4)]
        xT_hi_set = sem("xT_hi_set")
        small_loaded = sem("small_loaded")
        par_loaded, bc_loaded = sem("s5_par_loaded"), sem("s5_bc_loaded")
        mla_w_loaded, glu_w_loaded = sem("mla_w_loaded"), sem("glu_w_loaded")
        squares_done = sem("squares_done")
        latents_scaled = sem("latents_scaled")
        angles_set = sem("angles_set")
        sines_done = sem("sines_done")
        rope_set = sem("rope_set")
        keys_turned = sem("keys_turned")
        kpe_spread = sem("kpe_spread")
        pv_done = sem("pv_done")
        s5_par_set = sem("s5_par_set")
        s5_turns_set = sem("s5_turns_set")
        s5_phase_set = [sem("s5_phase_set_pool"), sem("s5_phase_set_dve")]
        s5_sin_set = sem("s5_sin_set")
        s5_cos_set = sem("s5_cos_set")
        s5_m_set, s5_b_set, s5_nx_set, s5_n2_set = map(sem, ("s5_m_set", "s5_b_set", "s5_nx_set", "s5_n2_set"))
        s5_powers_set = sem("s5_powers_set")
        s5_d_added, s5_tt_zero, s5_tt_set = sem("s5_d_added"), sem("s5_tt_zero"), sem("s5_tt_set")
        s5_scanned = sem("s5_scanned")
        s5_states_set = sem("s5_states_set")
        s5_out_set = sem("s5_out_set")
        bias_turned = sem("bias_turned")
        q_turned = sem("q_turned")
        max_set, prob_set = sem("max_set"), sem("prob_set")
        gated = sem("gated")
        w_out0_loaded, ln0_loaded = sem("w_out0_loaded"), sem("ln0_loaded")
        xres_loaded = [sem(f"xres_loaded{s}") for s in range(2)]
        var_set, root_set, centred = sem("var_set"), sem("root_set"), sem("centred")
        x1_set = sem("x1_set")
        x1_stored = [sem(f"x1_stored{s}") for s in range(2)]
        x1_hi_set = sem("x1_hi_set")
        wgk_loaded = sem("wgk_loaded")
        wqk_loaded = [sem(f"wqk_loaded{s}") for s in range(2)]
        wgk_split, wqk_split = sem("wgk_split"), sem("wqk_split")
        slices = {"gate0": wg0, "ina": wa, "ug": wug, "v1": wv, "g1": wg}
        slice_cols = {"gate0": c_g0, "ina": 0, "ug": c_u, "v1": 2 * GKW, "g1": c_gk + GR}
        slice_hi_set = {name: sem(f"{name}_slice_hi_set") for name in ("gate0", "ina", "ug")}
        slice_loaded = {name: [sem(f"{name}_slice_loaded{s}") for s in range(len(ring_))]
                        for name, ring_ in slices.items()}
        slice_split = {name: sem(f"{name}_slice_split") for name in slices}
        slice_used = {name: sem(f"{name}_slice_used") for name in slices}
        soft_set, scanned, decay_set = sem("soft_set"), sem("scanned"), sem("decay_set")
        qk_set = sem("qk_set")
        w_out1_loaded, ln1_loaded = [sem(f"w_out1_loaded{q}") for q in range(4)], sem("ln1_loaded")
        w_out1_hi_set, w_out1_split = sem("w_out1_hi_set"), sem("w_out1_split")
        two_ends_set = sem("two_ends_set")
        ks_set, qs_set, ms_set = sem("ks_set"), sem("qs_set"), sem("ms_set")
        yT1_hi_set = sem("yT1_hi_set")
        x1_back = [sem(f"x1_back{s}") for s in range(4)]
        y_set, y_last_set = sem("y_set"), sem("y_last_set")
        y_stored = [sem(f"y_stored{s}") for s in range(2)]

        psum = ctx.enter_context(nc.psum_tensor("psum", [P, 8, 512], F32))
        x1_dram = nc.dram_tensor("x1_scratch", [S, D], F32, kind="Internal")
        x1_rows = x1_dram.ap() if not isinstance(x1_dram, bass.AP) else x1_dram

        plan = PsumPlan(sem)
        turn, order = [0], list(range(8))

        def ring(*job):
            plan.give(job, order[turn[0] % 8])
            turn[0] += 1

        EARLY = 3
        X_LAG = 2
        for i in range(NT + X_LAG):
            if i < NT:
                plan.give(("xT", i, 0), 6 if i < NT - 1 else 7)
                plan.give(("xT", i, 1), 7)
            if i >= X_LAG:
                plan.give(("gate0", i - X_LAG), i - X_LAG)
        ring("par")
        ring("crow")
        for i in range(NT):
            ring("ina", i)
        for j in range(4):
            ring("inu", j)
        for m in range(2):
            for n in range(2):
                ring("ings", m, n)

        def middle_steps():
            for q in range(4):
                yield "UT", q
            for i in range(NT):
                yield "cT", i
            for q in range(4):
                yield "MT", q
            for q in range(4):
                yield "K", q
            for q in range(4):
                yield "v", q
            for n in range(NT):
                yield "kp", n
                yield "vp", n
            yield "q", 0
            for q in range(4):
                yield "y", q
            yield "qT", 0
            yield "q", 1
            for n in range(4):
                yield "yT", n
            for n in range(4):
                yield "s", n
            for n in range(4):
                yield "glu", n

        for what, n in middle_steps():
            if what in ("kp", "vp"):
                others = [b for b in range(8) if b not in [plan.bank(("v", q)) for q in range(1, 4)]]
                at_turn = others[(2 * n + (what == "vp")) % len(others)]
                plan.give((what, n // 2, n % 2) if what == "kp" else (what, n), at_turn)
            elif what == "s":
                plan.give(("s", n), n)
            elif what == "glu":
                plan.give((what, n // 2, n % 2), 4 + n)
            elif what in ("q", "qT"):
                ring(what, n, 0)
                ring(what, n, 1)
            elif what == "yT":
                ring(what, n // 2, n % 2)
            else:
                ring(what, n)

        heads = [(i, h) for i in range(NT) for h in range(H)]
        pt_jobs = {}
        count = 0
        for n, (i, h) in enumerate(heads):
            pt_jobs[i, h] = []
            for g in range(i // 4 + 1):
                pt_jobs[i, h].append((count, 4 * g, min(4, i + 1 - 4 * g)))
                count += 1

        SHORT = [n for n, (i, h) in enumerate(heads) if i < 4]

        def score_banks(n):
            return (n % 4,) if n in SHORT else (2 * (n % 2), 2 * (n % 2) + 1)

        def scores(n):
            i, b0, w = heads[n][0], score_banks(n)[0], (heads[n][0] + 1) * P
            return psum[:, b0:b0 + len(score_banks(n)), :].rearrange("p a b -> p (a b)")[:, 0:w], b0 * 512

        def attention_steps():
            for n, (i, h) in enumerate(heads):
                yield "pt", n
                if h < 2 and i + 1 < NT:
                    yield "qT", (i + 1, h)
                if h in (2, 3) and i + 2 < NT:
                    yield "q", (i + 2, h - 2)
                if n + 4 in SHORT:
                    yield "s", n + 4
                if n + 2 < len(heads) and n + 2 not in SHORT:
                    yield "s", n + 2
                if n:
                    yield "av", n - 1
                if h == 4 and i:
                    yield "OT", i - 1
            yield "av", len(heads) - 1
            yield "z0", 0
            yield "OT", NT - 1

        for what, n in attention_steps():
            if what in ("q", "qT"):
                plan.give((what, *n), 6)
            elif what == "s":
                plan.give(("s", n), *score_banks(n))
            elif what == "pt":
                for number, _, _ in pt_jobs[heads[n]]:
                    plan.give(("pt", number), 4 + number % 2)
            elif what == "av" and heads[n][1] == 0:
                plan.give(("o", heads[n][0]), 7)
            elif what == "z0":
                plan.give(("z0", 0, 0), 0)
                plan.give(("z0", 0, 1), 1)
            elif what == "OT":
                plan.give(("OT", n), 6)
        turn[0] = 2
        for i in range(NT):
            if i:
                ring("z0", i, 0)
                ring("z0", i, 1)
            if i:
                ring("x1T", i - 1, 0)
                ring("x1T", i - 1, 1)
        plan.give(("gk", 0), 0)
        plan.give(("q1", 0), 1)
        plan.give(("k1", 0), 2)
        plan.give(("x1T", NT - 1, 0), 3)
        plan.give(("x1T", NT - 1, 1), 4)
        plan.give(("gk", 1), 5)
        for h in range(GH + 1):
            for m in range(2 * h, 2 * h + 2 if h < GH else 0):
                plan.give(("gate", m), 6 + m % 2)
            for m in range(max(1, 2 * h - 1), min(2 * h + 1, 2 * GH)):
                plan.give(("q1", m), (2 * m + 1) % 6)
                plan.give(("k1", m), (2 * m + 2) % 6)
        turn[0], order[:] = 0, [5, 0, 6, 7, 1, 2, 3, 4]
        for what in ("v1", "g1"):
            for c in range(2):
                for i in range(NT):
                    ring(what, c, i)

        LAST = 5 * P
        LAG = 3

        def gla_steps():
            yield "kT1", 0
            yield "at", 0
            for i in range(NT + LAG):
                if i + 1 < NT:
                    yield "kT1", i + 1
                    yield "at", i + 1
                if i < NT:
                    if i >= LAG:
                        yield "z1", i - LAG
                    if i >= LAG - 1:
                        yield "yT1", i - LAG + 1
                    if i + 1 < NT:
                        yield "ks", i
                    yield "o", i
                else:
                    if i - LAG + 1 < NT:
                        yield "yT1", i - LAG + 1
                    yield "z1", i - LAG

        def y1t_slot(i):
            return int(i == NT - LAG + 1)

        def y1t_free(engine, i):
            before = [j for j in range(i) if y1t_slot(j) == y1t_slot(i)]
            if before:
                plan.filled(engine, ("z1", before[-1], 1))

        for what, n in gla_steps():
            if what in ("kT1", "at"):
                ring(what, n)
            else:
                ring({"o": "o1"}.get(what, what), n, 0)
                ring({"o": "o1"}.get(what, what), n, 1)

        def await_slice(engine, name, n):
            c, k = divmod(n, KD)
            if k == KD - 1:
                plan.filled(engine, {"ug": ("ings", 1, 1), "gate0": ("gate0", NT - 1), "ina": ("ina", NT - 1)}.get(
                    name, (name, c, NT - 1)))
            else:
                engine.wait_ge(slice_used[name], c * (KD - 1) + k + 1)

        def bank(*job):
            return psum[:, plan.bank(job), :]

        def squares(act, step, i):
            plan.drained(act, ("ina", i))
            step(act.activation(squared[:, 0:RQ], cqkv[:, i, 0:RQ], ACT.Square, accum_out=stat[:, i:i + 1]))
            step(act.activation(squared[:, RQ:RQ + RKV], cqkv[:, i, RQ:RQ + RKV], ACT.Square,
                                accum_out=stat[:, 8 + i:9 + i]))

        def values_done(engine, number):
            n = next(n for n, key in enumerate(heads) if number in [j[0] for j in pt_jobs[key]])
            i, h = heads[n]
            if h == H - 1:
                plan.filled(engine, ("o", i))
            else:
                engine.wait_ge(pv_done, i * (H - 1) + h + 1)

        def copy_probs(engine, step, number, first, blocks):
            plan.filled(engine, ("pt", number))
            if number >= 4:
                values_done(engine, number - 4)
            dst, src = probT[:, number % 4, 0:blocks * P], bank("pt", number)[:, 0:blocks * P]
            ins = engine.activation(dst, src, ACT.Copy) if engine is nc.scalar else engine.tensor_copy(dst, src)
            step.frees(ins, ("pt", number))

        def turn_pairs(engine, step, x1, x2, cos, sin, t1, t2, t3, t4, last):
            step(engine.tensor_tensor(t1, x1, cos, ALU.mult))
            step(engine.tensor_tensor(t2, x2, sin, ALU.mult))
            step(engine.tensor_tensor(t3, x2, cos, ALU.mult))
            step(engine.tensor_tensor(t4, x1, sin, ALU.mult))
            step(engine.tensor_tensor(x1, t1, t2, ALU.subtract))
            step(engine.tensor_tensor(x2, t3, t4, ALU.add), last)

        def y_turned(engine, step, m, n):
            plan.filled(engine, ("yT", m, n))
            dst = YT[:, m, :].rearrange("p (c t) -> p t c", t=LC)[:, 4 * n:4 * n + 4, :]
            src = bank("yT", m, n).rearrange("p (t c) -> p t c", t=4)
            step.frees(engine.activation(dst, src, ACT.Copy) if engine is nc.scalar else engine.tensor_copy(dst, src),
                       ("yT", m, n))

        def exact_exp(engine, step, y, t, r, k_int):
            step(engine.tensor_scalar(y, y, 88.8, -88.0, ALU.min, ALU.max))
            step(engine.tensor_scalar(t, y, float(np.float32(1 / math.log(2))), TO_INT, ALU.mult, ALU.add))
            step(engine.tensor_scalar(t, t, TO_INT, None, ALU.subtract))
            step(engine.scalar_tensor_tensor(r, t, -0.693359375, y, ALU.mult, ALU.add))
            step(engine.scalar_tensor_tensor(r, t, 2.12194440e-4, r, ALU.mult, ALU.add))
            step(engine.tensor_scalar(y, r, 1.0 / math.factorial(7), None, ALU.mult))
            for k in range(6, 0, -1):
                step(engine.scalar_tensor_tensor(y, y, 1.0 / math.factorial(k), r, ALU.add, ALU.mult))
            step(engine.tensor_scalar(t, t, 127.0, float(2 ** 23), ALU.add, ALU.mult))
            step(engine.tensor_copy(k_int, t))
            step(engine.scalar_tensor_tensor(y, y, 1.0, k_int.bitcast(F32), ALU.add, ALU.mult))

        def phases(engine, step, g0, w, between=None):
            g = slice(g0, g0 + 8)
            shape = [P, 8, NTAB]
            a, b, w = tabA[:, g, :], tabB[:, g, :], w.rearrange("p (g t) -> p g t", g=8)
            steps = times[:, :].unsqueeze(1).to_broadcast(shape)
            step(engine.tensor_tensor(a, sm[:, 4, g].unsqueeze(2).to_broadcast(shape), steps, ALU.mult))
            step(engine.tensor_tensor(b, sm[:, 5, g].unsqueeze(2).to_broadcast(shape), steps, ALU.mult))
            for last in range(2):
                step(engine.tensor_scalar(w, a, TO_INT, None, ALU.add))
                step(engine.tensor_scalar(w, w, TO_INT, None, ALU.subtract))
                step(engine.tensor_tensor(a, a, w, ALU.subtract), s5_phase_set[g0 // 8] if last else None)
                if not last:
                    step(engine.tensor_tensor(a, a, b, ALU.add))
                    if between:
                        between()

        scans = [t.rearrange("p (g c) -> p g c", g=4) for t in (rot[:, 2, :], work[:, 0:512])]

        def chunk_turns(q):
            return tuple(t[:, 4 * q:4 * q + 4, LC + 1:NTAB] for t in (tabA, tabB))

        def matrix_part(engine, step, work_, q, dst, n, a, left, b, right, op, signal):
            g = slice(4 * q, 4 * q + 4)
            shape = [P, 4, n, GS]
            w = work_.rearrange("p (g t h) -> p g t h", g=4, t=n)
            step(engine.tensor_tensor(dst[:, g, :, :], a[:, g, :].unsqueeze(3).to_broadcast(shape),
                                      left[:, g, :].unsqueeze(2).to_broadcast(shape), ALU.mult))
            step(engine.tensor_tensor(w, b[:, g, :].unsqueeze(3).to_broadcast(shape),
                                      right[:, g, :].unsqueeze(2).to_broadcast(shape), ALU.mult))
            step(engine.tensor_tensor(dst[:, g, :, :], dst[:, g, :, :], w, op), signal)

        block = ctx.enter_context(nc.Block())

        @block.sync
        def _(sp):
            def rows(w, c0, c1):
                return w.rearrange("(k p) n -> p k n", p=P)[:, :, c0:c1]

            def parameters():
                for half in range(2):
                    s = slice(half * NS, (half + 1) * NS)
                    sp.dma_start(par[:, 2, s], s5_a_re[0]).then_inc(par_loaded, 16)
                    sp.dma_start(par[:, 3, s], s5_a_im[0]).then_inc(par_loaded, 16)
                sp.dma_start(dts[:, 0:1], s5_log_dt[0].rearrange("(g a) -> g a", a=1),
                              allow_slow_non_contiguous=True).then_inc(par_loaded, 16)

            def matrices():
                re_im = (s5_b_re, s5_b_im)
                for half in range(2):
                    s = slice(half * NS, (half + 1) * NS)
                    sp.dma_start(BA[s, :, :], re_im[half][0].rearrange("g p h -> p g h")).then_inc(bc_loaded, 16)
                    sp.dma_start(BB[s, :, :], re_im[1 - half][0].rearrange("g p h -> p g h")).then_inc(bc_loaded, 16)
                c_re_im = (s5_c_re, s5_c_im)
                for swap in range(2):
                    for half in range(2):
                        src = c_re_im[half ^ swap][0].rearrange("(r g) h p -> (g h) r p", r=2)
                        sp.dma_start(crow[:, swap, :, half * NS:(half + 1) * NS], src).then_inc(bc_loaded, 16)
                sp.dma_start(Dt[:, :], s5_d[0].rearrange("(g h) -> h g", g=G),
                              allow_slow_non_contiguous=True).then_inc(bc_loaded, 16)

            def vectors():
                sp.dma_start(pos_i[:, :], positions[0].rearrange("(t p) -> p t", p=P),
                              allow_slow_non_contiguous=True).then_inc(small_loaded, 16)
                sp.dma_start(norm_w[:, 0:2], mla_q_norm[0].rearrange("(k p) -> p k", p=P),
                              allow_slow_non_contiguous=True).then_inc(small_loaded, 16)
                sp.dma_start(norm_w[:, 2:3], mla_kv_norm[0].rearrange("(k p) -> p k", p=P),
                              allow_slow_non_contiguous=True).then_inc(small_loaded, 16)
                sp.dma_start(gla_c[:, 0:4], gla_b_gk[0].rearrange("(k p) -> p k", p=P),
                              allow_slow_non_contiguous=True).then_inc(small_loaded, 16)
                sp.dma_start(gla_c[:, 4:6], gla_g_norm[0].rearrange("(k p) -> p k", p=P),
                              allow_slow_non_contiguous=True).then_inc(small_loaded, 16)
                sp.dma_start(gla_c[:, 6:8], s5_b_glu[0].rearrange("(k p) -> p k", p=P),
                              allow_slow_non_contiguous=True).then_inc(small_loaded, 16)
                sp.dma_start(gk2[:, :], gla_w_gk2[0]).then_inc(small_loaded, 16)

            def slice_load(name, n):
                ring_ = slices[name]
                slot, (c, k) = n % len(ring_), divmod(n, KD)
                if n >= len(ring_):
                    await_slice(sp, name, n - len(ring_))
                raw = ring_[slot][0]
                c0, w = slice_cols[name] + c * 512, w_in1 if name in ("v1", "g1") else w_in0
                sp.dma_start(raw[:, :], w[k * P:(k + 1) * P, c0:c0 + raw.shape[1]]).then_inc(
                    slice_loaded[name][slot], 16)

            for i in range(NT):
                if i >= 4:
                    plan.filled(sp, ("xT", i - 4, 1))
                sp.dma_start(x_ring[:, i % 4, :], x[0, i * P:(i + 1) * P, :]).then_inc(x_loaded[i % 4], 16)
                if i < EARLY:
                    slice_load("gate0", i)
                if i == 3:
                    parameters()
            for n in range(EARLY, 7):
                plan.filled(sp, ("xT", n + 1, 1))
                slice_load("gate0", n)
            matrices()
            for n in range(3):
                slice_load("ina", n)
            vectors()
            slice_load("gate0", 7)
            for n in range(2):
                slice_load("ug", n)
            for n in range(3, KD):
                slice_load("ina", n)
            await_slice(sp, "ina", KD - 1)
            for n in range(2, KD):
                slice_load("ug", n)
            await_slice(sp, "ug", KD - 1)
            sp.dma_start(w_uq[:, :, :], mla_w_uq[0].rearrange("(k p) n -> p k n", p=P)).then_inc(mla_w_loaded, 16)
            kv_cols = mla_w_ukv[0].rearrange("p (h s d) -> p s h d", h=H, s=2)
            for s in range(2):
                sp.dma_start(w_ukv[:, s, :, :], kv_cols[:, s, :, :]).then_inc(mla_w_loaded, 16)
            sp.dma_start(w_glu[:, :, :], s5_w_glu[0].rearrange("(k p) n -> p k n", p=P)).then_inc(glu_w_loaded, 16)
            sp.wait_ge(s5_tt_zero, 1)
            sp.wait_ge(s5_d_added, 1)
            for q in range(4):
                plan.drained(sp, ("K", q))
            for s in range(LC):
                sp.dma_start(TT[s * GS:(s + 1) * GS, :, s * GS:P],
                             Kt[:, :, 0:LC - s, :].rearrange("p g t h -> p g (t h)")).then_inc(s5_tt_set, 16)
            for i in range(NT):
                plan.drained(sp, ("cT", i))
            plan.filled(sp, ("ings", 1, 1))
            for h in range(H):
                sp.dma_start(kT[NOPE:QK, h, :], kpeT[NOPE:QK, :]).then_inc(kpe_spread, 16)
            plan.filled(sp, ("y", 3))
            sp.dma_start(w_out0[:, :, :], even_w_out[0].rearrange("(k p) n -> p k n", p=P)).then_inc(w_out0_loaded, 16)
            sp.dma_start(w_gk[0][:, :, :], rows(w_in1, c_gk, c_gk + GR)).then_inc(wgk_loaded, 16)

            def wqk_load(h):
                for n in range(2):
                    sp.dma_start(wqk[h % 2][0][:, :, n, :],
                                 rows(w_in1, n * GKW + h * P, n * GKW + (h + 1) * P)).then_inc(wqk_loaded[h % 2], 16)

            for q in range(4):
                plan.drained(sp, ("v", q))
            sp.wait_ge(s5_states_set, 4)
            plan.filled(sp, ("q", NT - 1, 1))
            sp.wait_ge(s5_out_set, 16)
            wqk_load(0)
            wqk_load(1)
            plan.filled(sp, ("pt", pt_jobs[heads[-1]][-1][0]))
            for i in range(NT):
                if i >= 2:
                    plan.drained(sp, ("z0", i - 2, 1))
                sp.dma_start(x_res[:, i % 2, :], x[0, i * P:(i + 1) * P, :]).then_inc(xres_loaded[i % 2], 16)
                if i == 1:
                    sp.wait_ge(gated, NT)
                    for n, w in enumerate((ln_g, ln_b)):
                        sp.dma_start(ln_gb[:, n, :], w[0:1, :].partition_broadcast(P)).then_inc(ln0_loaded, 16)
                if i >= 2:
                    sp.wait_ge(x1_set, i - 1)
                    sp.dma_start(x1_rows[(i - 2) * P:(i - 1) * P, :], zn[:, i % 2, :]).then_inc(x1_stored[i % 2], 16)
            for i in range(NT - 2, NT):
                sp.wait_ge(x1_set, i + 1)
                sp.dma_start(x1_rows[i * P:(i + 1) * P, :], zn[:, i % 2, :]).then_inc(x1_stored[i % 2], 16)
            for n, w in enumerate((ln_g, ln_b)):
                sp.dma_start(ln_gb[:, n, :], w[1:2, :].partition_broadcast(P)).then_inc(ln1_loaded, 16)

            plan.filled(sp, ("z0", NT - 1, 1))
            for n in range(4):
                slice_load("v1", n)
            for h in range(2, GH):
                plan.filled(sp, ("k1", 2 * (h - 2) + 1))
                wqk_load(h)
            for n in range(4, 2 * KD):
                if n == 6:
                    plan.filled(sp, ("k1", 2 * GH - 1))
                    sp.wait_ge(qk_set, 2 * GH)
                    for g in range(3):
                        slice_load("g1", g)
                slice_load("v1", n)

            def w_out1_load(q):
                await_slice(sp, "g1", KD + 2 * q + 1)
                sp.dma_start(w_out1[0][:, 2 * q:2 * q + 2, :],
                             odd_w_out[0].rearrange("(k p) n -> p k n", p=P)[:, 2 * q:2 * q + 2, :]).then_inc(
                    w_out1_loaded[q], 16)

            for n in range(3, 2 * KD):
                slice_load("g1", n)
                if n in (KD + 4, KD + 6):
                    w_out1_load((n - KD - 4) // 2)
            w_out1_load(2)
            w_out1_load(3)
            for s in range(2):
                sp.wait_ge(x1_stored[s], 16 * NT // 2)
            for i in range(NT + LAG):
                if i >= LAG:
                    j = i - LAG
                    if j == NT - 1:
                        sp.wait_ge(y_last_set, 1)
                    sp.wait_ge(y_set, j + 1)
                    sp.dma_start(out[0, j * P:(j + 1) * P, :], SG[:, j, :]).then_inc(y_stored[j % 2], 16)
                if i < NT:
                    plan.filled(sp, ("o1", i, 1))
                    sp.dma_start(V1[:, i, :], x1_rows[i * P:(i + 1) * P, :]).then_inc(x1_back[i % 4], 16)
            for s in range(2):
                sp.wait_ge(y_stored[s], 16 * NT // 2)

        @block.gpsimd
        def _(pool):
            step = Steps(pool, pool_step, plan)
            step(pool.memset(ident[:, :], 0.0))
            step(pool.affine_select(out=ident[:, :], in_=ident[:, :], compare_op=ALU.not_equal, fill=1.0,
                                    base=0, pattern=[[-1, P]], channel_multiplier=1), ident_set)
            step(pool.memset(ident_b[:, :], 0.0))
            step(pool.memset(causal_bias[:, :], 0.0))
            step(pool.memset(tile_tri[:, :, :], 1))
            step(pool.memset(sign[:, :], 1.0))
            step(pool.memset(eps[:, 0:1], 1e-5))
            step(pool.memset(eps[:, 1:2], 1e-6))
            for j in range(HALF):
                step(pool.memset(inv_freq[:, j:j + 1],
                                 float(np.float32(10000.0) ** np.float32(-j / HALF))))
            step(pool.iota(times[:, 0:LC + 1], [[1, LC + 1]], base=0, channel_multiplier=0,
                           allow_small_or_imprecise_dtypes=True))
            step(pool.iota(times[:, LC + 1:NTAB], [[LC, NC5]], base=0, channel_multiplier=0,
                           allow_small_or_imprecise_dtypes=True))
            step(pool.affine_select(out=ident_b[:, :], in_=ident_b[:, :], compare_op=ALU.not_equal, fill=1.0,
                                    base=0, pattern=[[-1, P]], channel_multiplier=1))
            step(pool.affine_select(out=causal_bias[:, :], in_=causal_bias[:, :], compare_op=ALU.is_ge,
                                    fill=-1e38, base=0, pattern=[[-1, P]], channel_multiplier=1))
            step(pool.affine_select(out=tile_tri[:, :, :], in_=tile_tri[:, :, :], compare_op=ALU.is_ge,
                                    fill=0.0, base=0, pattern=[[0, GH], [1, P]], channel_multiplier=-1))
            step.settle()
            step(pool.memset(sign[0:NS, 0:1], -1.0))
            step(pool.memset(sign[NS:P, 1:2], -1.0))
            step.settle()
            step(pool.memset(stat[:, :], 0.0), consts_set)

            pool.wait_ge(s5_turns_set, 1)
            phases(pool, step, 0, rot[:, :, :].rearrange("p a b -> p (a b)")[:, 0:8 * NTAB])

            pool.wait_ge(s5_powers_set, 1)
            for q in range(4):
                matrix_part(pool, step, rot[:, 1:3, :].rearrange("p a b -> p (a b)")[:, 0:4 * (LC + 1) * GS], q, NX,
                            LC + 1, LR[:, :, :], CA, LI[:, :, :], CB, ALU.subtract, s5_nx_set)
            for q in range(4):
                matrix_part(pool, step, rot[:, 2, :], q, N2, LC, LR[:, :, 1:LC + 1], CB, LI[:, :, 1:LC + 1], CA,
                            ALU.add, s5_n2_set)
            plan.filled(pool, ("MT", 3))
            step(pool.memset(TT[:, :, :], 0.0), s5_tt_zero)
            pool.wait_ge(rope_set, 1)
            for q in range(4):
                cos, sin = chunk_turns(q)
                pool.wait_ge(s5_scanned, q + 1)
                for table, turns in ((tabA, cos), (tabB, sin)):
                    step(pool.tensor_tensor(turns, scans[q % 2], turns, ALU.mult))
                    step(pool.memset(table[:, 4 * q:4 * q + 4, LC:LC + 1], 0.0),
                         s5_states_set if table is tabB else None)
            pool.wait_ge(s5_n2_set, 4)
            temps = [work[:, 128 * j:128 * (j + 1)].rearrange("p (h r) -> p h r", r=HALF) for j in range(4)]
            for i in range(NT):
                plan.drained(pool, ("q", i, 0))
                plan.drained(pool, ("q", i, 1))
                cos = rope_t[:, 2, i, :].unsqueeze(1).to_broadcast([P, H, HALF])
                sin = rope_t[:, 3, i, :].unsqueeze(1).to_broadcast([P, H, HALF])
                turn_pairs(pool, step, qt[:, :, NOPE:NOPE + HALF], qt[:, :, NOPE + HALF:QK], cos, sin, *temps,
                           q_turned)

            def split(raw, hi, lo, signal):
                step(pool.tensor_copy(hi, raw))
                step(pool.tensor_tensor(lo, raw, hi.bitcast(F32), ALU.subtract), signal)

            def wqk_split_head(h):
                pool.wait_ge(wqk_loaded[h % 2], 32 * (h // 2 + 1))
                for k in range(0, KD, 4):
                    split(*(t[:, k:k + 4, :, :].rearrange("p k n c -> p k (n c)") for t in wqk[h % 2]), wqk_split)

            def slice_split_at(name, n):
                ring_ = slices[name]
                pool.wait_ge(slice_loaded[name][n % len(ring_)], 16 * (n // len(ring_) + 1))
                split(*(t[:, :] for t in ring_[n % len(ring_)]), slice_split[name])

            pool.wait_ge(wgk_loaded, 16)
            split(*(t[:, :, :] for t in w_gk), wgk_split)
            for h in range(2):
                wqk_split_head(h)

            pool.wait_ge(ln0_loaded, 32)
            for i in range(NT):
                pool.wait_ge(centred, i + 1)
                z = zn[:, i % 2, :]
                step(pool.tensor_tensor(z, z, ln_gb[:, 0, :], ALU.mult))
                step(pool.tensor_tensor(z, z, ln_gb[:, 1, :], ALU.add), x1_set)
            for n in range(4):
                slice_split_at("v1", n)
            for h in range(2, GH):
                wqk_split_head(h)
            for name, first in (("v1", 4), ("g1", 0)):
                for n in range(first, 2 * KD):
                    slice_split_at(name, n)

            pool.wait_ge(two_ends_set, 1)
            plan.filled(pool, ("gate", 2 * GH - 1))

            def keys_at_end(i):
                if i >= 2:
                    plan.filled(pool, ("at", i - 2))
                first, second = slice(2 * i * GC, (2 * i + 1) * GC), slice((2 * i + 1) * GC, (2 * i + 2) * GC)
                step(pool.tensor_tensor(KS[i % 2][:, :, 0:GC], KI[:, :, first],
                                        ends[:, :, 2 * i:2 * i + 1].to_broadcast([P, GH, GC]), ALU.mult))
                step(pool.tensor_copy(KS[i % 2][:, :, GC:P], KI[:, :, second]), ks_set)

            keys_at_end(0)
            keys_at_end(1)
            pool.wait_ge(ln1_loaded, 32)
            for i in range(NT + LAG):
                if i + 2 < NT:
                    keys_at_end(i + 2)
                if i == 0:
                    plan.filled(pool, ("g1", 1, NT - 1))
                if 1 <= i < NT:
                    if i >= 3:
                        plan.filled(pool, ("o1", i - 2, 1))
                    for c, decays in enumerate((ends[:, :, 2 * i - 1:2 * i], two_ends[:, :, i:i + 1])):
                        step(pool.tensor_tensor(QS[:, i % 2, :, c * GC:(c + 1) * GC],
                                                QD[:, :, i * P + c * GC:i * P + (c + 1) * GC],
                                                decays.to_broadcast([P, GH, GC]), ALU.mult), qs_set if c else None)
                if i >= LAG:
                    j = i - LAG
                    pool.wait_ge(centred, NT + j + 1)
                    z = SG[:, j, LAST if j == NT - 1 else 0:D]
                    g, b = (ln_gb[:, n, LAST if j == NT - 1 else 0:D] for n in range(2))
                    step(pool.tensor_tensor(z, z, g, ALU.mult))
                    step(pool.tensor_tensor(z, z, b, ALU.add), y_set)

        @block.scalar
        def _(act):
            step = Steps(act, act_step, plan)
            def slice_hi(name, n):
                ring_ = slices[name]
                act.wait_ge(slice_loaded[name][n % len(ring_)], 16 * (n // len(ring_) + 1))
                raw, hi, _ = ring_[n % len(ring_)]
                step(act.activation(hi[:, :], raw[:, :], ACT.Copy), slice_hi_set[name])

            for i in range(NT):
                for half in range(2):
                    plan.filled(act, ("xT", i, half))
                    step(act.activation(xT_hi[:, 4 * half:4 * half + 4, i * P:(i + 1) * P],
                                        bank("xT", i, half).rearrange("p (k t) -> p k t", k=4), ACT.Copy), xT_hi_set)
                if i < EARLY:
                    slice_hi("gate0", i)
            for n in range(EARLY, 6):
                slice_hi("gate0", n)
            for n in range(3):
                slice_hi("ina", n)
            for n in range(6, KD):
                slice_hi("gate0", n)
            for i in range(NT):
                plan.filled(act, ("gate0", i))
                step.frees(act.activation(gate[:, i, :], bank("gate0", i), ACT.Silu), ("gate0", i))
            act.wait_ge(angles_set, 1)
            step(act.activation(rope_t[:, 3, :, :], rope_t[:, 0, :, :], ACT.Sin))
            step(act.activation(rope_t[:, 2, :, :], rope_t[:, 0, :, :], ACT.Sin, scale=0.5), sines_done)
            for n in range(2):
                slice_hi("ug", n)
            for n in range(3, KD):
                slice_hi("ina", n)
            for half in range(2):
                act.wait_ge(s5_phase_set[half], 1)
            step(act.activation(tabB[:, :, :], tabA[:, :, :], ACT.Sin, scale=-2 * PI_BELOW))
            step(act.activation(tabA[:, :, :], tabA[:, :, :], ACT.Sin, scale=PI_BELOW), s5_sin_set)
            act.wait_ge(consts_set, 1)
            for i in range(4):
                squares(act, step, i)
            slice_hi("ug", 2)
            for i in range(4, NT):
                squares(act, step, i)
            slice_hi("ug", 3)
            step(act.activation(stat[:, 16:24], stat[:, 0:8], ACT.Sqrt, bias=eps[:, 1:2], scale=1.0 / RQ))
            step(act.activation(stat[:, 24:32], stat[:, 8:16], ACT.Sqrt, bias=eps[:, 1:2], scale=1.0 / RKV),
                 squares_done)
            for n in range(4, KD):
                slice_hi("ug", n)
            for j in range(4):
                plan.filled(act, ("inu", j))
                step.frees(act.activation(U[:, :, 2 * j:2 * j + 2, :],
                                          bank("inu", j).rearrange("p (t g h) -> p g t h", t=2, g=G), ACT.Copy),
                           ("inu", j))
            for m in range(2):
                for n in range(2):
                    plan.filled(act, ("ings", m, n))
                    step.frees(act.activation(gs5[:, m, n * 512:(n + 1) * 512], bank("ings", m, n), ACT.Silu),
                               ("ings", m, n))
            for q in range(4):
                plan.filled(act, ("UT", q))
                step.frees(act.activation(UT[:, 4 * q:4 * q + 4, :].rearrange("p g c -> p (g c)"), bank("UT", q),
                                          ACT.Copy), ("UT", q))
            for q in range(4):
                plan.filled(act, ("K", q))
                step.frees(act.activation(Kt[:, 4 * q:4 * q + 4, :, :].rearrange("p g t h -> p (g t h)"),
                                          bank("K", q)[0:GS, :], ACT.Copy), ("K", q))
            act.wait_ge(s5_n2_set, 4)
            act.wait_ge(s5_d_added, 1)
            for i in range(NT):
                p, half = i // 2, i % 2
                plan.filled(act, ("kp", p, half))
                s = slice(half * 512, (half + 1) * 512)
                step(act.activation(kT[0:NOPE, 2 * p, s], bank("kp", p, half)[0:NOPE, :], ACT.Copy))
                step.frees(act.activation(kT[0:NOPE, 2 * p + 1, s], bank("kp", p, half)[NOPE:P, :], ACT.Copy),
                           ("kp", p, half))
                plan.filled(act, ("vp", i))
                step.frees(act.activation(V[:, i, :, :], bank("vp", i).rearrange("p (h d) -> p h d", h=H), ACT.Copy),
                           ("vp", i))
            def scaled_queries(n, half):
                plan.filled(act, ("q", n, half))
                step.frees(act.activation(qt[:, 4 * half:4 * half + 4, :],
                                          bank("q", n, half)[:, 0:4 * QK].rearrange("p (h d) -> p h d", h=4),
                                          ACT.Copy, scale=SCALE), ("q", n, half))

            scaled_queries(0, 0)
            scaled_queries(0, 1)
            for q in range(4):
                plan.filled(act, ("y", q))
                step.frees(act.activation(Y5[:, :, 4 * q:4 * q + 4, :],
                                          bank("y", q).rearrange("p (g t h) -> p t g h", g=4, t=LC),
                                          ACT.Gelu_apprx_tanh), ("y", q))
            scaled_queries(1, 0)
            scaled_queries(1, 1)
            y_turned(act, step, 0, 1)
            y_turned(act, step, 1, 1)
            act.wait_ge(small_loaded, 16 * 7)
            act.wait_ge(kpe_spread, 16 * H)
            act.wait_ge(s5_tt_set, 16 * LC)
            def exponentials(n):
                i, h = heads[n]
                src, place = scores(n)
                act.wait_ge(max_set, n + 1)
                before = n - (4 if n in SHORT else 2)
                if before >= 0:
                    plan.filled(act, ("pt", pt_jobs[heads[before]][-1][0]))
                step.frees(act.activation(prob[:, place:place + (i + 1) * P], src, ACT.Exp, bias=negmax[:, n % 4:n % 4 + 1],
                                          accum_out=rsum[:, i % 2, h:h + 1]), ("s", n))

            for n in range(4):
                exponentials(n)
            act.wait_ge(bias_turned, 1)
            for k in range(4):
                job = ("glu", k // 2, k % 2)
                plan.filled(act, job)
                step.frees(act.activation(SGL[:, k, :], bank(*job), ACT.Exp, scale=-1.0,
                                          bias=gla_c[:, 6 + k // 2:7 + k // 2]), job)
            for what, n in attention_steps():
                if what == "q":
                    scaled_queries(*n)
                elif what == "pt":
                    if 4 <= n + 1 < len(heads):
                        exponentials(n + 1)
                    for number, first, blocks in pt_jobs[heads[n]][1:]:
                        copy_probs(act, step, number, first, blocks)
            for i in range(NT + 1):
                if i < NT:
                    act.wait_ge(var_set, i + 1)
                    step(act.activation(stat[:, 20:21], stat[:, 1:2], ACT.Sqrt, bias=eps[:, 0:1]), root_set)
                if i == NT:
                    plan.filled(act, ("gk", 0))
                    step.frees(act.activation(gkT[:, 0:512], bank("gk", 0)[0:GR, :], ACT.Copy), ("gk", 0))
                if i:
                    for half in range(2):
                        plan.filled(act, ("x1T", i - 1, half))
                        step(act.activation(x1T_hi[:, 4 * half:4 * half + 4, (i - 1) * P:i * P],
                                            bank("x1T", i - 1, half).rearrange("p (k t) -> p k t", k=4), ACT.Copy),
                             x1_hi_set)
            plan.filled(act, ("gk", 1))
            step.frees(act.activation(gkT[:, 512:1024], bank("gk", 1)[0:GR, :], ACT.Copy), ("gk", 1))
            for h in range(GH + 1):
                if h < GH:
                    for n in range(2):
                        m = 2 * h + n
                        plan.filled(act, ("gate", m))
                        if h:
                            act.wait_ge(scanned, m - 1)
                        step.frees(act.activation(zb[:, n, :], bank("gate", m), ACT.Identity, bias=gla_c[:, h:h + 1]),
                                   ("gate", m))
                        step(act.activation(soft[:, n, :], zb[:, n, :], ACT.Abs))
                    step(act.activation(soft[:, :, :], soft[:, :, :], ACT.Exp, scale=-1.0))
                if h:
                    act.wait_ge(scanned, 2 * h)
                    if h >= 2:
                        act.wait_ge(qk_set, 2 * h - 2)
                    step(act.activation(dec[:, :, 0, :], cum[:, :, :], ACT.Exp, scale=1.0 / 16))
                    step(act.activation(dec[:, :, 1, :], cum[:, :, :], ACT.Exp, scale=-1.0 / 16), decay_set)
                if h < GH:
                    step(act.activation(soft[:, :, :], soft[:, :, :], ACT.Ln, bias=1.0), soft_set)
            for s in range(2):
                act.wait_ge(x1_stored[s], 16 * NT // 2)
            for c in range(2):
                for i in range(NT):
                    plan.filled(act, ("v1", c, i))
                    step.frees(act.activation(V1[:, i, c * 512:(c + 1) * 512], bank("v1", c, i), ACT.Copy),
                               ("v1", c, i))

            def w_out1_hi(k):
                act.wait_ge(w_out1_loaded[k // 2], 16)
                step(act.activation(w_out1[1][:, k, :], w_out1[0][:, k, :], ACT.Copy,
                                    scale=gla_c[:, 4 + k % 2:5 + k % 2]), w_out1_hi_set)

            for c in range(2):
                if c:
                    for k in range(KD - 2):
                        w_out1_hi(k)
                for i in range(NT):
                    plan.filled(act, ("g1", c, i))
                    step.frees(act.activation(SG[:, i, c * 512:(c + 1) * 512], bank("g1", c, i), ACT.Silu),
                               ("g1", c, i))
            for what, i in gla_steps():
                if what == "kT1":
                    plan.filled(act, ("kT1", i))
                    if i >= 2:
                        plan.filled(act, ("ks", i - 2, 1))
                    step.frees(act.activation(kTok[:, i % 2, :, :], bank("kT1", i).rearrange("p (h d) -> p h d", h=GH),
                                              ACT.Copy), ("kT1", i))
                elif what == "o":
                    for hp in range(2):
                        plan.filled(act, ("o1", i, hp))
                        for j in range(2):
                            step(act.activation(sq[:, :], bank("o1", i, hp)[:, j * GDV:(j + 1) * GDV], ACT.Square,
                                                accum_out=stat[:, 32 + 2 * hp + j:33 + 2 * hp + j]))
                            step.settle()
                    r = 36 + 4 * (i % 2)
                    step(act.activation(stat[:, r:r + 4], stat[:, 32:36], ACT.Sqrt, bias=eps[:, 1:2], scale=1.0 / GDV),
                         ms_set)
                    if i == 0:
                        w_out1_hi(KD - 2)
                        w_out1_hi(KD - 1)
                elif what == "yT1":
                    for half in range(2):
                        plan.filled(act, ("yT1", i, half))
                        if half == 0:
                            y1t_free(act, i)
                        step(act.activation(Y1T[y1t_slot(i)][0][:, 4 * half:4 * half + 4, :],
                                            bank("yT1", i, half).rearrange("p (k t) -> p k t", k=4), ACT.Copy),
                             yT1_hi_set)
                elif what == "z1":
                    act.wait_ge(var_set, NT + i + 1)
                    step(act.activation(stat[:, 20:21], stat[:, 1:2], ACT.Sqrt, bias=eps[:, 0:1]), root_set)

        @block.vector
        def _(vec):
            step = Steps(vec, vec_step, plan)
            C1, C2, C3 = two_pi_parts()
            INV_2PI = float(np.float32(1 / (2 * math.pi)))

            def serial(ins, signal=None):
                step(ins, signal)
                step.settle()

            def reduce_angle(angle, turns, signal=None):
                serial(vec.tensor_scalar(turns, angle, INV_2PI, TO_INT, ALU.mult, ALU.add))
                serial(vec.tensor_scalar(turns, turns, TO_INT, None, ALU.subtract))
                for part in (C1, C2, C3):
                    serial(vec.scalar_tensor_tensor(angle, turns, -part, angle, ALU.mult, ALU.add))
                serial(vec.tensor_scalar(angle, angle, PI_BELOW, -PI_BELOW, ALU.min, ALU.max), signal)

            def layer_norm(zt, res, job, i, tile_no):
                for n in range(2):
                    plan.filled(vec, (job, i, n))
                    s = slice(n * 512, (n + 1) * 512)
                    step.frees(vec.scalar_tensor_tensor(zt[:, s], res[:, s], ALPHA, bank(job, i, n),
                                                        ALU.mult, ALU.add), (job, i, n))
                    step.settle()
                    serial(vec.bn_stats(stat[:, 48 + 6 * n:54 + 6 * n], zt[:, s]))
                serial(vec.bn_aggr(stat[:, 0:2], stat[:, 48:60]), var_set)
                vec.wait_ge(root_set, tile_no + 1)
                serial(vec.reciprocal(stat[:, 21:22], stat[:, 20:21]))
                step(vec.tensor_scalar(zt, zt, stat[:, 0:1], stat[:, 21:22], ALU.subtract, ALU.mult), centred)

            def slice_lo(name, n):
                vec.wait_ge(slice_hi_set[name], n + 1)
                raw, hi, lo = slices[name][n % len(slices[name])]
                step(vec.tensor_tensor(lo[:, :], raw[:, :], hi[:, :].bitcast(F32), ALU.subtract), slice_split[name])

            for i in range(NT):
                for half in range(2):
                    vec.wait_ge(xT_hi_set, 2 * i + half + 1)
                    src = bank("xT", i, half).rearrange("p (k t) -> p k t", k=4)
                    for part, (a, b) in enumerate((((0, 2), (2, 4)), ((4, 7), (7, 8)))[half]):
                        ins = vec.tensor_tensor(xT_lo_parts[2 * half + part][:, :, i * P:(i + 1) * P],
                                                src[:, a - 4 * half:b - 4 * half, :],
                                                xT_hi[:, a:b, i * P:(i + 1) * P].bitcast(F32), ALU.subtract)
                        if part:
                            step.frees(ins, ("xT", i, half))
                        else:
                            step(ins)
                if i < EARLY:
                    slice_lo("gate0", i)
            vec.wait_ge(consts_set, 1)
            for n in range(EARLY, 6):
                slice_lo("gate0", n)
            for n in range(3):
                slice_lo("ina", n)
            vec.wait_ge(par_loaded, 16 * 5)
            exact_exp(vec, step, dts[:, 0:1], dts[:, 1:2], dts[:, 2:3], dti[:, 0:1])
            step(vec.tensor_scalar(par[:, 0, :], par[:, 2, :], dts[:, 0:1], None, ALU.mult))
            step(vec.tensor_scalar(par[:, 1, :], par[:, 3, :], dts[:, 0:1], None, ALU.mult), s5_par_set)
            vec.wait_ge(small_loaded, 16 * 7)
            step(vec.tensor_scalar(gla_c[:, 6:8], gla_c[:, 6:8], -1.0, None, ALU.mult), bias_turned)
            serial(vec.tensor_copy(pos_f[:, :], pos_i[:, :]))
            serial(vec.tensor_tensor(rope_t[:, 0, :, :], pos_f[:, :].unsqueeze(2).to_broadcast([P, NT, HALF]),
                                     inv_freq[:, :].unsqueeze(1).to_broadcast([P, NT, HALF]), ALU.mult))
            reduce_angle(rope_t[:, 0, :, :], rope_t[:, 1, :, :], angles_set)
            for n in range(6, KD):
                slice_lo("gate0", n)
            plan.filled(vec, ("par",))
            step.frees(vec.tensor_copy(parT[:, :, :], bank("par")[:, 0:4 * G].rearrange("p (a g) -> p a g", a=4)),
                       ("par",))
            step.settle()
            serial(vec.tensor_copy(sm[:, 0, :], parT[:, 1, :]))
            reduce_angle(sm[:, 0, :], sm[:, 1, :])
            serial(vec.tensor_scalar(sm[:, 0, :], sm[:, 0, :], INV_2PI, None, ALU.mult))
            serial(vec.tensor_scalar(sm[:, 4, :], sm[:, 0, :], TO_13_BITS, None, ALU.add))
            serial(vec.tensor_scalar(sm[:, 4, :], sm[:, 4, :], TO_13_BITS, None, ALU.subtract))
            serial(vec.tensor_tensor(sm[:, 5, :], sm[:, 0, :], sm[:, 4, :], ALU.subtract), s5_turns_set)
            plan.filled(vec, ("crow",))
            cps = bank("crow").rearrange("p (s n) -> p s n", s=2)
            step(vec.tensor_scalar(CA[:, :, :].rearrange("p g h -> p (g h)"), cps[:, 0, :], sign[:, 1:2], None,
                                   ALU.mult))
            step.frees(vec.tensor_copy(CB[:, :, :].rearrange("p g h -> p (g h)"), cps[:, 1, :]), ("crow",))
            vec.wait_ge(sines_done, 1)
            serial(vec.scalar_tensor_tensor(rope_t[:, 2, :, :], rope_t[:, 2, :, :], -2.0, rope_t[:, 2, :, :],
                                            ALU.mult, ALU.mult))
            serial(vec.tensor_scalar(rope_t[:, 2, :, :], rope_t[:, 2, :, :], 1.0, None, ALU.add), rope_set)
            for n in range(2):
                slice_lo("ug", n)
            slice_lo("ina", 3)
            e4 = [ex[:, j, :].rearrange("p (g t) -> p g t", g=G) for j in range(4)]
            serial(vec.tensor_tensor(e4[0], parT[:, 0, :].unsqueeze(2).to_broadcast([P, G, LC + 1]),
                                     times[:, 0:LC + 1].unsqueeze(1).to_broadcast([P, G, LC + 1]), ALU.mult))
            exact_exp(vec, step, ex[:, 0, :], ex[:, 1, :], ex[:, 2, :], exi[:, :])
            slice_lo("ina", 4)
            phases(vec, step, 8, turn_work[:, :], lambda: slice_lo("ina", 5))
            for n in range(6, KD):
                slice_lo("ina", n)
            for i in range(NT):
                plan.filled(vec, ("ina", i))
                step.frees(vec.tensor_copy(cqkv[:, i, :], bank("ina", i)[:, 0:NA]), ("ina", i))
            for n in range(2, 4):
                slice_lo("ug", n)
            vec.wait_ge(squares_done, 1)
            serial(vec.reciprocal(stat[:, 32:48], stat[:, 16:32]))
            for i in range(NT):
                step(vec.tensor_scalar(cqkv[:, i, 0:RQ], cqkv[:, i, 0:RQ], stat[:, 32 + i:33 + i], None, ALU.mult))
                step(vec.tensor_scalar(cqkv[:, i, RQ:RQ + RKV], cqkv[:, i, RQ:RQ + RKV], stat[:, 40 + i:41 + i],
                                       None, ALU.mult), latents_scaled)
            slice_lo("ug", 4)
            temps = [key_temps[:, j, :].rearrange("p (t r) -> p t r", r=HALF) for j in range(4)]
            k0 = RQ + RKV
            turn_pairs(vec, step, cqkv[:, :, k0:k0 + HALF], cqkv[:, :, k0 + HALF:k0 + ROPE], rope_t[:, 2, :, :],
                       rope_t[:, 3, :, :], *temps, keys_turned)
            slice_lo("ug", 5)
            slice_lo("ug", 6)
            vec.wait_ge(s5_sin_set, 1)
            serial(vec.scalar_tensor_tensor(tabA[:, :, :], tabA[:, :, :], -2.0, tabA[:, :, :], ALU.mult, ALU.mult))
            powers = slice(0, LC + 1)
            step(vec.tensor_tensor(LR[:, :, :], e4[0], tabA[:, :, powers], ALU.mult))
            step(vec.scalar_tensor_tensor(LI[:, :, :], e4[0], -1.0, tabB[:, :, powers], ALU.mult, ALU.mult))
            step(vec.tensor_copy(mag8[:, :], e4[0][:, :, LC]))
            serial(vec.tensor_scalar(sm[:, 0, :], e4[0][:, :, 1], -1.0, None, ALU.add))
            nr, ni, ar, ai = sm[:, 0, :], LI[:, :, 1], parT[:, 2, :], parT[:, 3, :]
            serial(vec.tensor_tensor(nr, nr, LR[:, :, 1], ALU.add))
            step(vec.tensor_tensor(LR[:, :, :], LR[:, :, :], e4[0], ALU.add))
            step(vec.tensor_scalar(tabA[:, :, :], tabA[:, :, :], 1.0, None, ALU.add), s5_powers_set)
            den, t1, t2, zr, zi, zs = (sm[:, j, :] for j in (1, 2, 3, 4, 5, 6))
            step(vec.tensor_tensor(t1, ar, ar, ALU.mult))
            step(vec.tensor_tensor(t2, ai, ai, ALU.mult))
            step.settle()
            serial(vec.tensor_tensor(den, t1, t2, ALU.add))
            serial(vec.reciprocal(den, den))
            step(vec.tensor_tensor(t1, nr, ar, ALU.mult))
            step(vec.tensor_tensor(t2, ni, ai, ALU.mult))
            step.settle()
            serial(vec.tensor_tensor(zr, t1, t2, ALU.add))
            step(vec.tensor_tensor(t1, ni, ar, ALU.mult))
            step(vec.tensor_tensor(t2, nr, ai, ALU.mult))
            step.settle()
            serial(vec.tensor_tensor(zi, t1, t2, ALU.subtract))
            step(vec.tensor_tensor(zr, zr, den, ALU.mult))
            serial(vec.tensor_tensor(zi, zi, den, ALU.mult))
            serial(vec.tensor_scalar(zs, zi, sign[:, 0:1], None, ALU.mult))
            vec.wait_ge(bc_loaded, 16 * 9)
            wide = [P, G, GS]
            zr_b, zs_b = zr.unsqueeze(2).to_broadcast(wide), zs.unsqueeze(2).to_broadcast(wide)
            w0 = work[:, 0:G * GS].rearrange("p (g h) -> p g h", g=G)
            w1 = work[:, G * GS:2 * G * GS].rearrange("p (g h) -> p g h", g=G)
            step(vec.tensor_tensor(Bst[:, :, :], BA[:, :, :], zr_b, ALU.mult))
            step(vec.tensor_tensor(w0, BB[:, :, :], zs_b, ALU.mult))
            step(vec.tensor_tensor(Bsw[:, :, :], BB[:, :, :], zr_b, ALU.mult))
            step(vec.tensor_tensor(w1, BA[:, :, :], zs_b, ALU.mult))
            step.settle()
            step(vec.tensor_tensor(Bst[:, :, :], Bst[:, :, :], w0, ALU.add), s5_b_set)
            serial(vec.tensor_tensor(Bsw[:, :, :], Bsw[:, :, :], w1, ALU.subtract))

            LIs = ex[:, 1, :].rearrange("p (g t) -> p g t", g=G)
            serial(vec.tensor_scalar(LIs, LI[:, :, :], sign[:, 0:1], None, ALU.mult))
            def make_m(t):
                j = LC - 1 - t
                a = LR[:, :, j].unsqueeze(2).to_broadcast(wide)
                b = LIs[:, :, j].unsqueeze(2).to_broadcast(wide)
                w = w0 if t % 2 else w1
                step(vec.tensor_tensor(M[:, :, t, :], Bst[:, :, :], a, ALU.mult))
                step(vec.tensor_tensor(w, Bsw[:, :, :], b, ALU.mult))
                step(vec.tensor_tensor(M[:, :, t, :], M[:, :, t, :], w, ALU.add), s5_m_set)

            for i in range(NT):
                make_m(i)
                if i == 1:
                    slice_lo("ug", 7)
            for i in range(NT):
                plan.filled(vec, ("cT", i))
                s = slice(i * P, (i + 1) * P)
                step(vec.tensor_tensor(cT[:, :, s], bank("cT", i)[:, 0:384].rearrange("p (k t) -> p k t", k=3),
                                       norm_w[:, :].unsqueeze(2).to_broadcast([P, 3, P]), ALU.mult))
                step.frees(vec.tensor_copy(kpeT[NOPE:QK, s], bank("cT", i)[0:ROPE, 384:512]), ("cT", i))
            for q in range(4):
                plan.filled(vec, ("MT", q))
                step.frees(vec.tensor_copy(MT[:, 4 * q:4 * q + 4, :],
                                           bank("MT", q).rearrange("p (g s) -> p g s", g=4)), ("MT", q))
            for q in range(4):
                plan.drained(vec, ("K", q))
            serial(vec.tensor_tensor(DD[:, :, :], ident[0:GS, 0:GS].unsqueeze(1).to_broadcast([GS, G, GS]),
                                     Dt[:, :].unsqueeze(2).to_broadcast([GS, G, GS]), ALU.mult))
            step(vec.tensor_tensor(Kt[:, :, 0, :], Kt[:, :, 0, :], DD[:, :, :], ALU.add), s5_d_added)
            vec.wait_ge(s5_n2_set, 4)
            for q in range(4):
                cos, sin = chunk_turns(q)
                w, v = (rot[:, j, :].rearrange("p (g c) -> p g c", g=4) for j in range(2))
                h = scans[q % 2]
                if q >= 2:
                    vec.wait_ge(s5_states_set, q - 1)
                plan.filled(vec, ("v", q))
                step(vec.tensor_tensor(w, bank("v", q).rearrange("p (g c) -> p g c", g=4), cos, ALU.mult))
                src = bank("v", q).rearrange("p (g c) -> p g c", g=4)
                step(vec.tensor_tensor(v[0:NS], src[NS:P], sin[NS:P], ALU.mult))
                step.frees(vec.tensor_tensor(v[NS:P], src[0:NS], sin[0:NS], ALU.mult), ("v", q))
                serial(vec.scalar_tensor_tensor(rot[:, 0, :], rot[:, 1, :], sign[:, 0:1], rot[:, 0, :],
                                                ALU.mult, ALU.add))
                for j in range(4):
                    step(vec.tensor_tensor_scan(h[:, j, :], mag8[:, 4 * q + j:4 * q + j + 1].to_broadcast([P, NC5]),
                                                w[:, j, :], 0.0, ALU.mult, ALU.add), s5_scanned if j == 3 else None)

            def queries_turned(n, half):
                plan.filled(vec, ("qT", n, half))
                step.frees(vec.tensor_copy(qTt[:, n % 2, 4 * half:4 * half + 4, :],
                                           bank("qT", n, half)[0:QK, :].rearrange("p (h t) -> p h t", h=4)),
                           ("qT", n, half))

            def score_max(n):
                plan.filled(vec, ("s", n))
                step(vec.tensor_reduce(negmax[:, n % 4:n % 4 + 1], scores(n)[0], AX_X, ALU.max, negate=True), max_set)

            vec.wait_ge(kpe_spread, 16 * H)
            vec.wait_ge(s5_tt_set, 16 * LC)
            queries_turned(0, 0)
            queries_turned(0, 1)
            y_turned(vec, step, 0, 0)
            y_turned(vec, step, 1, 0)
            for n in range(4):
                score_max(n)
            for k in range(4):
                plan.drained(vec, ("yT", k // 2, k % 2))
            for k in range(4):
                m, n = k // 2, k % 2
                s = slice(n * 512, (n + 1) * 512)
                step(vec.tensor_tensor(gs5[:, m, s], gs5[:, m, s], YT[:, m, s], ALU.mult))

            def sigmoid_gate(j):
                k, s = j // 4, slice(j % 4 * P, (j % 4 + 1) * P)
                m, c0 = k // 2, k % 2 * 512 + j % 4 * P
                plan.drained(vec, ("glu", m, k % 2))
                step(vec.tensor_scalar(SGL[:, k, s], SGL[:, k, s], 1.0, None, ALU.add))
                step(vec.reciprocal(SGL[:, k, s], SGL[:, k, s]))
                step(vec.tensor_tensor(gs5[:, m, c0:c0 + P], gs5[:, m, c0:c0 + P], SGL[:, k, s], ALU.mult), s5_out_set)

            for what, n in attention_steps():
                if what == "qT":
                    queries_turned(*n)
                elif what == "s":
                    score_max(n)
                elif what == "pt":
                    number, first, blocks = pt_jobs[heads[n]][0]
                    copy_probs(vec, step, number, first, blocks)
                    if 44 <= n < 60:
                        sigmoid_gate(n - 44)
                elif what == "av" and heads[n][1] == H - 1:
                    i = heads[n][0]
                    plan.filled(vec, ("o", i))
                    plan.drained(vec, ("s", n))
                    serial(vec.reciprocal(rinv[:, i % 2, :], rsum[:, i % 2, :]))
                    o3 = rot[:, 0, :].rearrange("p (h d) -> p h d", h=H)
                    step.frees(vec.tensor_tensor(o3, bank("o", i).rearrange("p (h d) -> p h d", h=H),
                                                 rinv[:, i % 2, :].unsqueeze(2).to_broadcast([P, H, VD]), ALU.mult),
                               ("o", i))
                    step.settle()
                    step(vec.tensor_tensor(gate[:, i, :], gate[:, i, :], rot[:, 0, :], ALU.mult), gated)
                elif what == "OT":
                    plan.filled(vec, ("OT", n))
                    step.frees(vec.tensor_copy(OT[:, :, n * P:(n + 1) * P],
                                               bank("OT", n).rearrange("p (k t) -> p k t", k=4)), ("OT", n))
            for i in range(NT + 1):
                if i < NT:
                    vec.wait_ge(xres_loaded[i % 2], 16 * (i // 2 + 1))
                    if i >= 2:
                        vec.wait_ge(x1_stored[i % 2], 16 * (i // 2))
                    layer_norm(zn[:, i % 2, :], x_res[:, i % 2, :], "z0", i, i)
                if i:
                    for half in range(2):
                        vec.wait_ge(x1_hi_set, 2 * (i - 1) + half + 1)
                        at_ = (slice(None), slice(4 * half, 4 * half + 4), slice((i - 1) * P, i * P))
                        step.frees(vec.tensor_tensor(x1T_lo[at_], bank("x1T", i - 1, half).rearrange("p (k t) -> p k t", k=4),
                                                     x1T_hi[at_].bitcast(F32), ALU.subtract), ("x1T", i - 1, half))
            step(vec.memset(resets[:, :], 1.0))
            step.settle()
            serial(vec.memset(resets[:, :].rearrange("p (c t) -> p c t", t=GC)[:, :, 0:1], 0.0))
            for h in range(GH + 1):
                for n in range(2 if h else 0):
                    m = 2 * h - 2 + n
                    s = slice(n * 512, (n + 1) * 512)
                    vec.wait_ge(decay_set, h)
                    plan.filled(vec, ("q1", m))
                    step.frees(vec.scalar_tensor_tensor(QD[:, h - 1, s], bank("q1", m), GDK ** -0.5, dec[:, n, 0, :],
                                                        ALU.mult, ALU.mult), ("q1", m))
                    plan.filled(vec, ("k1", m))
                    step.frees(vec.tensor_tensor(KI[:, h - 1, s], bank("k1", m), dec[:, n, 1, :], ALU.mult),
                               ("k1", m))
                    step(vec.tensor_copy(ends[:, h - 1, 8 * n:8 * n + 8],
                                         dec[:, n, 0, :].rearrange("p (c t) -> p c t", t=GC)[:, :, GC - 1]), qk_set)
                for n in range(2 if h < GH else 0):
                    vec.wait_ge(soft_set, h + 1)
                    z = zb[:, n, :]
                    serial(vec.scalar_tensor_tensor(z, z, 0.0, soft[:, n, :], ALU.min, ALU.subtract))
                    step(vec.tensor_tensor_scan(cum[:, n, :], resets[:, :], z, 0.0, ALU.mult, ALU.add), scanned)
            step(vec.tensor_tensor(two_ends[:, :, 1:NT], ends[:, :, 1:NCH - 1:2], ends[:, :, 2:NCH:2], ALU.mult),
                 two_ends_set)
            step(vec.memset(att[:, :, :, :], 0.0))

            def w_out1_lo(k):
                vec.wait_ge(w_out1_hi_set, k + 1)
                step(vec.scalar_tensor_tensor(w_out1[2][:, k, :], w_out1[0][:, k, :], gla_c[:, 4 + k % 2:5 + k % 2],
                                              w_out1[1][:, k, :].bitcast(F32), ALU.mult, ALU.subtract), w_out1_split)

            for k in range(KD - 2):
                w_out1_lo(k)
            for what, i in gla_steps():
                if what == "at":
                    plan.filled(vec, ("at", i))
                    if i >= 2:
                        plan.filled(vec, ("o1", i - 2, 1))
                    step.frees(vec.copy_predicated(att[:, i % 2, :, :], tile_tri[:, :, :],
                                                   bank("at", i).rearrange("p (h c) -> p h c", h=GH)), ("at", i))
                elif what == "ks":
                    for hp in range(2):
                        plan.filled(vec, ("ks", i, hp))
                        for j in range(2):
                            h = 2 * hp + j
                            src = bank("ks", i, hp)[:, j * GDV:(j + 1) * GDV]
                            if i == 0:
                                ins = vec.tensor_copy(state[:, 0, h, :], src)
                            else:
                                ins = vec.scalar_tensor_tensor(state[:, i % 2, h, :], state[:, (i - 1) % 2, h, :],
                                                               two_ends[:, h, i:i + 1], src, ALU.mult, ALU.add)
                            if j:
                                step.frees(ins, ("ks", i, hp))
                            else:
                                step(ins)
                    step.settle()
                elif what == "o":
                    vec.wait_ge(ms_set, i + 1)
                    serial(vec.reciprocal(stat[:, 44:48], stat[:, 36 + 4 * (i % 2):40 + 4 * (i % 2)]))
                    for hp in range(2):
                        for j in range(2):
                            h = 2 * hp + j
                            s = slice(h * GDV, (h + 1) * GDV)
                            ins = vec.scalar_tensor_tensor(SG[:, i, s], bank("o1", i, hp)[:, j * GDV:(j + 1) * GDV],
                                                           stat[:, 44 + h:45 + h], SG[:, i, s], ALU.mult, ALU.mult)
                            if j:
                                step.frees(ins, ("o1", i, hp))
                            else:
                                step(ins)
                    if i == 0:
                        w_out1_lo(KD - 2)
                        w_out1_lo(KD - 1)
                elif what == "yT1":
                    for half in range(2):
                        vec.wait_ge(yT1_hi_set, 2 * i + half + 1)
                        ks = slice(4 * half, 4 * half + 4)
                        hi, lo = Y1T[y1t_slot(i)]
                        step.frees(vec.tensor_tensor(lo[:, ks, :],
                                                     bank("yT1", i, half).rearrange("p (k t) -> p k t", k=4),
                                                     hi[:, ks, :].bitcast(F32), ALU.subtract), ("yT1", i, half))
                elif what == "z1":
                    vec.wait_ge(x1_back[i % 4], 16 * (i // 4 + 1))
                    layer_norm(SG[:, i, :], V1[:, i, :], "z1", i, NT + i)
                    if i == NT - 1:
                        vec.wait_ge(ln1_loaded, 32)
                        z = SG[:, i, 0:LAST]
                        step(vec.tensor_tensor(z, z, ln_gb[:, 0, 0:LAST], ALU.mult))
                        step(vec.tensor_tensor(z, z, ln_gb[:, 1, 0:LAST], ALU.add), y_last_set)

        @block.tensor
        def _(pe):
            def group(job, out, pairs, last=True):
                for k, (lhsT, rhs) in enumerate(pairs):
                    mm = pe.matmul(out, lhsT, rhs, start=(k == 0), stop=(k == len(pairs) - 1))
                if last:
                    mm.then_inc(plan.full(job), 1)

            def turned(job, blocks, identity=ident):
                plan.claim(pe, job)
                for k, (block_in, rows) in enumerate(blocks):
                    cols = block_in.shape[0]
                    mm = pe.transpose(bank(*job)[0:rows, k * P:k * P + cols], block_in, identity[0:cols, 0:cols])
                mm.then_inc(plan.full(job), 1)

            def split_pairs(pairs):
                return [pair for (a_hi, a_lo), (b_hi, b_lo) in pairs
                        for pair in ((a_hi, b_hi), (a_hi, b_lo), (a_lo, b_hi))]

            pe.wait_ge(ident_set, 1)
            def by_slices(name, chunks, products, ks=range(KD), frees=True):
                ring_ = slices[name]
                for c in range(chunks):
                    for k in ks:
                        n = c * KD + k
                        pe.wait_ge(slice_split[name], n + 1)
                        claimed = set()
                        for job, c0, c1, last, pairs in products(c, k, [w_[:, :] for w_ in ring_[n % len(ring_)][1:]]):
                            if k == 0 and job not in claimed:
                                plan.claim(pe, job)
                                claimed.add(job)
                            pairs = split_pairs([pairs])
                            for j, (lhsT, rhs) in enumerate(pairs):
                                mm = pe.matmul(bank(*job)[:, c0:c1], lhsT, rhs, start=(k == 0 and j == 0 and c0 == 0),
                                               stop=(k == KD - 1 and j == len(pairs) - 1), skip_group_check=True)
                            if k == KD - 1 and last:
                                mm.then_inc(plan.full(job), 1)
                        if k < KD - 1 and frees:
                            mm.then_inc(slice_used[name], 1)

            def x_parts(k):
                return xT_hi[:, k, :], xT_lo[k]

            def token_tiles(name, columns, tiles=range(NT)):
                return lambda c, k, w: [((name, i), 0, columns, True, ([x_[:, i * P:(i + 1) * P] for x_ in x_parts(k)], w))
                                        for i in tiles]

            def u_and_gate(c, k, w):
                steps = [x_.rearrange("p (c t) -> p t c", t=LC) for x_ in x_parts(k)]
                for t in range(LC):
                    yield ("inu", t // 2), t % 2 * W5, (t % 2 + 1) * W5, t % 2 == 1, ([x_[:, t, :] for x_ in steps],
                                                                                     [w_[:, 0:W5] for w_ in w])
                for m in range(2):
                    for n in range(2):
                        yield ("ings", m, n), 0, 512, True, ([w_[:, W5 + m * P:W5 + (m + 1) * P] for w_ in w],
                                                             [x_[:, n * 512:(n + 1) * 512] for x_ in x_parts(k)])

            for i in range(NT + X_LAG):
                if i < NT:
                    pe.wait_ge(x_loaded[i % 4], 16 * (i // 4 + 1))
                    for half in range(2):
                        turned(("xT", i, half), [(x_ring[:, i % 4, k * P:(k + 1) * P], P)
                                                 for k in range(4 * half, 4 * half + 4)])
                if i >= X_LAG:
                    for half in range(2):
                        plan.drained(pe, ("xT", i - X_LAG, half))
                    by_slices("gate0", 1, token_tiles("gate0", 512, [i - X_LAG]),
                              range(EARLY), i == NT + X_LAG - 1)
            by_slices("gate0", 1, token_tiles("gate0", 512), range(EARLY, KD))
            pe.wait_ge(s5_par_set, 1)
            plan.claim(pe, ("par",))
            for j in range(4):
                mm = pe.transpose(bank("par")[:, j * G:(j + 1) * G], par[:, j, :], ident[0:G, 0:G])
            mm.then_inc(plan.full(("par",)), 1)
            pe.wait_ge(bc_loaded, 16 * 9)
            turned(("crow",), [(crow[:, s, r, :], P) for s in range(2) for r in range(2)])
            by_slices("ina", 1, token_tiles("ina", NA))
            by_slices("ug", 1, u_and_gate)

            def queries(n, half):
                plan.claim(pe, ("q", n, half))
                cols = slice(4 * half * QK, 4 * (half + 1) * QK)
                group(("q", n, half), bank("q", n, half)[:, 0:4 * QK],
                      [(cT[:, k, n * P:(n + 1) * P], w_uq[:, k, cols]) for k in range(2)])

            def queries_turn(n, half):
                pe.wait_ge(q_turned, n + 1)
                turned(("qT", n, half), [(qt[:, h, :], QK) for h in range(4 * half, 4 * half + 4)])

            def score(n):
                i, h = heads[n]
                if h % 4 == 0:
                    plan.drained(pe, ("qT", i, h // 4))
                plan.claim(pe, ("s", n))
                slot = score_banks(n)[0]
                w = (i + 1) * P
                for part in range((w + 511) // 512):
                    c0, c1 = part * 512, min(w, part * 512 + 512)
                    diag = c1 == w
                    mm = pe.matmul(psum[:, slot + part, 0:c1 - c0], qTt[:, i % 2, h, :], kT[:, h, c0:c1],
                                   start=True, stop=not diag, skip_group_check=diag)
                    if diag:
                        mm = pe.matmul(psum[:, slot + part, c1 - c0 - P:c1 - c0], ident_b[:, :],
                                       causal_bias[:, :], start=False, stop=True, skip_group_check=True)
                mm.then_inc(plan.full(("s", n)), 1)

            for what, n in middle_steps():
                if what == "UT":
                    if n == 0:
                        for j in range(4):
                            plan.drained(pe, ("inu", j))
                    turned(("UT", n), [(U[:, g, :, :].rearrange("p t h -> p (t h)"), P) for g in range(4 * n, 4 * n + 4)])
                elif what == "cT":
                    if n == 0:
                        pe.wait_ge(latents_scaled, NT)
                        pe.wait_ge(keys_turned, 1)
                    turned(("cT", n), [(cqkv[:, n, 0:P], P), (cqkv[:, n, P:2 * P], P), (cqkv[:, n, 2 * P:3 * P], P),
                                       (cqkv[:, n, 3 * P:NA], ROPE)])
                elif what == "MT":
                    if n == 0:
                        pe.wait_ge(s5_m_set, LC)
                    turned(("MT", n), [(M[:, g, :, :].rearrange("p t h -> p (t h)"), P) for g in range(4 * n, 4 * n + 4)])
                elif what == "K":
                    if n == 0:
                        pe.wait_ge(s5_b_set, 1)
                        pe.wait_ge(s5_nx_set, 4)
                    plan.claim(pe, ("K", n))
                    for j in range(4):
                        g = 4 * n + j
                        group(("K", n), bank("K", n)[0:GS, j * P:(j + 1) * P],
                              [(Bst[:, g, :], NX[:, g, 0:LC, :].rearrange("p t h -> p (t h)"))], last=(j == 3))
                elif what == "v":
                    plan.drained(pe, ("UT", n))
                    plan.drained(pe, ("MT", n))
                    plan.claim(pe, ("v", n))
                    for j in range(4):
                        g = 4 * n + j
                        group(("v", n), bank("v", n)[:, j * P:(j + 1) * P], [(MT[:, g, :], UT[:, g, :])], last=(j == 3))
                elif what == "kp":
                    if n == 0:
                        pe.wait_ge(mla_w_loaded, 48)
                        for i in range(NT):
                            plan.drained(pe, ("cT", i))
                    job, p, half = ("kp", n // 2, n % 2), n // 2, n % 2
                    plan.claim(pe, job)
                    group(job, bank(*job), [(w_ukv[:, 0, 2 * p:2 * p + 2, :].rearrange("p h d -> p (h d)"),
                                             cT[:, 2, half * 512:(half + 1) * 512])])
                elif what == "vp":
                    plan.claim(pe, ("vp", n))
                    group(("vp", n), bank("vp", n),
                          [(cT[:, 2, n * P:(n + 1) * P], w_ukv[:, 1, :, :].rearrange("p h d -> p (h d)"))])
                elif what == "q":
                    queries(n, 0)
                    queries(n, 1)
                elif what == "qT":
                    queries_turn(n, 0)
                    queries_turn(n, 1)
                elif what == "s":
                    if n == 0:
                        pe.wait_ge(kpe_spread, 16 * H)
                        for j in range(NT):
                            plan.drained(pe, ("kp", j // 2, j % 2))
                            plan.drained(pe, ("vp", j))
                    score(n)
                elif what == "y":
                    if n == 0:
                        pe.wait_ge(s5_tt_set, 16 * LC)
                        pe.wait_ge(s5_n2_set, 4)
                    pe.wait_ge(s5_states_set, n + 1)
                    plan.claim(pe, ("y", n))
                    for j in range(4):
                        g = 4 * n + j
                        group(("y", n), bank("y", n)[:, j * P:(j + 1) * P],
                              [(UT[:, g, :], TT[:, g, :]),
                               (tabA[:, g, LC:LC + NC5], NX[:, g, 1:LC + 1, :].rearrange("p t h -> p (t h)")),
                               (tabB[:, g, LC:LC + NC5], N2[:, g, :, :].rearrange("p t h -> p (t h)"))], last=(j == 3))
                elif what == "yT":
                    if n == 0:
                        for q in range(4):
                            plan.drained(pe, ("y", q))
                    m, half = n // 2, n % 2
                    turned(("yT", m, half), [(Y5[:, t, 8 * m:8 * m + 8, :].rearrange("p g h -> p (g h)"), P)
                                             for t in range(4 * half, 4 * half + 4)])
                elif what == "glu":
                    if n == 0:
                        pe.wait_ge(glu_w_loaded, 16)
                        for j in range(4):
                            plan.drained(pe, ("yT", j // 2, j % 2))
                    job, m, half = ("glu", n // 2, n % 2), n // 2, n % 2
                    plan.claim(pe, job)
                    group(job, bank(*job),
                          [(w_glu[:, k, m * P:(m + 1) * P], YT[:, k, half * 512:(half + 1) * 512]) for k in range(2)])
            def output(i):
                if i == 0:
                    pe.wait_ge(w_out0_loaded, 16)
                    pe.wait_ge(s5_out_set, 16)
                plan.drained(pe, ("OT", i))
                for n in range(2):
                    plan.claim(pe, ("z0", i, n))
                    ts, cs = slice(i * P, (i + 1) * P), slice(n * 512, (n + 1) * 512)
                    group(("z0", i, n), bank("z0", i, n),
                          [(OT[:, k, ts] if k < 4 else gs5[:, k - 4, ts], w_out0[:, k, cs]) for k in range(6)])

            def x1_turned(i):
                pe.wait_ge(x1_set, i + 1)
                for half in range(2):
                    turned(("x1T", i, half), [(zn[:, i % 2, k * P:(k + 1) * P], P)
                                              for k in range(4 * half, 4 * half + 4)])

            for what, n in attention_steps():
                if what == "q":
                    queries(*n)
                elif what == "z0":
                    output(n)
                elif what == "qT":
                    queries_turn(*n)
                elif what == "s":
                    score(n)
                elif what == "pt":
                    plan.drained(pe, ("s", n))
                    for number, first, blocks in pt_jobs[heads[n]]:
                        place = scores(n)[1] + first * P
                        turned(("pt", number), [(prob[:, place + b * P:place + (b + 1) * P], P)
                                                for b in range(blocks)])
                elif what == "av":
                    i, h = heads[n]
                    if h == 0:
                        plan.claim(pe, ("o", i))
                    pairs = []
                    for number, first, blocks in pt_jobs[i, h]:
                        plan.drained(pe, ("pt", number))
                        pairs += [(probT[:, number % 4, b * P:(b + 1) * P], V[:, first + b, h, :])
                                  for b in range(blocks)]
                    for k, (lhsT, rhs) in enumerate(pairs):
                        mm = pe.matmul(bank("o", i)[:, h * VD:(h + 1) * VD], lhsT, rhs, start=(k == 0),
                                       stop=(k == len(pairs) - 1))
                    mm.then_inc(plan.full(("o", i)) if h == H - 1 else pv_done, 1)
                elif what == "OT":
                    pe.wait_ge(gated, n + 1)
                    turned(("OT", n), [(gate[:, n, k * P:(k + 1) * P], P) for k in range(4)])
            for i in range(1, NT):
                output(i)
                x1_turned(i - 1)
            x1T = (x1T_hi, x1T_lo)

            def low_rank(n):
                plan.claim(pe, ("gk", n))
                group(("gk", n), bank("gk", n)[0:GR, :],
                      split_pairs([([w[:, k, :] for w in w_gk[1:]], [x_[:, k, n * 512:(n + 1) * 512] for x_ in x1T])
                                   for k in range(KD)]))

            def gate_z(m):
                h, n = m // 2, m % 2
                plan.drained(pe, ("gk", n))
                plan.claim(pe, ("gate", m))
                group(("gate", m), bank("gate", m), [(gk2[:, h * P:(h + 1) * P], gkT[:, n * 512:(n + 1) * 512])])

            def queries_keys(m):
                h, n = m // 2, m % 2
                pe.wait_ge(wqk_split, 2 * (h + 1))
                for side, name in enumerate(("q1", "k1")):
                    plan.claim(pe, (name, m))
                    group((name, m), bank(name, m),
                          split_pairs([([w[:, k, side, :] for w in wqk[h % 2][1:]],
                                        [x_[:, k, n * 512:(n + 1) * 512] for x_ in x1T]) for k in range(KD)]))

            for i in range(NT // 2):
                for half in range(2):
                    plan.drained(pe, ("x1T", i, half))
            pe.wait_ge(wgk_split, 1)
            low_rank(0)
            queries_keys(0)
            x1_turned(NT - 1)
            for i in range(NT // 2, NT):
                for half in range(2):
                    plan.drained(pe, ("x1T", i, half))
            low_rank(1)
            pe.wait_ge(small_loaded, 16 * 7)
            for h in range(GH + 1):
                for m in range(2 * h, 2 * h + 2 if h < GH else 0):
                    gate_z(m)
                for m in range(max(1, 2 * h - 1), min(2 * h + 1, 2 * GH)):
                    queries_keys(m)
            for name in ("v1", "g1"):
                by_slices(name, 2, lambda c, k, w: [((name, c, i), 0, 512, True,
                                                     ([x_[:, k, i * P:(i + 1) * P] for x_ in x1T], w))
                                                    for i in range(NT)])
            for c in range(2):
                for i in range(NT):
                    plan.drained(pe, ("v1", c, i))
            for what, i in gla_steps():
                if what == "kT1":
                    pe.wait_ge(ks_set, i + 1)
                    turned(("kT1", i), [(KS[i % 2][:, h, :], P) for h in range(GH)])
                elif what == "at":
                    plan.claim(pe, ("at", i))
                    for h in range(GH):
                        for c, keys in enumerate((KI[:, h, i * P:(i + 1) * P], KS[i % 2][:, h, :])):
                            c0 = c * GC
                            group(("at", i), bank("at", i)[:, h * P + c0:h * P + c0 + GC],
                                  [(keys, QD[:, h, i * P + c0:i * P + c0 + GC])], last=(h == GH - 1 and c == 1))
                elif what == "ks":
                    plan.drained(pe, ("kT1", i))
                    for hp in range(2):
                        plan.claim(pe, ("ks", i, hp))
                        for j in range(2):
                            h = 2 * hp + j
                            group(("ks", i, hp), bank("ks", i, hp)[:, j * GDV:(j + 1) * GDV],
                                  [(kTok[:, i % 2, h, :], V1[:, i, h * GDV:(h + 1) * GDV])], last=(j == 1))
                elif what == "o":
                    plan.drained(pe, ("at", i))
                    if i:
                        plan.drained(pe, ("ks", i - 1, 0))
                        plan.drained(pe, ("ks", i - 1, 1))
                        pe.wait_ge(qs_set, i)
                    for hp in range(2):
                        plan.claim(pe, ("o1", i, hp))
                        for j in range(2):
                            h = 2 * hp + j
                            group(("o1", i, hp), bank("o1", i, hp)[:, j * GDV:(j + 1) * GDV],
                                  [(att[:, i % 2, h, :], V1[:, i, h * GDV:(h + 1) * GDV])]
                                  + ([(QS[:, i % 2, h, :], state[:, (i - 1) % 2, h, :])] if i else []), last=(j == 1))
                elif what == "yT1":
                    plan.drained(pe, ("o1", i, 0))
                    plan.drained(pe, ("o1", i, 1))
                    for half in range(2):
                        turned(("yT1", i, half), [(SG[:, i, k * P:(k + 1) * P], P) for k in range(4 * half, 4 * half + 4)])
                elif what == "z1":
                    if i == 0:
                        pe.wait_ge(w_out1_split, KD)
                    plan.drained(pe, ("yT1", i, 0))
                    plan.drained(pe, ("yT1", i, 1))
                    for n in range(2):
                        plan.claim(pe, ("z1", i, n))
                        group(("z1", i, n), bank("z1", i, n),
                              split_pairs([([y[:, k, :] for y in Y1T[y1t_slot(i)]],
                                            [w[:, k, n * 512:(n + 1) * 512] for w in w_out1[1:]])
                                           for k in range(KD)]))


_OUT = ("out_dram", (1, 1024, 1024))


def kernel(**inputs):
    import concourse.bacc as bacc
    from concourse.bass_utils import run_bass_kernel_spmd

    nc = bacc.Bacc("TRN2", target_bir_lowering=False, num_devices=1)
    arrays, args = {}, {}
    for name, value in inputs.items():
        a = np.ascontiguousarray(value)
        arrays[f"{name}_dram"] = a
        args[name] = nc.dram_tensor(f"{name}_dram", a.shape, mybir.dt.from_np(a.dtype), kind="ExternalInput").ap()
    args["out"] = nc.dram_tensor(_OUT[0], _OUT[1], F32, kind="ExternalOutput").ap()
    hybrid_trunk(nc, **args)
    return run_bass_kernel_spmd(nc, [arrays], core_ids=[0]).results[0][_OUT[0]]
```
